# Optimizing a Trainium2 kernel written in Bass

```python
import math
import jax, jax.numpy as jnp
from jax import lax
import numpy as np

D_MODEL = 1024
BATCH = 1
SEQ = 512
DEPTH = 1

N_META = 16
HEAD_DIM = 64
N_HEADS = 8
N_KV_HEADS = 2
Q_PER_KV = N_HEADS // N_KV_HEADS
ATTN_W = N_HEADS * HEAD_DIM
KV_W = N_KV_HEADS * HEAD_DIM
F_GROUPS = 8
F_GROUP_DIM = 64
F_W = F_GROUPS * F_GROUP_DIM
MIX_W = ATTN_W + F_W
IN_W = ATTN_W + 2 * KV_W + F_W
WINDOW = 128
BLOCK = 128
D_FF = 2816
ALIBI_MAX = 8.0
EPS = 1e-6
NEG = -1e30

kernel_name = "hybrid_swa_fnet_macaron_encoder"

def rms_norm(x, g):
    xf = x.astype(jnp.float32)
    y = xf * lax.rsqrt(jnp.mean(xf * xf, axis=-1, keepdims=True) + EPS)
    return (y * g.astype(jnp.float32)).astype(x.dtype)

def swiglu(x, w_gate, w_up, w_down):
    return (jax.nn.silu(x @ w_gate) * (x @ w_up)) @ w_down

def alibi_slopes():
    h = jnp.arange(1, N_HEADS + 1, dtype=jnp.float32)
    return jnp.exp2(-ALIBI_MAX * h / N_HEADS)

def windowed_gqa(q, k, v, sink):
    B = q.shape[0]
    slopes = alibi_slopes().reshape(N_KV_HEADS, Q_PER_KV)
    sink_f = sink.astype(jnp.float32).reshape(N_KV_HEADS, Q_PER_KV)
    scale = HEAD_DIM ** -0.5

    qm, qr = q[:, :N_META], q[:, N_META:]
    km, kr = k[:, :N_META], k[:, N_META:]
    vm, vr = v[:, :N_META], v[:, N_META:]
    S = qr.shape[1]
    nb = S // BLOCK

    qb = qr.reshape(B, nb, BLOCK, N_KV_HEADS, Q_PER_KV, HEAD_DIM)
    pad = ((0, 0), (BLOCK, BLOCK), (0, 0), (0, 0))
    kp = jnp.pad(kr, pad).reshape(B, nb + 2, BLOCK, N_KV_HEADS, HEAD_DIM)
    vp = jnp.pad(vr, pad).reshape(B, nb + 2, BLOCK, N_KV_HEADS, HEAD_DIM)
    kb = jnp.concatenate([kp[:, :-2], kp[:, 1:-1], kp[:, 2:]], axis=2)
    vb = jnp.concatenate([vp[:, :-2], vp[:, 1:-1], vp[:, 2:]], axis=2)

    tpos = N_META + jnp.arange(S).reshape(nb, BLOCK)
    kpos = N_META + (jnp.arange(nb)[:, None] - 1) * BLOCK + jnp.arange(3 * BLOCK)[None]
    dist = jnp.abs(tpos[:, :, None] - kpos[:, None, :])
    valid = (dist <= WINDOW) & (kpos[:, None, :] >= N_META) & (kpos[:, None, :] < N_META + S)
    bias_band = jnp.where(valid[:, None, None],
                          -slopes[None, :, :, None, None] * dist[:, None, None].astype(jnp.float32),
                          NEG)
    mpos = jnp.arange(N_META)
    dist_m = jnp.minimum(jnp.abs(tpos[:, :, None] - mpos[None, None, :]), WINDOW)
    bias_meta = -slopes[None, :, :, None, None] * dist_m[:, None, None].astype(jnp.float32)

    s_band = jnp.einsum('bnqkgd,bnskd->bnkgqs', qb, kb).astype(jnp.float32) * scale + bias_band[None]
    s_meta = jnp.einsum('bnqkgd,bmkd->bnkgqm', qb, km).astype(jnp.float32) * scale + bias_meta[None]
    s_sink = jnp.broadcast_to(sink_f[None, None, :, :, None, None], s_meta.shape[:-1] + (1,))
    p = jax.nn.softmax(jnp.concatenate([s_meta, s_band, s_sink], axis=-1), axis=-1)
    p_meta = p[..., :N_META].astype(v.dtype)
    p_band = p[..., N_META:N_META + 3 * BLOCK].astype(v.dtype)
    out_r = (jnp.einsum('bnkgqm,bmkd->bnqkgd', p_meta, vm)
             + jnp.einsum('bnkgqs,bnskd->bnqkgd', p_band, vb))
    out_r = out_r.reshape(B, S, ATTN_W)

    qmm = qm.reshape(B, N_META, N_KV_HEADS, Q_PER_KV, HEAD_DIM)
    kr0, vr0 = kr[:, :WINDOW], vr[:, :WINDOW]
    rpos = N_META + jnp.arange(WINDOW)
    d_mm = jnp.abs(mpos[:, None] - mpos[None, :]).astype(jnp.float32)
    d_mr = jnp.abs(mpos[:, None] - rpos[None, :])
    b_mm = -slopes[:, :, None, None] * d_mm[None, None]
    b_mr = jnp.where((d_mr <= WINDOW)[None, None],
                     -slopes[:, :, None, None] * d_mr[None, None].astype(jnp.float32), NEG)
    s_mm = jnp.einsum('bqkgd,bmkd->bkgqm', qmm, km).astype(jnp.float32) * scale + b_mm[None]
    s_mr = jnp.einsum('bqkgd,bskd->bkgqs', qmm, kr0).astype(jnp.float32) * scale + b_mr[None]
    s_ms = jnp.broadcast_to(sink_f[None, :, :, None, None], s_mm.shape[:-1] + (1,))
    pm = jax.nn.softmax(jnp.concatenate([s_mm, s_mr, s_ms], axis=-1), axis=-1)
    out_m = (jnp.einsum('bkgqm,bmkd->bqkgd', pm[..., :N_META].astype(v.dtype), vm)
             + jnp.einsum('bkgqs,bskd->bqkgd', pm[..., N_META:N_META + WINDOW].astype(v.dtype), vr0))
    out_m = out_m.reshape(B, N_META, ATTN_W)
    return jnp.concatenate([out_m, out_r], axis=1)

def fourier_mix(f):
    B, L, _ = f.shape
    ff = f.astype(jnp.float32).reshape(B, L, F_GROUPS, F_GROUP_DIM)
    y = jnp.fft.fft2(ff, axes=(1, 3), norm="ortho").real
    return y.reshape(B, L, F_W).astype(f.dtype)

def setup_inputs(seed: int = 0) -> dict:
    key = jax.random.key(seed)
    ks = jax.random.split(key, 24)
    f32 = jnp.float32

    def nrm(k, shape, scale):
        return jax.random.normal(k, shape, f32) * scale

    def gain(k, n):
        return 1.0 + 0.05 * jax.random.normal(k, (n,), f32)

    return {
        "x": jax.random.normal(ks[0], (BATCH, SEQ, D_MODEL), f32),
        "meta_tokens": nrm(ks[1], (N_META, D_MODEL), 1.0),
        "ffn1_norm": gain(ks[2], D_MODEL),
        "ffn1_w_gate": nrm(ks[3], (D_MODEL, D_FF), D_MODEL ** -0.5),
        "ffn1_w_up": nrm(ks[4], (D_MODEL, D_FF), D_MODEL ** -0.5),
        "ffn1_w_down": nrm(ks[5], (D_FF, D_MODEL), D_FF ** -0.5),
        "mix_norm": gain(ks[6], D_MODEL),
        "w_in": nrm(ks[7], (D_MODEL, IN_W), D_MODEL ** -0.5),
        "q_norm": gain(ks[8], HEAD_DIM),
        "k_norm": gain(ks[9], HEAD_DIM),
        "sink": nrm(ks[10], (N_HEADS,), 0.5),
        "attn_out_norm": gain(ks[11], ATTN_W),
        "fourier_out_norm": gain(ks[12], F_W),
        "w_out": nrm(ks[13], (MIX_W, D_MODEL), MIX_W ** -0.5),
        "ffn2_norm": gain(ks[14], D_MODEL),
        "ffn2_w_gate": nrm(ks[15], (D_MODEL, D_FF), D_MODEL ** -0.5),
        "ffn2_w_up": nrm(ks[16], (D_MODEL, D_FF), D_MODEL ** -0.5),
        "ffn2_w_down": nrm(ks[17], (D_FF, D_MODEL), D_FF ** -0.5),
        "final_norm": gain(ks[18], D_MODEL),
    }

def reference(x, meta_tokens, ffn1_norm, ffn1_w_gate, ffn1_w_up, ffn1_w_down,
              mix_norm, w_in, q_norm, k_norm, sink, attn_out_norm, fourier_out_norm,
              w_out, ffn2_norm, ffn2_w_gate, ffn2_w_up, ffn2_w_down, final_norm):
    B = x.shape[0]
    meta = jnp.broadcast_to(meta_tokens[None].astype(x.dtype), (B, N_META, D_MODEL))
    h = jnp.concatenate([meta, x], axis=1)
    L = h.shape[1]

    for _ in range(DEPTH):
        h = h + 0.5 * swiglu(rms_norm(h, ffn1_norm), ffn1_w_gate, ffn1_w_up, ffn1_w_down)

        u = rms_norm(h, mix_norm) @ w_in
        q = u[..., :ATTN_W].reshape(B, L, N_HEADS, HEAD_DIM)
        k = u[..., ATTN_W:ATTN_W + KV_W].reshape(B, L, N_KV_HEADS, HEAD_DIM)
        v = u[..., ATTN_W + KV_W:ATTN_W + 2 * KV_W].reshape(B, L, N_KV_HEADS, HEAD_DIM)
        f = u[..., ATTN_W + 2 * KV_W:]
        q = rms_norm(q, q_norm)
        k = rms_norm(k, k_norm)

        a_out = windowed_gqa(q, k, v, sink)
        f_out = fourier_mix(f)
        mixed = jnp.concatenate([rms_norm(a_out, attn_out_norm),
                                 rms_norm(f_out, fourier_out_norm)], axis=-1)
        h = h + mixed @ w_out

        h = h + 0.5 * swiglu(rms_norm(h, ffn2_norm), ffn2_w_gate, ffn2_w_up, ffn2_w_down)
        h = rms_norm(h, final_norm)

    return h[:, N_META:]


_drawn_inputs = setup_inputs


def setup_inputs(seed=0):
    import zlib

    import numpy as np

    out = dict(_drawn_inputs(seed))
    spreads = {}
    factors = {'q_norm': 2.879, 'ffn2_norm': 3.946, 'sink': 5.015}
    for name, (base, spread) in spreads.items():
        noise = np.random.default_rng([zlib.crc32(name.encode()), seed]).standard_normal(out[name].shape)
        drawn = base * np.exp(spread * noise) if base else spread * noise
        out[name] = __import__('jax').numpy.asarray(drawn.astype(out[name].dtype))
    for name, factor in factors.items():
        out[name] = (out[name] * factor).astype(out[name].dtype)
    return out
```

```python
from contextlib import ExitStack

import numpy as np

import concourse.bass as bass
from concourse import mybir

F32 = mybir.dt.float32
F32R = mybir.dt.float32r
ALU = mybir.AluOpType
ACT = mybir.ActivationFunctionType
AX_X = mybir.AxisListType.X

P = 128
D_MODEL, SEQ, N_META = 1024, 512, 16
L = SEQ + N_META
HEAD_DIM, N_HEADS, N_KV = 64, 8, 2
GROUP = N_HEADS // N_KV
ATTN_W = N_HEADS * HEAD_DIM
KV_W = N_KV * HEAD_DIM
F_W = 512
F_DIM = 64
IN_W = ATTN_W + 2 * KV_W + F_W
WINDOW = 128
D_FF = 2816
EPS = 1e-6
MASKED = -float(2 ** 100)

KD = D_MODEL // P
KF = D_FF // P
NB = SEQ // P
HALF = L // 2
RING = 4
SLOT = 8
DOWN_UNITS = [(0, 6), (6, 6), (12, 5), (17, 5)]

U_FFN1_A = 0
U_FFN1_B = U_FFN1_A + 2 * KF
U_IN = U_FFN1_B + 4 * KD
U_OUT = U_IN + IN_W // P
U_FFN2_A = U_OUT + KD
U_FFN2_B = U_FFN2_A + 2 * KF

IN_ORDER = ["f0", "f1", "f2", "f3", "v", "k", "q0", "q1", "q2", "q3"]
IN_BANKS = [4, 0, 2]

META_W = N_META + 2
KEYS_W = META_W + SEQ + META_W
SCORE_W = [META_W + 2 * P, META_W + 3 * P, META_W + 3 * P, META_W + 2 * P]
SCORE_AT = [0, 0, META_W + P, META_W + 2 * P]
BIAS_AT = [sum(SCORE_W[:b]) for b in range(NB)]
BIAS_W = sum(SCORE_W)
MAX_W = max(SCORE_W)


def segments(b):
    real = [n for n in (b - 1, b, b + 1) if 0 <= n < NB]
    if b < 2:
        return [(0, META_W, 0)] + [(META_W + P * i, P, n + 1) for i, n in enumerate(real)]
    return [(P * i, P, n + 1) for i, n in enumerate(real)] + [(P * len(real), META_W, 0)]


def sink_column(b):
    return next(c for c, _, n in segments(b) if n == 0) + N_META


STEPS = [(b, g) for b in range(NB) for g in range(N_KV)]
SEG_BASE = [sum(len(segments(b)) for b, _ in STEPS[:s]) for s in range(len(STEPS) + 1)]


def split_constant(a):
    a = np.asarray(a, np.float64).astype(np.float32)
    bits = a.view(np.uint32)
    hi = ((bits + np.uint32(0x7FF) + ((bits >> np.uint32(12)) & np.uint32(1))) & np.uint32(0xFFFFF000)).view(np.float32)
    return hi, a - hi


def constant_tables():
    ident = np.eye(P, dtype=np.float32)
    ones = np.ones((P, P), np.float32)
    pair = np.kron(np.eye(2), np.ones((HEAD_DIM, HEAD_DIM))).astype(np.float32)
    square = np.concatenate([ident, ones, pair], axis=1)

    c = np.arange(F_DIM)
    phase = 2 * np.pi * (np.outer(c, c) % F_DIM) / F_DIM
    channel = np.concatenate([np.kron(np.eye(2), np.cos(phase)), np.kron(np.eye(2), np.sin(phase))], axis=1)
    channel = np.stack(split_constant(channel / np.sqrt(F_DIM)))

    pos, t = np.arange(L), np.arange(1, HALF + 1)
    phase = 2 * np.pi * (np.outer(pos, t) % L) / L
    wave = np.stack([np.cos(phase), np.sin(phase)], axis=1) / np.sqrt(L)
    wave[:, 1, HALF - 1] = 0.0
    rows = np.zeros((1 + NB, P, 2, HALF))
    rows[0, :N_META] = wave[:N_META]
    rows[1:] = wave[N_META:].reshape(NB, P, 2, HALF)
    position = np.stack(split_constant(rows.transpose(1, 0, 2, 3).reshape(P, -1)))

    bias = np.full((P, BIAS_W), MASKED, np.float32)
    q = np.arange(P)
    for b in range(NB):
        for col, _, n in segments(b):
            at = BIAS_AT[b] + col
            if n == 0:
                dist = np.abs(N_META + b * P + q[:, None] - np.arange(N_META)[None])
                bias[:, at:at + N_META] = -np.minimum(dist, WINDOW)
            else:
                dist = np.abs(b * P + q[:, None] - ((n - 1) * P + q[None]))
                bias[:, at:at + P] = np.where(dist <= WINDOW, -dist, MASKED)
    return {"square": square, "channel": channel.astype(np.float32),
            "position": position.astype(np.float32), "bias": bias}


class NormSems:

    def __init__(self, sem, name):
        self.hi = sem(f"xg_hi_ready_{name}")
        self.ready = sem(f"xg_ready_{name}")
        self.sq = sem(f"squares_ready_{name}")
        self.sq_used = sem(f"squares_used_{name}")
        self.root = sem(f"root_ready_{name}")
        self.rstd = sem(f"rstd_ready_{name}")


class FfnSems:

    def __init__(self, sem, name):
        self.gate_scaled = sem(f"gate_scaled_{name}")
        self.silu_ready = sem(f"silu_ready_{name}")
        self.up_scaled = sem(f"up_scaled_{name}")
        self.act_ready = sem(f"act_ready_{name}")
        self.h_hi_ready = sem(f"h_hi_ready_{name}")
        self.h_ready = sem(f"h_ready_{name}")
        self.x_updated = sem(f"x_updated_{name}")
        self.turned = sem(f"turned_{name}")
        self.turned_read = sem(f"turned_read_{name}")


class Ffn:

    def __init__(self, n, first, spans, unit_a, unit_b, gate_bank, up_bank, down_bank, sems):
        self.n, self.first, self.spans, self.tokens = n, first, spans, sum(w for _, w in spans)
        self.unit_a, self.unit_b = unit_a, unit_b
        self.gate_bank, self.up_bank, self.down_bank = gate_bank, up_bank, down_bank
        self.s = sems


def build(nc, t, out):
    with ExitStack() as ctx:
        top = [((nc.sbuf_base + 31) // 32) * 32]

        def width(shape):
            n = 4
            for s in shape[1:]:
                n *= s
            return (n + 31) // 32 * 32

        def persist(name, shape, dt=F32):
            at = top[0]
            top[0] += width(shape)
            return nc.alloc_sbuf_tensor_at(name, shape, dt, offset=at)

        def region(start, items):
            got, at = {}, start
            for name, shape, dt in items:
                got[name] = nc.alloc_sbuf_tensor_at(name, shape, dt, offset=at)
                at += width(shape)
            return got, at

        xT = persist("xT", [P, KD, L])
        rstd = persist("rstd", [P, L])
        square = persist("square", [P, 3, P])
        gains = persist("gains", [P, 3, KD])
        out_gain = persist("out_gain", [P, 2, GROUP])
        qk_gain = persist("qk_gain", [P, 2])
        sinks = persist("sinks", [P, N_HEADS])
        neg_sinks = persist("neg_sinks", [P, N_HEADS])
        eps = persist("eps", [P, 1])
        score_max = persist("score_max", [P, 2 * len(STEPS), 2])
        neg_max = persist("neg_max", [P, 2 * len(STEPS), 2])
        sink_diff = persist("sink_diff", [P, 2 * len(STEPS), 2])
        row_sums = persist("row_sums", [P, NB, KD])
        row_rstd = persist("row_rstd", [P, NB])
        scratch_a = [persist(f"scratch_a{p}", [P, L]) for p in range(2)]
        scratch_b = [persist(f"scratch_b{p}", [P, L]) for p in range(2)]
        raw = [persist(f"raw{s}", [P, SLOT, P]) for s in range(RING)]
        w_hi = [persist(f"w_hi{s}", [P, SLOT, P], F32R) for s in range(RING)]
        w_lo = [persist(f"w_lo{s}", [P, SLOT, P], F32R) for s in range(RING)]
        channel_hi = persist("channel_hi", [P, 2 * P], F32R)
        bias_tab = persist("bias_tab", [P, BIAS_W], F32R)

        x_region = top[0]
        xr, h_region = region(x_region, [("xg_hi", [P, KD, L], F32R), ("xg_lo", [P, KD, L], F32R)])
        xg_hi, xg_lo = xr["xg_hi"], xr["xg_lo"]
        hr, end = region(h_region, [("h_hi", [P, KF, L], F32R), ("h_lo", [P, KF, L], F32R)])
        h_hi, h_lo = hr["h_hi"], hr["h_lo"]
        assert end <= nc.sbuf_usable_end, (end, nc.sbuf_usable_end)

        st, _ = region(end - width([P, NB + 1, D_MODEL]), [("x_rows", [P, NB, D_MODEL], F32), ("meta_rows", [P, D_MODEL], F32)])
        x_rows, meta_rows = st["x_rows"], st["meta_rows"]
        start_sq = region(h_region, [("start_sq", [P, KD, L], F32)])[0]["start_sq"]

        mx, mix_end = region(h_region, [
            ("f_hi", [P, 4, L], F32R), ("f_lo", [P, 4, L], F32R),
            ("q_stack", [P, N_HEADS, SEQ], F32R),
            ("k_hi", [P, N_KV, KEYS_W], F32R), ("k_lo", [P, N_KV, KEYS_W], F32R), ("k_norm_rows", [P, KEYS_W], F32),
            ("v_hi", [P, N_KV, 1 + NB, P], F32R), ("v_lo", [P, N_KV, 1 + NB, P], F32R),
            ("rstd_f", [P, SEQ], F32), ("rstd_a", [P, SEQ], F32), ("channel_lo", [P, 2 * P], F32R),
            ("mix_f_hi", [P, 4, SEQ], F32R), ("mix_f_lo", [P, 4, SEQ], F32R),
            ("mix_a_hi", [P, 4, SEQ], F32R), ("mix_a_lo", [P, 4, SEQ], F32R)])
        assert mix_end <= end
        f_hi, f_lo, q_stack, k_hi, k_lo, k_rows = (mx[n] for n in ("f_hi", "f_lo", "q_stack", "k_hi", "k_lo", "k_norm_rows"))
        v_hi, v_lo, rstd_f, rstd_a, channel_lo = (mx[n] for n in ("v_hi", "v_lo", "rstd_f", "rstd_a", "channel_lo"))
        mix_f_hi, mix_f_lo, mix_a_hi, mix_a_lo = (mx[n] for n in ("mix_f_hi", "mix_f_lo", "mix_a_hi", "mix_a_lo"))
        tb, tb_end = region(mix_end - 4 * width([P, 4, SEQ]), [("position_hi", [P, 1 + NB, 2, HALF], F32R),
                                                               ("position_lo", [P, 1 + NB, 2, HALF], F32R)])
        position_hi, position_lo = tb["position_hi"], tb["position_lo"]
        assert tb_end <= mix_end
        fr, fr_end = region(x_region, [("f_out", [P, 4, SEQ], F32), ("z_hi0", [P, 1 + NB, 2 * P], F32R), ("z_lo0", [P, 1 + NB, 2 * P], F32R),
                                       ("z_hi1", [P, 1 + NB, 2 * P], F32R), ("z_lo1", [P, 1 + NB, 2 * P], F32R)])
        assert fr_end <= h_region
        f_out, z_hi, z_lo = fr["f_out"], [fr["z_hi0"], fr["z_hi1"]], [fr["z_lo0"], fr["z_lo1"]]
        ar, ar_end = region(x_region + width([P, 4, SEQ]), [
            ("probs0", [P, GROUP, MAX_W], F32), ("probs1", [P, GROUP, MAX_W], F32),
            ("attn0", [P, GROUP, P], F32), ("attn1", [P, GROUP, P], F32), ("inv_den", [P, GROUP, P], F32), ("attn_sq", [P, GROUP, P], F32)])
        assert ar_end <= h_region
        probs, attn = [ar["probs0"], ar["probs1"]], [ar["attn0"], ar["attn1"]]
        inv_den, attn_sq = ar["inv_den"], ar["attn_sq"]
        br, br_end = region(h_region, [
            ("slopes", [P, N_HEADS, P], F32R), ("pt_hi0", [P, GROUP, P], F32R), ("pt_lo0", [P, GROUP, P], F32R),
            ("pt_hi1", [P, GROUP, P], F32R), ("pt_lo1", [P, GROUP, P], F32R), ("attn_gained", [P, GROUP, P], F32)])
        assert br_end <= h_region + 2 * width([P, 4, L])
        slopes, attn_gained = br["slopes"], br["attn_gained"]
        pt_hi, pt_lo = [br["pt_hi0"], br["pt_hi1"]], [br["pt_lo0"], br["pt_lo1"]]
        er, er_end = region(x_region, [("y_rows", [P, NB, D_MODEL], F32), ("final_gain", [P, D_MODEL], F32)])
        assert er_end <= h_region
        y_rows, final_gain = er["y_rows"], er["final_gain"]

        ps = ctx.enter_context(nc.psum_tensor("ps", [P, 8, 512], F32))
        ident, ones, pair_ones = square[:, 0, :], square[:, 1, :], square[:, 2, :]

        def sem(name):
            return ctx.enter_context(nc.semaphore(name))

        x_landed = [sem(f"x_landed{i}") for i in range(NB + 1)]
        square_landed, small_landed = sem("square_landed"), sem("small_landed")
        mix_tables_landed, position_landed, gain_row_landed = sem("mix_tables_landed"), sem("position_landed"), sem("gain_row_landed")
        raw_landed = [sem(f"raw_landed{s}") for s in range(RING)]
        hi_ready, split_ready, unit_used = sem("hi_ready"), sem("split_ready"), sem("unit_used")
        constants_ready = sem("constants_ready")
        x_turned, x_copied = sem("x_turned"), sem("x_copied")
        norms = [NormSems(sem, n) for n in ("ffn1", "mix", "ffn2")]
        ffns = [FfnSems(sem, n) for n in ("ffn1", "ffn2")]
        in_read = sem("in_read")
        f_hi_ready, f_ready = sem("f_hi_ready"), sem("f_ready")
        fills_ready = sem("fills_ready")
        v_turned, v_hi_ready, v_ready = sem("v_turned"), sem("v_hi_ready"), sem("v_ready")
        qk_sq_ready, qk_summed, qk_root_ready = sem("qk_sq_ready"), sem("qk_summed"), sem("qk_root_ready")
        qk_inv_ready, qk_normed, qk_hi_ready, qk_ready = sem("qk_inv_ready"), sem("qk_normed"), sem("qk_hi_ready"), sem("qk_ready")
        z_done, z_hi_ready, z_ready = sem("z_done"), sem("z_hi_ready"), sem("z_ready")
        waves_done, sine_copied, waves_read = sem("waves_done"), sem("sine_copied"), sem("waves_read")
        fsq_ready, fsq_summed, f_root_ready, rstd_f_ready = sem("fsq_ready"), sem("fsq_summed"), sem("f_root_ready"), sem("rstd_f_ready")
        f_normed, mix_f_hi_ready, mix_f_ready = sem("f_normed"), sem("mix_f_hi_ready"), sem("mix_f_ready")
        slopes_ready = sem("slopes_ready")
        scores_done, max_ready, shift_ready, exp_done = sem("scores_done"), sem("max_ready"), sem("shift_ready"), sem("exp_done")
        pt_done, pt_hi_ready, pt_ready, pv_used = sem("pt_done"), sem("pt_hi_ready"), sem("pt_ready"), sem("pv_used")
        den_inverted, attn_ready = sem("den_inverted"), sem("attn_ready")
        attn_sq_ready, attn_sq_summed, gained_ready = sem("attn_sq_ready"), sem("attn_sq_summed"), sem("gained_ready")
        mix_a_hi_ready, mix_a_ready = sem("mix_a_hi_ready"), sem("mix_a_ready")
        a_root_ready, rstd_a_ready = sem("a_root_ready"), sem("rstd_a_ready")
        attn_part_scaled, x_plus_f, x_mixed = sem("attn_part_scaled"), sem("x_plus_f"), sem("x_mixed")
        sums_ready, mean_ready, final_root, final_rstd, rows_scaled, stored = (
            sem("sums_ready"), sem("mean_ready"), sem("final_root"), sem("final_rstd"), sem("rows_scaled"), sem("stored"))

        def count(i, k0, k1=0):
            return k0 if i is None else i * k1 + k0

        def need(eng, semaphore, value):
            if not isinstance(value, int) or value > 0:
                eng.wait_ge(semaphore, value)

        FFN = [Ffn(0, 0, [(0, HALF), (HALF, HALF)], U_FFN1_A, U_FFN1_B, [0, 4], [2, 6], [0, 2], ffns[0]),
               Ffn(1, N_META, [(0, SEQ)], U_FFN2_A, U_FFN2_B, [4, 2], [5, 3], [0, 1], ffns[1])]

        def banks(bank, spans):
            n = spans[0][1]
            return ps[:, bank, 0:n] if len(spans) == 1 else ps[:, bank:bank + 2, 0:n]

        def like(ap, spans):
            return ap if len(spans) == 1 else ap.rearrange("p (a n) -> p a n", a=2)

        HALVES = FFN[0].spans

        def pairs(eng, steps, body):
            body(0, 0, 0, None)
            body(1, 1, 0, None)
            with eng.Fori(0, (steps - 2) // 2) as i:
                body(0, 2, 2, i)
                body(1, 3, 2, i)

        block = ctx.enter_context(nc.Block())

        @block.sync
        def _(sp):
            def raw_slot(n, i=None, per=0):
                need(sp, split_ready, count(i, n + 1 - RING, per))
                return raw[n % RING], raw_landed[n % RING]

            def load_columns(w, unit, column, i=None, per=0):
                slot, landed = raw_slot(unit, i, per)
                sp.dma_start(slot[:], w.rearrange("(k p) n -> p k n", p=P)[:, :, bass.ds(column, P)]).then_inc(landed, 16)

            def ffn(f, w_gate, w_up, w_down):
                def step_a(parity, k0, k1, i):
                    column = count(i, k0 * P, k1 * P)
                    load_columns(w_gate, f.unit_a + 2 * k0, column, i, 2 * k1)
                    load_columns(w_up, f.unit_a + 2 * k0 + 1, column, i, 2 * k1)

                def step_b(parity, k0, k1, i):
                    for j, (f0, n) in enumerate(DOWN_UNITS):
                        slot, landed = raw_slot(f.unit_b + 4 * k0 + j, i, 4 * k1)
                        src = w_down.rearrange("(k p) n -> p k n", p=P)[:, f0:f0 + n, bass.ds(count(i, k0 * P, k1 * P), P)]
                        sp.dma_start(slot[:, 0:n, :], src).then_inc(landed, 16)

                pairs(sp, KF, step_a)
                pairs(sp, KD, step_b)

            sp.dma_start(square[:], t["square"].rearrange("p (a n) -> p a n", a=3)).then_inc(square_landed, 16)
            for b in range(NB):
                sp.dma_start(x_rows[:, b, :], t["x"][0, b * P:(b + 1) * P, :]).then_inc(x_landed[b], 16)
            ffn(FFN[0], t["ffn1_w_gate"], t["ffn1_w_up"], t["ffn1_w_down"])
            w_in = t["w_in"].rearrange("(k p) n -> p k n", p=P)
            for j, name in enumerate(IN_ORDER):
                slot, landed = raw_slot(U_IN + j)
                if name[0] == "q":
                    for g in range(N_KV):
                        c = (g * GROUP + int(name[1])) * HEAD_DIM
                        sp.dma_start(slot[:, :, g * HEAD_DIM:(g + 1) * HEAD_DIM], w_in[:, :, c:c + HEAD_DIM]).then_inc(landed, 16)
                else:
                    c = ATTN_W + 2 * KV_W + P * int(name[1]) if name[0] == "f" else {"k": ATTN_W, "v": ATTN_W + KV_W}[name]
                    sp.dma_start(slot[:], w_in[:, :, c:c + P]).then_inc(landed, 16)
            for d in range(KD):
                slot, landed = raw_slot(U_OUT + d)
                cols = slice(d * P, (d + 1) * P)
                sp.dma_start(slot[:, 0:4, :], t["w_out"][ATTN_W:, cols].rearrange("(k p) n -> p k n", p=P)).then_inc(landed, 16)
                for g in range(N_KV):
                    rows = slice(g * GROUP * HEAD_DIM, (g + 1) * GROUP * HEAD_DIM)
                    sp.dma_start(slot[g * HEAD_DIM:(g + 1) * HEAD_DIM, 4:8, :],
                                 t["w_out"][rows, cols].rearrange("(j p) n -> p j n", p=HEAD_DIM)).then_inc(landed, 16)
            ffn(FFN[1], t["ffn2_w_gate"], t["ffn2_w_up"], t["ffn2_w_down"])
            for b in range(NB):
                sp.wait_ge(rows_scaled, b + 1)
                sp.dma_start(out[0, b * P:(b + 1) * P, :], y_rows[:, b, :]).then_inc(stored, 16)
            sp.wait_ge(stored, 16 * NB)

        def transfers(n):
            if U_IN <= n < U_OUT:
                return 2 if IN_ORDER[n - U_IN][0] == "q" else 1
            return 3 if U_OUT <= n < U_FFN2_A else 1

        def landed_count(n):
            return 16 * sum(transfers(m) for m in range(n % RING, n + 1, RING))

        @block.gpsimd
        def _(pool):
            pool.dma_start(channel_hi[:], t["channel"][0]).then_inc(mix_tables_landed, 16)
            pool.dma_start(bias_tab[:], t["bias"]).then_inc(mix_tables_landed, 16)
            pool.wait_ge(unit_used, U_IN)
            pool.dma_start(channel_lo[:], t["channel"][1]).then_inc(mix_tables_landed, 16)
            pool.dma_start(position_hi[:], t["position"][0].rearrange("p (a b n) -> p a b n", a=1 + NB, b=2)).then_inc(position_landed, 16)
            pool.dma_start(position_lo[:], t["position"][1].rearrange("p (a b n) -> p a b n", a=1 + NB, b=2)).then_inc(position_landed, 16)
            nc.gpsimd.memset(k_rows[:], 0.0).then_inc(fills_ready, 1)
            nc.gpsimd.memset(v_lo[:].bitcast(F32), 0.0).then_inc(fills_ready, 1)
            for g in range(N_KV):
                dims = slice(g * HEAD_DIM, (g + 1) * HEAD_DIM)
                rest = slice((1 - g) * HEAD_DIM, (2 - g) * HEAD_DIM)
                nc.gpsimd.memset(v_hi[:, g, :, rest].bitcast(F32), 1.0).then_inc(fills_ready, 1)
                nc.gpsimd.memset(v_hi[0:32, g, 0, dims].bitcast(F32), 0.0).then_inc(fills_ready, 1)
            pool.wait_ge(unit_used, U_FFN2_B)
            pool.dma_start(final_gain[:], t["final_norm"].rearrange("(a n) -> a n", a=1).to_broadcast([P, D_MODEL])).then_inc(gain_row_landed, 16)

        FILLS = 2 + 2 * N_KV

        @block.scalar
        def _(act):
            def split_hi(n, tiles, i=None, per=0):
                act.wait_ge(raw_landed[n % RING], count(i, landed_count(n), 16 * per // RING))
                need(act, unit_used, count(i, n + 1 - RING, per))
                nc.scalar.activation(w_hi[n % RING][:, 0:tiles, :], raw[n % RING][:, 0:tiles, :], ACT.Copy).then_inc(hi_ready, 1)

            def gained_hi(norm, ready, k, k1, i, first, spans, squares=None):
                s = norms[norm]
                chunk = count(i, k, k1)
                n = sum(w for _, w in spans)
                if squares is None:
                    need(act, s.sq_used, count(i, k, k1))
                act.wait_ge(ready, count(i, k + 1, k1))
                nc.scalar.activation(xg_hi[:, chunk, 0:n], xT[:, chunk, first:first + n], ACT.Copy,
                                     scale=gains[:, norm, bass.ds(chunk, 1)]).then_inc(s.hi, 1)
                if squares is None:
                    nc.scalar.activation(scratch_a[k % 2][:, 0:n], xT[:, chunk, first:first + n], ACT.Square).then_inc(s.sq, 1)

            def norm_root(norm, bank, spans):
                n = sum(w for _, w in spans)
                act.wait_ge(norms[norm].sq_used, KD)
                nc.scalar.activation(like(rstd[:, 0:n], spans), banks(bank, spans), ACT.Sqrt, bias=eps[:, 0:1],
                                     scale=1.0 / D_MODEL).then_inc(norms[norm].root, 1)

            def ffn(f, at_first, at_second):
                s = f.s

                def finish_a(parity, k0, k1, i):
                    act.wait_ge(s.gate_scaled, count(i, k0 + 1, k1))
                    a = scratch_a[parity][:, 0:f.tokens]
                    nc.scalar.activation(a, a, ACT.Silu).then_inc(s.silu_ready, 1)
                    act.wait_ge(s.act_ready, count(i, k0 + 1, k1))
                    nc.scalar.activation(h_hi[:, count(i, k0, k1), 0:f.tokens], scratch_b[parity][:, 0:f.tokens],
                                         ACT.Copy).then_inc(s.h_hi_ready, 1)

                def step_a(parity, k0, k1, i):
                    split_hi(f.unit_a + 2 * k0, KD, i, 2 * k1)
                    split_hi(f.unit_a + 2 * k0 + 1, KD, i, 2 * k1)
                    if k0 == 0:
                        at_first()
                    else:
                        if k0 == 1:
                            at_second()
                        finish_a(1 - parity, k0 - 1, k1, i)

                def finish_b(k0, k1, i):
                    if f.n == 0:
                        gained_hi(1, s.x_updated, k0, k1, i, 0, HALVES)
                    else:
                        act.wait_ge(s.turned, count(i, k0 + 1, k1))
                        for b in range(NB):
                            last = nc.scalar.activation(scratch_a[k0 % 2][:, b * P:(b + 1) * P], ps[:, 6 + k0 % 2, b * P:(b + 1) * P],
                                                        ACT.Square, accum_out=row_sums[:, b, bass.ds(count(i, k0, k1), 1)])
                        last.then_inc(sums_ready, 1)

                def step_b(parity, k0, k1, i):
                    for j, (_, n) in enumerate(DOWN_UNITS):
                        if j == 3:
                            if k0 == 0:
                                finish_a(1, KF - 1, 0, None)
                            else:
                                finish_b(k0 - 1, k1, i)
                        split_hi(f.unit_b + 4 * k0 + j, n, i, 4 * k1)

                pairs(act, KF, step_a)
                pairs(act, KD, step_b)

            with nc.allow_non_contiguous_dma(reason="gains by feature: a few KB"):
                for n, name in enumerate(("ffn1_norm", "mix_norm", "ffn2_norm")):
                    act.dma_start(gains[:, n, :], t[name].rearrange("(k p) -> p k", p=P)).then_inc(small_landed, 16)
                    if n == 0:
                        act.dma_start(meta_rows[0:N_META, :], t["meta_tokens"]).then_inc(x_landed[NB], 16)
                act.dma_start(out_gain[:, 1, :], t["fourier_out_norm"].rearrange("(k p) -> p k", p=P)).then_inc(small_landed, 16)
                for g in range(N_KV):
                    rows = slice(g * HEAD_DIM, (g + 1) * HEAD_DIM)
                    width_g = GROUP * HEAD_DIM
                    act.dma_start(out_gain[rows, 0, :], t["attn_out_norm"][g * width_g:(g + 1) * width_g].rearrange(
                        "(j p) -> p j", p=HEAD_DIM)).then_inc(small_landed, 16)
                    act.dma_start(qk_gain[rows, 0:1], t["q_norm"].rearrange("(p a) -> p a", a=1)).then_inc(small_landed, 16)
                    act.dma_start(qk_gain[rows, 1:2], t["k_norm"].rearrange("(p a) -> p a", a=1)).then_inc(small_landed, 16)
                act.dma_start(sinks[:], t["sink"].rearrange("(a h) -> a h", a=1).to_broadcast([P, N_HEADS])).then_inc(small_landed, 16)

            act.wait_ge(small_landed, 16 * SMALL)
            act.wait_ge(constants_ready, 1)

            def start():
                for k in range(KD):
                    gained_hi(0, x_copied, k, 0, None, 0, HALVES, squares=start_sq)
                for k in range(KD):
                    nc.scalar.activation(start_sq[:, k, :], xT[:, k, :], ACT.Square).then_inc(norms[0].sq, 1)

            ffn(FFN[0], start, lambda: norm_root(0, 6, HALVES))

            def in_finish(e):
                name = IN_ORDER[e]
                a, b = scratch_a[e % 2], scratch_b[e % 2]
                if name[0] == "f":
                    act.wait_ge(in_read, e + 1)
                    nc.scalar.activation(f_hi[:, int(name[1]), :], b[:], ACT.Copy).then_inc(f_hi_ready, 1)
                elif name == "v":
                    act.wait_ge(v_turned, 1)
                    act.wait_ge(fills_ready, FILLS)
                    for g in range(N_KV):
                        dims = slice(g * HEAD_DIM, (g + 1) * HEAD_DIM)
                        nc.scalar.activation(v_hi[:, g, 1:, dims], ps[:, 6, :].rearrange("p (a n) -> p a n", a=NB)[:, :, dims],
                                             ACT.Copy).then_inc(v_hi_ready, 1)
                        nc.scalar.activation(v_hi[0:N_META, g, 0, dims], ps[0:N_META, 7, dims], ACT.Copy).then_inc(v_hi_ready, 1)
                else:
                    act.wait_ge(in_read, e + 1)
                    n = e - IN_ORDER.index("k")
                    nc.scalar.activation(a[:], b[:], ACT.Square).then_inc(qk_sq_ready, 1)

            def qk_root(n):
                act.wait_ge(qk_summed, n + 1)
                a = scratch_a[(n + IN_ORDER.index("k")) % 2]
                nc.scalar.activation(like(a[:], HALVES), banks(6, HALVES), ACT.Sqrt, bias=eps[:, 0:1],
                                     scale=1.0 / HEAD_DIM).then_inc(qk_root_ready, 1)

            def qk_hi(n):
                act.wait_ge(qk_normed, n + 1)
                if n == 0:
                    for g in range(N_KV):
                        for at in range(2):
                            nc.scalar.activation(k_hi[at * HEAD_DIM:(at + 1) * HEAD_DIM, g, :],
                                                 k_rows[g * HEAD_DIM:(g + 1) * HEAD_DIM, :], ACT.Copy).then_inc(qk_hi_ready, 1)
                else:
                    b = scratch_b[(n + IN_ORDER.index("k")) % 2]
                    for g in range(N_KV):
                        rows = slice(g * HEAD_DIM, (g + 1) * HEAD_DIM)
                        nc.scalar.activation(q_stack[rows, g * GROUP + n - 1, :], b[rows, N_META:L], ACT.Copy).then_inc(qk_hi_ready, 1)

            K_AT = IN_ORDER.index("k")
            split_hi(U_IN, KD)
            for j in range(len(IN_ORDER)):
                if j + 1 < len(IN_ORDER) and j:
                    split_hi(U_IN + j + 1, KD)
                if j == 0:
                    gained_hi(1, ffns[0].x_updated, KD - 1, 0, None, 0, HALVES)
                    split_hi(U_IN + 1, KD)
                    norm_root(1, 6, HALVES)
                elif IN_ORDER[j - 1] != "v":
                    in_finish(j - 1)
                if j == K_AT + 1:
                    in_finish(IN_ORDER.index("v"))
                if j >= K_AT + 2:
                    qk_root(j - K_AT - 2)
                    qk_hi(j - K_AT - 2)
            in_finish(len(IN_ORDER) - 1)
            QK = len(IN_ORDER) - K_AT
            qk_root(QK - 2)
            qk_hi(QK - 2)

            def z_split(c):
                act.wait_ge(z_done, c + 1)
                if c >= 2:
                    act.wait_ge(waves_done, c - 1)
                bank = 3 * (c % 2)
                nc.scalar.activation(z_hi[c % 2][:, 1:, :].rearrange("p a n -> p (a n)"), ps[:, bank:bank + 2, :].rearrange("p a n -> p (a n)"),
                                     ACT.Copy).then_inc(z_hi_ready, 1)
                nc.scalar.activation(z_hi[c % 2][0:N_META, 0, :], ps[0:N_META, bank + 2, 0:2 * P], ACT.Copy).then_inc(z_hi_ready, 1)

            def copy_sine(c):
                act.wait_ge(waves_done, c + 1)
                if c >= 2:
                    act.wait_ge(waves_read, c - 1)
                nc.scalar.activation(scratch_b[c % 2][:, 0:HALF], ps[:, 7, 0:HALF], ACT.Copy).then_inc(sine_copied, 1)

            def square_f(c):
                act.wait_ge(waves_read, c + 1)
                need(act, fsq_summed, c - 1)
                nc.scalar.activation(scratch_a[c % 2][:, 0:SEQ], f_out[:, c, :], ACT.Square).then_inc(fsq_ready, 1)

            z_split(0)
            qk_root(QK - 1)
            z_split(1)
            qk_hi(QK - 1)
            copy_sine(0)
            z_split(2)
            copy_sine(1)
            square_f(0)
            z_split(3)
            copy_sine(2)
            square_f(1)
            copy_sine(3)
            square_f(2)
            square_f(3)
            act.wait_ge(fsq_summed, 4)
            nc.scalar.activation(rstd_f[:], ps[:, 0, :], ACT.Sqrt, bias=eps[:, 0:1], scale=1.0 / F_W).then_inc(f_root_ready, 1)

            def exps(s, half):
                b, g = STEPS[s]
                n = 2 * s + half
                act.wait_ge(shift_ready, 2 * (n + 1))
                need(act, pt_done, SEG_BASE[s - 1] if s >= 2 else 0)
                for h in range(2):
                    nc.scalar.activation(probs[s % 2][:, 2 * half + h, 0:SCORE_W[b]], ps[:, 2 * half + h, 0:SCORE_W[b]], ACT.Exp,
                                         bias=neg_max[:, n, h:h + 1], scale=HEAD_DIM ** -0.5).then_inc(exp_done, 1)
                act.wait_ge(exp_done, EXPS * n + 2)
                nc.scalar.activation(probs[s % 2][:, 2 * half:2 * half + 2, sink_column(b)], sink_diff[:, n, :], ACT.Exp).then_inc(exp_done, 1)

            def probs_hi(s, j):
                m = SEG_BASE[s] + j
                _, keys, _ = segments(STEPS[s][0])[j]
                act.wait_ge(pt_done, m + 1)
                need(act, pv_used, m - 1)
                nc.scalar.activation(pt_hi[m % 2][0:keys].rearrange("p a n -> p (a n)"), ps[0:keys, 4 + m % 2, :], ACT.Copy).then_inc(pt_hi_ready, 1)

            def square_attn(b):
                act.wait_ge(attn_ready, 2 * (b + 1))
                need(act, attn_sq_summed, b)
                nc.scalar.activation(attn_sq[:], attn[b % 2][:], ACT.Square).then_inc(attn_sq_ready, 1)

            def mix_hi(b):
                act.wait_ge(gained_ready, b + 1)
                nc.scalar.activation(mix_a_hi[:, :, b * P:(b + 1) * P], attn_gained[:], ACT.Copy).then_inc(mix_a_hi_ready, 1)

            exps(0, 0)
            exps(0, 1)
            for c in range(4):
                act.wait_ge(f_normed, c + 1)
                nc.scalar.activation(mix_f_hi[:, c, :], f_out[:, c, :], ACT.Copy).then_inc(mix_f_hi_ready, 1)
            for s in range(len(STEPS)):
                b, g = STEPS[s]
                n_seg = len(segments(b))
                probs_hi(s, 0)
                if s + 1 < len(STEPS):
                    exps(s + 1, 0)
                probs_hi(s, 1)
                if s + 1 < len(STEPS):
                    exps(s + 1, 1)
                for j in range(2, n_seg):
                    probs_hi(s, j)
                if s >= 2 and g == 0:
                    square_attn(b - 1)
                    mix_hi(b - 1)
            square_attn(NB - 1)
            mix_hi(NB - 1)

            split_hi(U_OUT, KD)
            for d in range(KD):
                if d + 1 < KD:
                    split_hi(U_OUT + d + 1, KD)
                if d == 0:
                    act.wait_ge(attn_sq_summed, NB)
                    nc.scalar.activation(rstd_a[:], ps[:, 7, :], ACT.Sqrt, bias=eps[:, 0:1], scale=1.0 / ATTN_W).then_inc(a_root_ready, 1)
                else:
                    gained_hi(2, x_mixed, d - 1, 0, None, N_META, FFN[1].spans)

            def second_norm():
                gained_hi(2, x_mixed, KD - 1, 0, None, N_META, FFN[1].spans)

            ffn(FFN[1], second_norm, lambda: norm_root(2, 6, FFN[1].spans))
            act.wait_ge(ffns[1].turned, KD)
            for b in range(NB):
                last = nc.scalar.activation(scratch_a[1][:, b * P:(b + 1) * P], ps[:, 7, b * P:(b + 1) * P], ACT.Square,
                                            accum_out=row_sums[:, b, KD - 1:KD])
            last.then_inc(sums_ready, 1)
            act.wait_ge(mean_ready, 1)
            nc.scalar.activation(row_rstd[:], row_rstd[:], ACT.Sqrt, bias=eps[:, 0:1], scale=1.0 / D_MODEL).then_inc(final_root, 1)

        @block.vector
        def _(dve):
            def split_lo(n, tiles, i=None, per=0):
                dve.wait_ge(hi_ready, count(i, n + 1, per))
                s = n % RING
                nc.vector.tensor_tensor(w_lo[s][:, 0:tiles, :], raw[s][:, 0:tiles, :], w_hi[s][:, 0:tiles, :].bitcast(F32),
                                        ALU.subtract).then_inc(split_ready, 1)

            def gained_lo(norm, k, k1, i, first, n):
                chunk = count(i, k, k1)
                dve.wait_ge(norms[norm].hi, count(i, k + 1, k1))
                nc.vector.scalar_tensor_tensor(xg_lo[:, chunk, 0:n], xT[:, chunk, first:first + n], gains[:, norm, bass.ds(chunk, 1)],
                                               xg_hi[:, chunk, 0:n].bitcast(F32), ALU.mult, ALU.subtract).then_inc(norms[norm].ready, 1)

            def norm_inverse(norm, n):
                dve.wait_ge(norms[norm].root, 1)
                nc.vector.reciprocal(rstd[:, 0:n], rstd[:, 0:n]).then_inc(norms[norm].rstd, 1)
                dve.wait_ge(norms[norm].rstd, 1)

            def ffn(f, at_first, norm):
                s = f.s
                r = like(rstd[:, 0:f.tokens], f.spans)

                def scale_gate(parity, k0, k1, i):
                    dve.wait_ge(unit_used, count(i, f.unit_a + 2 * k0 + 1, 2 * k1))
                    nc.vector.tensor_tensor(like(scratch_a[parity][:, 0:f.tokens], f.spans), banks(f.gate_bank[parity], f.spans), r,
                                            ALU.mult).then_inc(s.gate_scaled, 1)

                def finish_a(parity, k0, k1, i):
                    a, b = scratch_a[parity][:, 0:f.tokens], scratch_b[parity][:, 0:f.tokens]
                    dve.wait_ge(unit_used, count(i, f.unit_a + 2 * k0 + 2, 2 * k1))
                    nc.vector.tensor_tensor(like(b, f.spans), banks(f.up_bank[parity], f.spans), r, ALU.mult).then_inc(s.up_scaled, 1)
                    dve.wait_ge(s.up_scaled, count(i, k0 + 1, k1))
                    dve.wait_ge(s.silu_ready, count(i, k0 + 1, k1))
                    nc.vector.tensor_tensor(b, b, a, ALU.mult).then_inc(s.act_ready, 1)
                    dve.wait_ge(s.h_hi_ready, count(i, k0 + 1, k1))
                    chunk = count(i, k0, k1)
                    nc.vector.tensor_tensor(h_lo[:, chunk, 0:f.tokens], b, h_hi[:, chunk, 0:f.tokens].bitcast(F32),
                                            ALU.subtract).then_inc(s.h_ready, 1)

                def step_a(parity, k0, k1, i):
                    split_lo(f.unit_a + 2 * k0, KD, i, 2 * k1)
                    if k0 > 1:
                        scale_gate(1 - parity, k0 - 1, k1, i)
                    split_lo(f.unit_a + 2 * k0 + 1, KD, i, 2 * k1)
                    if k0 == 0:
                        at_first()
                    else:
                        if k0 == 1:
                            norm_inverse(norm, f.tokens)
                            scale_gate(0, 0, 0, None)
                        finish_a(1 - parity, k0 - 1, k1, i)

                def finish_b(parity, k0, k1, i):
                    chunk = count(i, k0, k1)
                    x = xT[:, chunk, f.first:L]
                    dve.wait_ge(unit_used, count(i, f.unit_b + 4 * k0 + 4, 4 * k1))
                    total = x if f.n == 0 else scratch_b[parity][:, 0:SEQ]
                    nc.vector.scalar_tensor_tensor(like(total, f.spans), banks(f.down_bank[parity], f.spans), 0.5, like(x, f.spans),
                                                   ALU.mult, ALU.add).then_inc(s.x_updated, 1)
                    if f.n == 0:
                        gained_lo(1, k0, k1, i, 0, L)

                def gain_rows(k0, k1, i):
                    dve.wait_ge(sums_ready, count(i, k0 + 1, k1))
                    cols = bass.ds(count(i, k0 * P, k1 * P), P)
                    for b in range(NB):
                        last = nc.vector.tensor_tensor(y_rows[:, b, cols], ps[:, 6 + k0 % 2, b * P:(b + 1) * P], final_gain[:, cols], ALU.mult)
                    last.then_inc(s.turned_read, 1)

                def step_b(parity, k0, k1, i):
                    for j, (_, n) in enumerate(DOWN_UNITS):
                        if j == 3:
                            if k0 == 0:
                                scale_gate(1, KF - 1, 0, None)
                                finish_a(1, KF - 1, 0, None)
                            else:
                                finish_b(1 - parity, k0 - 1, k1, i)
                        split_lo(f.unit_b + 4 * k0 + j, n, i, 4 * k1)
                    if f.n == 1 and k0 >= 1:
                        gain_rows(k0 - 1, k1, i)

                pairs(dve, KF, step_a)
                if f.n == 1:
                    dve.wait_ge(gain_row_landed, 16)
                pairs(dve, KD, step_b)
                return finish_b, gain_rows

            nc.vector.memset(eps[:], EPS).then_inc(constants_ready, 1)
            dve.wait_ge(small_landed, 16 * SMALL)
            nc.vector.tensor_scalar(neg_sinks[:], sinks[:], -1.0, None, ALU.mult).then_inc(constants_ready, 1)

            def start():
                dve.wait_ge(x_turned, 1)
                nc.vector.tensor_copy(xT[:, :, 0:N_META], ps[:, 3, 0:KD * N_META].rearrange("p (k n) -> p k n", k=KD))

                def copy(k):
                    dve.wait_ge(x_turned, k + 2)
                    nc.vector.tensor_copy(xT[:, k, N_META:L], ps[:, 4 + k % 2, :]).then_inc(x_copied, 1)

                copy(0)
                for k in range(KD):
                    if k + 1 < KD:
                        copy(k + 1)
                    gained_lo(0, k, 0, None, 0, L)

            finish_b, _ = ffn(FFN[0], start, 0)

            K_AT = IN_ORDER.index("k")
            QK = len(IN_ORDER) - K_AT

            def in_finish(e):
                b = scratch_b[e % 2]
                dve.wait_ge(unit_used, U_IN + e + 1)
                if e >= 2:
                    done, value = {"f": (f_ready, e - 1), "v": (v_turned, 1), "k": (qk_normed, 1),
                                   "q": (qk_ready, 4 + 2 * (e - 2 - K_AT))}[IN_ORDER[e - 2][0]]
                    dve.wait_ge(done, value)
                nc.vector.tensor_tensor(like(b[:], HALVES), banks(IN_BANKS[e % 3], HALVES), like(rstd[:], HALVES), ALU.mult).then_inc(in_read, 1)

            def f_low(e):
                c = int(IN_ORDER[e][1])
                dve.wait_ge(f_hi_ready, c + 1)
                nc.vector.tensor_tensor(f_lo[:, c, :], scratch_b[e % 2][:], f_hi[:, c, :].bitcast(F32), ALU.subtract).then_inc(f_ready, 1)

            def v_low():
                dve.wait_ge(v_hi_ready, 2 * N_KV)
                for g in range(N_KV):
                    dims = slice(g * HEAD_DIM, (g + 1) * HEAD_DIM)
                    nc.vector.tensor_tensor(v_lo[:, g, 1:, dims], ps[:, 6, :].rearrange("p (a n) -> p a n", a=NB)[:, :, dims],
                                            v_hi[:, g, 1:, dims].bitcast(F32), ALU.subtract).then_inc(v_ready, 1)
                    nc.vector.tensor_tensor(v_lo[0:N_META, g, 0, dims], ps[0:N_META, 7, dims],
                                            v_hi[0:N_META, g, 0, dims].bitcast(F32), ALU.subtract).then_inc(v_ready, 1)

            def qk_norm(n):
                a, b = scratch_a[(n + K_AT) % 2], scratch_b[(n + K_AT) % 2]
                dve.wait_ge(qk_root_ready, n + 1)
                nc.vector.reciprocal(a[:], a[:]).then_inc(qk_inv_ready, 1)
                dve.wait_ge(qk_inv_ready, n + 1)
                if n == 0:
                    dve.wait_ge(fills_ready, FILLS)
                    for at, first, w in ((0, 0, N_META), (META_W, N_META, SEQ), (META_W + SEQ, 0, N_META)):
                        last = nc.vector.scalar_tensor_tensor(k_rows[:, at:at + w], b[:, first:first + w], qk_gain[:, 1:2],
                                                              a[:, first:first + w], ALU.mult, ALU.mult)
                else:
                    last = nc.vector.scalar_tensor_tensor(b[:], b[:], qk_gain[:, 0:1], a[:], ALU.mult, ALU.mult)
                last.then_inc(qk_normed, 1)

            def qk_low(n):
                if n == 0:
                    for g in range(N_KV):
                        rows = slice(g * HEAD_DIM, (g + 1) * HEAD_DIM)
                        dve.wait_ge(qk_hi_ready, 2 * g + 2)
                        for at in range(2):
                            nc.vector.tensor_tensor(k_lo[at * HEAD_DIM:(at + 1) * HEAD_DIM, g, :], k_rows[rows, :],
                                                    k_hi[rows, g, :].bitcast(F32), ALU.subtract).then_inc(qk_ready, 1)
                else:
                    b = scratch_b[(n + K_AT) % 2]
                    for g in range(N_KV):
                        rows, other = slice(g * HEAD_DIM, (g + 1) * HEAD_DIM), slice((1 - g) * HEAD_DIM, (2 - g) * HEAD_DIM)
                        dve.wait_ge(qk_hi_ready, 4 + 2 * (n - 1) + g + 1)
                        nc.vector.tensor_tensor(q_stack[other, g * GROUP + n - 1, :], b[rows, N_META:L],
                                                q_stack[rows, g * GROUP + n - 1, :].bitcast(F32), ALU.subtract).then_inc(qk_ready, 1)

            split_lo(U_IN, KD)
            for j in range(len(IN_ORDER)):
                if j + 1 < len(IN_ORDER) and j:
                    split_lo(U_IN + j + 1, KD)
                if j == 0:
                    finish_b(1, KD - 1, 0, None)
                    split_lo(U_IN + 1, KD)
                    norm_inverse(1, L)
                else:
                    in_finish(j - 1)
                    if IN_ORDER[j - 1][0] == "f":
                        f_low(j - 1)
                if j == K_AT + 1:
                    v_low()
                if j >= K_AT + 2:
                    qk_norm(j - K_AT - 2)
                    qk_low(j - K_AT - 2)
            in_finish(len(IN_ORDER) - 1)
            qk_norm(QK - 2)
            qk_low(QK - 2)

            def z_low(c):
                bank = 3 * (c % 2)
                dve.wait_ge(z_hi_ready, 2 * (c + 1))
                nc.vector.tensor_tensor(z_lo[c % 2][:, 1:, :].rearrange("p a n -> p (a n)"), ps[:, bank:bank + 2, :].rearrange("p a n -> p (a n)"),
                                        z_hi[c % 2][:, 1:, :].rearrange("p a n -> p (a n)").bitcast(F32), ALU.subtract).then_inc(z_ready, 1)
                nc.vector.tensor_tensor(z_lo[c % 2][0:N_META, 0, :], ps[0:N_META, bank + 2, 0:2 * P],
                                        z_hi[c % 2][0:N_META, 0, :].bitcast(F32), ALU.subtract).then_inc(z_ready, 1)

            def waves(c):
                dve.wait_ge(sine_copied, c + 1)
                cosine, sine = ps[:, 6, 0:HALF], scratch_b[c % 2][:, 0:HALF]
                near = HALF - N_META
                nc.vector.tensor_tensor(f_out[:, c, 0:near], cosine[:, N_META - 1:HALF - 1], sine[:, N_META - 1:HALF - 1], ALU.subtract)
                nc.vector.tensor_tensor(f_out[:, c, near:SEQ][:, ::-1], cosine, sine, ALU.add).then_inc(waves_read, 1)

            z_low(0)
            z_low(1)
            qk_norm(QK - 1)
            qk_low(QK - 1)
            waves(0)
            z_low(2)
            waves(1)
            z_low(3)
            waves(2)
            waves(3)
            dve.wait_ge(z_done, 4)
            for h in range(N_HEADS):
                last = nc.vector.tensor_scalar(slopes[:, h, :], ident, 2.0 ** -(h + 1) * HEAD_DIM ** 0.5, None, ALU.mult)
            last.then_inc(slopes_ready, 1)
            dve.wait_ge(f_root_ready, 1)
            nc.vector.reciprocal(rstd_f[:], rstd_f[:]).then_inc(rstd_f_ready, 1)
            dve.wait_ge(rstd_f_ready, 1)

            def maxima(s, half):
                b, g = STEPS[s]
                n = 2 * s + half
                heads = slice(g * GROUP + 2 * half, g * GROUP + 2 * half + 2)
                dve.wait_ge(scores_done, n + 1)
                nc.vector.tensor_reduce(score_max[:, n, :], ps[:, 2 * half:2 * half + 2, 0:SCORE_W[b]], AX_X, ALU.max).then_inc(max_ready, 1)
                dve.wait_ge(max_ready, n + 1)
                nc.vector.scalar_tensor_tensor(neg_max[:, n, :], score_max[:, n, :], -(HEAD_DIM ** -0.5), neg_sinks[:, heads],
                                               ALU.mult, ALU.min).then_inc(shift_ready, 1)
                dve.wait_ge(shift_ready, 2 * n + 1)
                nc.vector.tensor_tensor(sink_diff[:, n, :], neg_max[:, n, :], sinks[:, heads], ALU.add).then_inc(shift_ready, 1)

            def probs_low(s, j):
                m = SEG_BASE[s] + j
                _, keys, _ = segments(STEPS[s][0])[j]
                dve.wait_ge(pt_hi_ready, m + 1)
                nc.vector.tensor_tensor(pt_lo[m % 2][0:keys].rearrange("p a n -> p (a n)"), ps[0:keys, 4 + m % 2, :],
                                        pt_hi[m % 2][0:keys].rearrange("p a n -> p (a n)").bitcast(F32), ALU.subtract).then_inc(pt_ready, 1)

            def normalize(s):
                b, g = STEPS[s]
                rows, other = slice(g * HEAD_DIM, (g + 1) * HEAD_DIM), slice((1 - g) * HEAD_DIM, (2 - g) * HEAD_DIM)
                dve.wait_ge(pv_used, SEG_BASE[s + 1])
                nc.vector.reciprocal(inv_den[rows].rearrange("p a n -> p (a n)"), ps[other, 6, :]).then_inc(den_inverted, 1)
                dve.wait_ge(den_inverted, s + 1)
                nc.vector.tensor_tensor(attn[b % 2][rows].rearrange("p a n -> p (a n)"), ps[rows, 6, :],
                                        inv_den[rows].rearrange("p a n -> p (a n)"), ALU.mult).then_inc(attn_ready, 1)

            def gain_attn(b):
                dve.wait_ge(attn_ready, 2 * (b + 1))
                need(dve, mix_a_hi_ready, b)
                gain = out_gain[:, 0, :].unsqueeze(2).to_broadcast([P, GROUP, P])
                nc.vector.tensor_tensor(attn_gained[:], attn[b % 2][:], gain, ALU.mult).then_inc(gained_ready, 1)
                dve.wait_ge(mix_a_hi_ready, b + 1)
                nc.vector.tensor_tensor(mix_a_lo[:, :, b * P:(b + 1) * P], attn_gained[:], mix_a_hi[:, :, b * P:(b + 1) * P].bitcast(F32),
                                        ALU.subtract).then_inc(mix_a_ready, 1)

            dve.wait_ge(constants_ready, 2)
            maxima(0, 0)
            maxima(0, 1)
            for c in range(4):
                nc.vector.scalar_tensor_tensor(f_out[:, c, :], f_out[:, c, :], out_gain[:, 1, c:c + 1], rstd_f[:], ALU.mult,
                                               ALU.mult).then_inc(f_normed, 1)
            for c in range(4):
                dve.wait_ge(mix_f_hi_ready, c + 1)
                nc.vector.tensor_tensor(mix_f_lo[:, c, :], f_out[:, c, :], mix_f_hi[:, c, :].bitcast(F32), ALU.subtract).then_inc(mix_f_ready, 1)
            for s in range(len(STEPS)):
                b, g = STEPS[s]
                if s + 1 < len(STEPS):
                    maxima(s + 1, 0)
                probs_low(s, 0)
                if s + 1 < len(STEPS):
                    maxima(s + 1, 1)
                probs_low(s, 1)
                for j in range(2, len(segments(b))):
                    probs_low(s, j)
                if g == 0 and b > 0:
                    gain_attn(b - 1)
                normalize(s)
            gain_attn(NB - 1)

            def out_finish(e):
                p, x = e % 2, xT[:, e, N_META:L]
                dve.wait_ge(unit_used, U_OUT + e + 1)
                nc.vector.tensor_tensor(scratch_b[p][:, 0:SEQ], ps[:, 2 * p + 1, :], rstd_a[:], ALU.mult).then_inc(attn_part_scaled, 1)
                nc.vector.tensor_tensor(x, ps[:, 2 * p, :], x, ALU.add).then_inc(x_plus_f, 1)
                dve.wait_ge(attn_part_scaled, e + 1)
                dve.wait_ge(x_plus_f, e + 1)
                nc.vector.tensor_tensor(x, x, scratch_b[p][:, 0:SEQ], ALU.add).then_inc(x_mixed, 1)
                gained_lo(2, e, 0, None, N_META, SEQ)

            split_lo(U_OUT, KD)
            for d in range(KD):
                if d + 1 < KD:
                    split_lo(U_OUT + d + 1, KD)
                if d == 0:
                    dve.wait_ge(a_root_ready, 1)
                    nc.vector.reciprocal(rstd_a[:], rstd_a[:]).then_inc(rstd_a_ready, 1)
                    dve.wait_ge(rstd_a_ready, 1)
                else:
                    out_finish(d - 1)

            def second_norm():
                out_finish(KD - 1)

            finish_b, gain_rows = ffn(FFN[1], second_norm, 2)
            finish_b(1, KD - 1, 0, None)
            dve.wait_ge(sums_ready, KD)
            nc.vector.tensor_reduce(row_rstd[:], row_sums[:], AX_X, ALU.add).then_inc(mean_ready, 1)
            gain_rows(KD - 1, 0, None)
            dve.wait_ge(final_root, 1)
            nc.vector.reciprocal(row_rstd[:], row_rstd[:]).then_inc(final_rstd, 1)
            dve.wait_ge(final_rstd, 1)
            dve.wait_ge(ffns[1].turned_read, KD)
            for b in range(NB):
                nc.vector.tensor_scalar(y_rows[:, b, :], y_rows[:, b, :], row_rstd[:, b:b + 1], None, ALU.mult).then_inc(rows_scaled, 1)

        @block.tensor
        def _(pe):
            def mm3(outs, hi, lo, x_hi, x_lo, start, stop):
                for n, (w, x) in enumerate(((hi, x_hi), (hi, x_lo), (lo, x_hi))):
                    for o, m in zip(outs, x):
                        last = nc.tensor.matmul(o, w, m, start=start and n == 0, stop=stop and n == 2)
                return last

            def out_spans(bank, spans):
                return [ps[:, bank + a, 0:n] for a, (_, n) in enumerate(spans)]

            def xg(k, spans):
                return [xg_hi[:, k, c:c + n] for c, n in spans], [xg_lo[:, k, c:c + n] for c, n in spans]

            def sum_squares(norm, k, bank, spans, i=None, k1=0):
                pe.wait_ge(norms[norm].sq, count(i, k + 1, k1))
                sq = start_sq[:, k, :] if norm == 0 else scratch_a[k % 2]
                for o, (c, n) in zip(out_spans(bank, spans), spans):
                    last = nc.tensor.matmul(o, ones, sq[:, c:c + n], start=first_sum(k, i), stop=last_sum(k, i),
                                            skip_group_check=True)
                last.then_inc(norms[norm].sq_used, 1)

            def first_sum(k, i):
                return k == 0 and i is None

            def last_sum(k, i):
                return k == KD - 1

            def ffn(f, norm, stat_bank, free):
                s = f.s

                def step_a(parity, k0, k1, i):
                    unit = f.unit_a + 2 * k0
                    gate, up = out_spans(f.gate_bank[parity], f.spans), out_spans(f.up_bank[parity], f.spans)
                    if k0 < 2:
                        free(k0)
                    else:
                        pe.wait_ge(s.up_scaled, count(i, k0 - 1, k1))
                    pe.wait_ge(split_ready, count(i, unit + 1, 2 * k1))
                    g, u = unit % RING, (unit + 1) % RING
                    if k0 == 0:
                        pe.wait_ge(split_ready, unit + 2)
                        for k in range(KD):
                            pe.wait_ge(norms[norm].ready, k + 1)
                            a = mm3(gate, w_hi[g][:, k], w_lo[g][:, k], *xg(k, f.spans), k == 0, k == KD - 1)
                            if k == KD - 1:
                                a.then_inc(unit_used, 1)
                            b = mm3(up, w_hi[u][:, k], w_lo[u][:, k], *xg(k, f.spans), k == 0, k == KD - 1)
                        b.then_inc(unit_used, 1)
                        for k in ([KD - 1] if f.n else range(KD)):
                            sum_squares(norm, k, stat_bank, f.spans)
                        return
                    for k in range(KD):
                        a = mm3(gate, w_hi[g][:, k], w_lo[g][:, k], *xg(k, f.spans), k == 0, k == KD - 1)
                    a.then_inc(unit_used, 1)
                    pe.wait_ge(split_ready, count(i, unit + 2, 2 * k1))
                    for k in range(KD):
                        b = mm3(up, w_hi[u][:, k], w_lo[u][:, k], *xg(k, f.spans), k == 0, k == KD - 1)
                    b.then_inc(unit_used, 1)

                def turn_rows(k, i=None, k1=0):
                    pe.wait_ge(s.x_updated, count(i, k + 1, k1))
                    need(pe, s.turned_read, count(i, k, k1))
                    for b in range(NB):
                        last = nc.tensor.transpose(ps[:, 6 + k % 2, b * P:(b + 1) * P],
                                                   scratch_b[k % 2][:, b * P:(b + 1) * P], ident)
                    last.then_inc(s.turned, 1)

                def step_b(parity, k0, k1, i):
                    y = out_spans(f.down_bank[parity], f.spans)
                    if k0 == 0 and f.n == 0:
                        pe.wait_ge(s.up_scaled, KF - 1)
                    need(pe, s.x_updated, count(i, k0 - 1, k1))
                    for j, (f0, n) in enumerate(DOWN_UNITS):
                        unit = f.unit_b + 4 * k0 + j
                        slot = unit % RING
                        pe.wait_ge(split_ready, count(i, unit + 1, 4 * k1))
                        if k0 == 0:
                            pe.wait_ge(s.h_ready, f0 + n)
                        for m in range(n):
                            h = f0 + m
                            a = mm3(y, w_hi[slot][:, m], w_lo[slot][:, m], [h_hi[:, h, c:c + w] for c, w in f.spans],
                                    [h_lo[:, h, c:c + w] for c, w in f.spans], h == 0, h == KF - 1)
                        a.then_inc(unit_used, 1)
                        if j == 1 and k0 >= 1:
                            if f.n == 0:
                                sum_squares(1, k0 - 1, 6, f.spans, i, k1)
                            else:
                                turn_rows(k0 - 1, i, k1)

                pairs(pe, KF, step_a)
                pairs(pe, KD, step_b)
                return turn_rows

            pe.wait_ge(square_landed, 16)
            pe.wait_ge(x_landed[NB], 16)
            for k in range(KD):
                last = nc.tensor.transpose(ps[:, 3, k * N_META:(k + 1) * N_META], meta_rows[0:N_META, k * P:(k + 1) * P], ident[0:N_META, 0:N_META])
            last.then_inc(x_turned, 1)
            for k in range(KD):
                need(pe, x_copied, k - 1)
                for b in range(NB):
                    if k == 0:
                        pe.wait_ge(x_landed[b], 16)
                    last = nc.tensor.transpose(ps[:, 4 + k % 2, b * P:(b + 1) * P], x_rows[:, b, k * P:(k + 1) * P], ident)
                last.then_inc(x_turned, 1)

            ffn(FFN[0], 0, 6, lambda c: pe.wait_ge(norms[0].root, 1) if c else None)

            K_AT = IN_ORDER.index("k")

            def qk_sums(n):
                a = scratch_a[(n + K_AT) % 2]
                pe.wait_ge(qk_sq_ready, n + 1)
                if n == 0:
                    pe.wait_ge(v_ready, 2 * N_KV)
                else:
                    pe.wait_ge(qk_root_ready, n)
                for o, (c, w) in zip(out_spans(6, HALVES), HALVES):
                    last = nc.tensor.matmul(o, pair_ones, a[:, c:c + w], start=True, stop=True)
                last.then_inc(qk_summed, 1)

            for j, name in enumerate(IN_ORDER):
                slot = (U_IN + j) % RING
                outs = out_spans(IN_BANKS[j % 3], HALVES)
                pe.wait_ge(split_ready, U_IN + j + 1)
                if j >= 3:
                    pe.wait_ge(in_read, j - 2)
                elif j:
                    pe.wait_ge(ffns[0].x_updated, KD - 2 + j)
                for k in range(KD):
                    if j == 0:
                        pe.wait_ge(norms[1].ready, k + 1)
                    last = mm3(outs, w_hi[slot][:, k], w_lo[slot][:, k], *xg(k, HALVES), k == 0, k == KD - 1)
                last.then_inc(unit_used, 1)
                if j == 0:
                    sum_squares(1, KD - 1, 6, HALVES)
                if name == "k":
                    v = scratch_b[IN_ORDER.index("v") % 2]
                    pe.wait_ge(in_read, IN_ORDER.index("v") + 1)
                    pe.wait_ge(norms[1].root, 1)
                    nc.tensor.transpose(ps[0:N_META, 7, 0:P], v[:, 0:N_META], ident)
                    for b in range(NB):
                        last = nc.tensor.transpose(ps[:, 6, b * P:(b + 1) * P], v[:, N_META + b * P:N_META + (b + 1) * P], ident)
                    last.then_inc(v_turned, 1)
                if j > K_AT:
                    qk_sums(j - K_AT - 1)

            def channel_stage(c):
                pe.wait_ge(f_ready, c + 1)
                if c >= 2:
                    pe.wait_ge(z_ready, 2 * (c - 1))
                else:
                    pe.wait_ge(in_read, len(IN_ORDER) - 1 + c)
                bank = 3 * (c % 2)
                for blk in range(1 + NB):
                    if blk == 0:
                        cols, o = slice(0, N_META), ps[0:N_META, bank + 2, 0:2 * P]
                    else:
                        cols = slice(N_META + (blk - 1) * P, N_META + blk * P)
                        o = ps[:, bank + (blk - 1) // 2, (blk - 1) % 2 * 2 * P:((blk - 1) % 2 + 1) * 2 * P]
                    last = mm3([o], f_hi[:, c, cols], f_lo[:, c, cols], [channel_hi[:]], [channel_lo[:]], True, True)
                last.then_inc(z_done, 1)

            def position_stage(c):
                pe.wait_ge(z_ready, 2 * (c + 1))
                if c:
                    pe.wait_ge(waves_read, c)
                else:
                    pe.wait_ge(qk_root_ready, len(IN_ORDER) - K_AT)
                for part in range(2):
                    for blk in range(1 + NB):
                        rows = slice(0, N_META if blk == 0 else P)
                        cols = slice(part * P, (part + 1) * P)
                        last = mm3([ps[:, 6 + part, 0:HALF]], z_hi[c % 2][rows, blk, cols], z_lo[c % 2][rows, blk, cols],
                                   [position_hi[rows, blk, part, :]], [position_lo[rows, blk, part, :]], blk == 0, blk == NB)
                last.then_inc(waves_done, 1)

            pe.wait_ge(mix_tables_landed, 48)
            channel_stage(0)
            qk_sums(len(IN_ORDER) - K_AT - 1)
            channel_stage(1)
            pe.wait_ge(position_landed, 32)
            position_stage(0)
            channel_stage(2)
            position_stage(1)
            channel_stage(3)
            position_stage(2)
            position_stage(3)
            pe.wait_ge(z_ready, 8)
            for c in range(4):
                pe.wait_ge(fsq_ready, c + 1)
                nc.tensor.matmul(ps[:, 0, :], ones, scratch_a[c % 2][:, 0:SEQ], start=c == 0, stop=c == 3).then_inc(fsq_summed, 1)

            def scores(s, half):
                b, g = STEPS[s]
                n = 2 * s + half
                w, at = SCORE_W[b], SCORE_AT[b]
                if s == 0:
                    pe.wait_ge(f_root_ready, 1)
                    pe.wait_ge(slopes_ready, 1)
                    pe.wait_ge(qk_ready, 4 + 2 * GROUP)
                else:
                    pe.wait_ge(exp_done, EXPS * (n - 1))
                for a in range(2):
                    h = g * GROUP + 2 * half + a
                    o = ps[:, 2 * half + a, 0:w]
                    q = q_stack[:, h, b * P:(b + 1) * P]
                    nc.tensor.matmul(o, q, k_hi[:, g, at:at + w], start=True, stop=False)
                    nc.tensor.matmul(o, q, k_lo[:, g, at:at + w], start=False, stop=False)
                    last = nc.tensor.matmul(o, slopes[:, h, :], bias_tab[:, BIAS_AT[b]:BIAS_AT[b] + w], start=False, stop=True)
                last.then_inc(scores_done, 1)

            def turn_probs(s, j):
                b, g = STEPS[s]
                m = SEG_BASE[s] + j
                col, keys, _ = segments(b)[j]
                if j == 0:
                    pe.wait_ge(exp_done, EXPS * (2 * s + 2))
                need(pe, pt_ready, m - 1)
                for a in range(GROUP):
                    last = nc.tensor.transpose(ps[0:keys, 4 + m % 2, a * P:(a + 1) * P], probs[s % 2][:, a, col:col + keys], ident)
                last.then_inc(pt_done, 1)

            def weigh_values(s, j):
                b, g = STEPS[s]
                m = SEG_BASE[s] + j
                _, keys, n = segments(b)[j]
                pe.wait_ge(pt_ready, m + 1)
                if j == 0:
                    need(pe, attn_ready, s)
                ph, pl = (x[m % 2][0:keys].rearrange("p a n -> p (a n)") for x in (pt_hi, pt_lo))
                last = mm3([ps[:, 6, :]], v_hi[0:keys, g, n, :], v_lo[0:keys, g, n, :], [ph], [pl], j == 0, j == len(segments(b)) - 1)
                last.then_inc(pv_used, 1)

            def sum_attn_squares(b):
                pe.wait_ge(attn_sq_ready, b + 1)
                for j in range(GROUP):
                    last = nc.tensor.matmul(ps[:, 7, b * P:(b + 1) * P], ones, attn_sq[:, j, :], start=j == 0, stop=j == GROUP - 1)
                last.then_inc(attn_sq_summed, 1)

            scores(0, 0)
            scores(0, 1)
            pe.wait_ge(waves_read, 4)
            for s in range(len(STEPS)):
                b, g = STEPS[s]
                n_seg = len(segments(b))
                turn_probs(s, 0)
                if s + 1 < len(STEPS):
                    scores(s + 1, 0)
                turn_probs(s, 1)
                weigh_values(s, 0)
                if s + 1 < len(STEPS):
                    scores(s + 1, 1)
                for j in range(2, n_seg):
                    turn_probs(s, j)
                    weigh_values(s, j - 1)
                weigh_values(s, n_seg - 1)
                if g == 1 and b > 0:
                    sum_attn_squares(b - 1)

            def out_part(d, part):
                slot = (U_OUT + d) % RING
                hi, lo = ((mix_f_hi, mix_f_lo), (mix_a_hi, mix_a_lo))[part]
                for k in range(4):
                    last = mm3([ps[:, 2 * (d % 2) + part, :]], w_hi[slot][:, 4 * part + k], w_lo[slot][:, 4 * part + k],
                               [hi[:, k, :]], [lo[:, k, :]], k == 0, k == 3)
                return last

            for d in range(KD):
                pe.wait_ge(split_ready, U_OUT + d + 1)
                if d == 0:
                    pe.wait_ge(exp_done, EXPS * 2 * len(STEPS))
                    pe.wait_ge(mix_f_ready, 4)
                elif d >= 2:
                    pe.wait_ge(x_plus_f, d - 1)
                out_part(d, 0)
                if d == 0:
                    sum_attn_squares(NB - 1)
                    pe.wait_ge(mix_a_ready, NB)
                out_part(d, 1).then_inc(unit_used, 1)
                if d >= 1:
                    if d == 1:
                        pe.wait_ge(attn_ready, 2 * NB)
                    sum_squares(2, d - 1, 6, FFN[1].spans)

            turn_rows = ffn(FFN[1], 2, 6, lambda c: None)
            turn_rows(KD - 1)


SMALL = 3 + 1 + 3 * N_KV + 1
EXPS = 3

_INS = ["x", "meta_tokens", "ffn1_norm", "ffn1_w_gate", "ffn1_w_up", "ffn1_w_down", "mix_norm", "w_in", "q_norm", "k_norm",
        "sink", "attn_out_norm", "fourier_out_norm", "w_out", "ffn2_norm", "ffn2_w_gate", "ffn2_w_up", "ffn2_w_down", "final_norm"]


def kernel(**inputs):
    import concourse.bacc as _bacc
    from concourse.bass_utils import run_bass_kernel_spmd as _run

    nc = _bacc.Bacc("TRN2", target_bir_lowering=False, num_devices=1)
    arrays, tensors = {}, {}
    for name, a in [(n, inputs[n]) for n in _INS] + list(constant_tables().items()):
        a = np.ascontiguousarray(a)
        arrays[f"in_{name}_dram"] = a
        tensors[name] = nc.dram_tensor(f"in_{name}_dram", a.shape, mybir.dt.from_np(a.dtype), kind="ExternalInput").ap()
    out = nc.dram_tensor("out_0_dram", (1, SEQ, D_MODEL), F32, kind="ExternalOutput").ap()
    build(nc, tensors, out)
    r = _run(nc, [arrays], core_ids=[0])
    return r.results[0]["out_0_dram"]
```

```python
from contextlib import ExitStack

import numpy as np

import concourse.bass as bass
from concourse import mybir

F32 = mybir.dt.float32
F32R = mybir.dt.float32r
ALU = mybir.AluOpType
ACT = mybir.ActivationFunctionType
AX_X = mybir.AxisListType.X

P = 128
D_MODEL, SEQ, N_META = 1024, 512, 16
L = SEQ + N_META
HEAD_DIM, N_HEADS, N_KV = 64, 8, 2
GROUP = N_HEADS // N_KV
ATTN_W = N_HEADS * HEAD_DIM
KV_W = N_KV * HEAD_DIM
F_W = 512
F_DIM = 64
IN_W = ATTN_W + 2 * KV_W + F_W
WINDOW = 128
D_FF = 2816
EPS = 1e-6
MASKED = -float(2 ** 100)

KD = D_MODEL // P
KF = D_FF // P
NB = SEQ // P
HALF = L // 2
X_PARTS = 4
X_COLS = D_MODEL // X_PARTS
RING = 4
SLOT = 8
DOWN_UNITS = [(0, 6), (6, 6), (12, 5), (17, 5)]

U_FFN1_A = 0
U_FFN1_B = U_FFN1_A + 2 * KF
U_IN = U_FFN1_B + 4 * KD
U_OUT = U_IN + IN_W // P
U_FFN2_A = U_OUT + KD
U_FFN2_B = U_FFN2_A + 2 * KF

IN_ORDER = ["k", "v", "q0", "q1", "q2", "q3", "f0", "f1", "f2", "f3"]
V_AT = IN_ORDER.index("v")
NORMS = 1 + GROUP
IN_BANKS = [4, 0, 2]

KEYS_W = N_META + SEQ + N_META
SCORE_W = [N_META + 2 * P, N_META + 3 * P, N_META + 3 * P, N_META + 2 * P]
SCORE_AT = [0, 0, N_META + P, N_META + 2 * P]
BIAS_AT = [sum(SCORE_W[:b]) for b in range(NB)]
BIAS_W = sum(SCORE_W)
MAX_W = max(SCORE_W)


def segments(b):
    real = [n for n in (b - 1, b, b + 1) if 0 <= n < NB]
    if b < 2:
        return [(0, N_META, 0)] + [(N_META + P * i, P, n + 1) for i, n in enumerate(real)]
    return [(P * i, P, n + 1) for i, n in enumerate(real)] + [(P * len(real), N_META, 0)]


STEPS = [(b, g) for b in range(NB) for g in range(N_KV)]
SEG_BASE = [sum(len(segments(b)) for b, _ in STEPS[:s]) for s in range(len(STEPS) + 1)]


def split_constant(a):
    a = np.asarray(a, np.float64).astype(np.float32)
    bits = a.view(np.uint32)
    hi = ((bits + np.uint32(0x7FF) + ((bits >> np.uint32(12)) & np.uint32(1))) & np.uint32(0xFFFFF000)).view(np.float32)
    return hi, a - hi


def constant_tables():
    ident = np.eye(P, dtype=np.float32)
    ones = np.ones((P, P), np.float32)
    pair = np.kron(np.eye(2), np.ones((HEAD_DIM, HEAD_DIM))).astype(np.float32)
    square = np.concatenate([ident, ones, pair], axis=1)

    c = np.arange(F_DIM)
    phase = 2 * np.pi * (np.outer(c, c) % F_DIM) / F_DIM
    channel = np.concatenate([np.kron(np.eye(2), np.cos(phase)), np.kron(np.eye(2), np.sin(phase))], axis=1)
    channel = np.stack(split_constant(channel / np.sqrt(F_DIM)))

    pos, t = np.arange(L), np.arange(1, HALF + 1)
    phase = 2 * np.pi * (np.outer(pos, t) % L) / L
    wave = np.stack([np.cos(phase), np.sin(phase)], axis=1) / np.sqrt(L)
    wave[:, 1, HALF - 1] = 0.0
    rows = np.zeros((1 + NB, P, 2, HALF))
    rows[0, :N_META] = wave[:N_META]
    rows[1:] = wave[N_META:].reshape(NB, P, 2, HALF)
    position = np.stack(split_constant(rows.transpose(1, 0, 2, 3).reshape(P, -1)))

    bias = np.full((P, BIAS_W), MASKED, np.float32)
    q = np.arange(P)
    for b in range(NB):
        for col, _, n in segments(b):
            at = BIAS_AT[b] + col
            if n == 0:
                dist = np.abs(N_META + b * P + q[:, None] - np.arange(N_META)[None])
                bias[:, at:at + N_META] = -np.minimum(dist, WINDOW)
            else:
                dist = np.abs(b * P + q[:, None] - ((n - 1) * P + q[None]))
                bias[:, at:at + P] = np.where(dist <= WINDOW, -dist, MASKED)
    return {"square": square, "channel": channel.astype(np.float32),
            "position": position.astype(np.float32), "bias": bias}


class NormSems:

    def __init__(self, sem, name):
        self.hi = sem(f"xg_hi_ready_{name}")
        self.ready = sem(f"xg_ready_{name}")
        self.sq = sem(f"squares_ready_{name}")
        self.sq_added = sem(f"squares_added_{name}")
        self.summed = sem(f"squares_summed_{name}")
        self.root = sem(f"root_ready_{name}")
        self.rstd = sem(f"rstd_ready_{name}")


class FfnSems:

    def __init__(self, sem, name):
        self.gate_scaled = sem(f"gate_scaled_{name}")
        self.silu_ready = sem(f"silu_ready_{name}")
        self.up_scaled = sem(f"up_scaled_{name}")
        self.act_ready = sem(f"act_ready_{name}")
        self.h_hi_ready = sem(f"h_hi_ready_{name}")
        self.h_ready = sem(f"h_ready_{name}")
        self.x_updated = sem(f"x_updated_{name}")
        self.turned = sem(f"turned_{name}")
        self.turned_read = sem(f"turned_read_{name}")


class Ffn:

    def __init__(self, n, first, spans, unit_a, unit_b, gate_bank, up_bank, down_bank, sems):
        self.n, self.first, self.spans, self.tokens = n, first, spans, sum(w for _, w in spans)
        self.unit_a, self.unit_b = unit_a, unit_b
        self.gate_bank, self.up_bank, self.down_bank = gate_bank, up_bank, down_bank
        self.s = sems


def build(nc, t, out):
    with ExitStack() as ctx:
        top = [((nc.sbuf_base + 31) // 32) * 32]

        def width(shape):
            n = 4
            for s in shape[1:]:
                n *= s
            return (n + 31) // 32 * 32

        def persist(name, shape, dt=F32):
            at = top[0]
            top[0] += width(shape)
            return nc.alloc_sbuf_tensor_at(name, shape, dt, offset=at)

        def region(start, items):
            got, at = {}, start
            for name, shape, dt in items:
                got[name] = nc.alloc_sbuf_tensor_at(name, shape, dt, offset=at)
                at += width(shape)
            return got, at

        xT = persist("xT", [P, KD, L])
        rstd = persist("rstd", [P, L])
        square = persist("square", [P, 3, P])
        gains = persist("gains", [P, 3, KD])
        out_gain = persist("out_gain", [P, 2, GROUP])
        qk_gain = persist("qk_gain", [P, 2])
        sinks = persist("sinks", [P, N_HEADS])
        neg_sinks = persist("neg_sinks", [P, N_HEADS])
        eps = persist("eps", [P, 1])
        score_max = persist("score_max", [P, 2 * len(STEPS), 2])
        neg_max = persist("neg_max", [P, 2 * len(STEPS), 2])
        sink_diff = persist("sink_diff", [P, 2 * len(STEPS), 2])
        prob_sums = persist("prob_sums", [P, 2 * len(STEPS), 2])
        sink_exp = persist("sink_exp", [P, 2 * len(STEPS), 2])
        inv_den = persist("inv_den", [P, 2 * len(STEPS), 2])
        row_sums = persist("row_sums", [P, NB, KD])
        row_rstd = persist("row_rstd", [P, NB])
        token_rstd = persist("token_rstd", [P, NB + 1])
        scratch_a = [persist(f"scratch_a{p}", [P, L]) for p in range(2)]
        scratch_b = [persist(f"scratch_b{p}", [P, L]) for p in range(2)]
        raw = [persist(f"raw{s}", [P, SLOT, P]) for s in range(RING)]
        w_hi = [persist(f"w_hi{s}", [P, SLOT, P], F32R) for s in range(RING)]
        w_lo = [persist(f"w_lo{s}", [P, SLOT, P], F32R) for s in range(RING)]
        channel_hi = persist("channel_hi", [P, 2 * P], F32R)
        bias_tab = persist("bias_tab", [P, BIAS_W], F32R)

        x_region = top[0]
        xr, h_region = region(x_region, [("xg_hi", [P, KD, L], F32R), ("xg_lo", [P, KD, L], F32R)])
        xg_hi, xg_lo = xr["xg_hi"], xr["xg_lo"]
        hr, end = region(h_region, [("h_hi", [P, KF, L], F32R), ("h_lo", [P, KF, L], F32R)])
        h_hi, h_lo = hr["h_hi"], hr["h_lo"]
        assert end <= nc.sbuf_usable_end, (end, nc.sbuf_usable_end)

        st, _ = region(end - width([P, NB + 1, D_MODEL]), [("x_rows", [P, NB, D_MODEL], F32), ("meta_rows", [P, D_MODEL], F32)])
        x_rows, meta_rows = st["x_rows"], st["meta_rows"]
        sg, _ = region(h_region, [("squared_rows", [P, D_MODEL], F32), ("rstd_diag", [P, NB + 1, P], F32)])
        squared_rows, rstd_diag = sg["squared_rows"], sg["rstd_diag"]

        mx, mix_end = region(h_region, [
            ("f_hi", [P, 4, L], F32R), ("f_lo", [P, 4, L], F32R),
            ("q_stack", [P, N_HEADS, SEQ], F32R),
            ("k_hi", [P, N_KV, KEYS_W], F32R), ("k_lo", [P, N_KV, KEYS_W], F32R), ("k_norm_rows", [P, KEYS_W], F32),
            ("v_hi", [P, N_KV, 1 + NB, P], F32R), ("v_lo", [P, N_KV, 1 + NB, P], F32R),
            ("rstd_f", [P, SEQ], F32), ("rstd_a", [P, SEQ], F32), ("channel_lo", [P, 2 * P], F32R),
            ("mix_f_hi", [P, 4, SEQ], F32R), ("mix_f_lo", [P, 4, SEQ], F32R),
            ("mix_a_hi", [P, 4, SEQ], F32R), ("mix_a_lo", [P, 4, SEQ], F32R)])
        assert mix_end <= end
        f_hi, f_lo, q_stack, k_hi, k_lo, k_rows = (mx[n] for n in ("f_hi", "f_lo", "q_stack", "k_hi", "k_lo", "k_norm_rows"))
        v_hi, v_lo, rstd_f, rstd_a, channel_lo = (mx[n] for n in ("v_hi", "v_lo", "rstd_f", "rstd_a", "channel_lo"))
        mix_f_hi, mix_f_lo, mix_a_hi, mix_a_lo = (mx[n] for n in ("mix_f_hi", "mix_f_lo", "mix_a_hi", "mix_a_lo"))
        tb, tb_end = region(mix_end - 4 * width([P, 4, SEQ]), [("position_hi", [P, 1 + NB, 2, HALF], F32R),
                                                               ("position_lo", [P, 1 + NB, 2, HALF], F32R)])
        position_hi, position_lo = tb["position_hi"], tb["position_lo"]
        assert tb_end <= mix_end
        fr, fr_end = region(x_region, [("f_out", [P, 4, SEQ], F32), ("z_hi0", [P, 1 + NB, 2 * P], F32R), ("z_lo0", [P, 1 + NB, 2 * P], F32R),
                                       ("z_hi1", [P, 1 + NB, 2 * P], F32R), ("z_lo1", [P, 1 + NB, 2 * P], F32R)])
        assert fr_end <= h_region
        f_out, z_hi, z_lo = fr["f_out"], [fr["z_hi0"], fr["z_hi1"]], [fr["z_lo0"], fr["z_lo1"]]
        ar, ar_end = region(x_region + width([P, 4, SEQ]), [
            ("probs0", [P, GROUP, MAX_W], F32), ("probs1", [P, GROUP, MAX_W], F32),
            ("attn_sq", [P, GROUP, P], F32)])
        assert ar_end <= h_region
        probs, attn_sq = [ar["probs0"], ar["probs1"]], ar["attn_sq"]
        br, br_end = region(h_region, [
            ("slopes", [P, N_HEADS, P], F32R), ("pt_hi0", [P, GROUP, P], F32R), ("pt_lo0", [P, GROUP, P], F32R),
            ("pt_hi1", [P, GROUP, P], F32R), ("pt_lo1", [P, GROUP, P], F32R), ("attn_gained", [P, GROUP, P], F32)])
        assert br_end <= h_region + 2 * width([P, 4, L])
        slopes, attn_gained = br["slopes"], br["attn_gained"]
        pt_hi, pt_lo = [br["pt_hi0"], br["pt_hi1"]], [br["pt_lo0"], br["pt_lo1"]]
        fourier_part = region(h_region, [("fourier_part", [P, 2, SEQ], F32)])[0]["fourier_part"]
        er, er_end = region(x_region, [("y_rows", [P, NB, D_MODEL], F32), ("final_gain", [P, D_MODEL], F32)])
        assert er_end <= h_region
        y_rows, final_gain = er["y_rows"], er["final_gain"]

        ps = ctx.enter_context(nc.psum_tensor("ps", [P, 8, 512], F32))
        ident, ones, pair_ones = square[:, 0, :], square[:, 1, :], square[:, 2, :]

        def sem(name):
            return ctx.enter_context(nc.semaphore(name))

        x_landed = [sem(f"x_landed{i}") for i in range(X_PARTS)]
        meta_landed, first_gain_landed = sem("meta_landed"), sem("first_gain_landed")
        square_landed, small_landed = sem("square_landed"), sem("small_landed")
        mix_tables_landed, position_landed, gain_row_landed = sem("mix_tables_landed"), sem("position_landed"), sem("gain_row_landed")
        raw_landed = [sem(f"raw_landed{s}") for s in range(RING)]
        hi_ready, split_ready, unit_used = sem("hi_ready"), sem("split_ready"), sem("unit_used")
        constants_ready = sem("constants_ready")
        x_turned, x_copied = sem("x_turned"), sem("x_copied")
        rows_squared, token_root_ready, token_inv_ready = sem("rows_squared"), sem("token_root_ready"), sem("token_inv_ready")
        diag_ready, rstd_spread = sem("diag_ready"), sem("rstd_spread")
        norms = [NormSems(sem, n) for n in ("ffn1", "mix", "ffn2")]
        ffns = [FfnSems(sem, n) for n in ("ffn1", "ffn2")]
        in_read = sem("in_read")
        f_hi_ready, f_ready = sem("f_hi_ready"), sem("f_ready")
        fills_ready = sem("fills_ready")
        v_turned, v_hi_ready, v_ready = sem("v_turned"), sem("v_hi_ready"), sem("v_ready")
        qk_sq_ready, qk_summed, qk_root_ready = sem("qk_sq_ready"), sem("qk_summed"), sem("qk_root_ready")
        qk_inv_ready, qk_normed, qk_hi_ready, qk_ready = sem("qk_inv_ready"), sem("qk_normed"), sem("qk_hi_ready"), sem("qk_ready")
        z_done, z_hi_ready, z_ready = sem("z_done"), sem("z_hi_ready"), sem("z_ready")
        waves_done, sine_copied, waves_read = sem("waves_done"), sem("sine_copied"), sem("waves_read")
        fsq_ready, fsq_added, fsq_summed = sem("fsq_ready"), sem("fsq_added"), sem("fsq_summed")
        f_mean_ready, f_inv_ready, f_root_ready = sem("f_mean_ready"), sem("f_inv_ready"), sem("f_root_ready")
        mix_f_hi_ready, mix_f_ready = sem("mix_f_hi_ready"), sem("mix_f_ready")
        slopes_ready, neg_sinks_ready = sem("slopes_ready"), sem("neg_sinks_ready")
        scores_done, max_ready, shift_ready, exp_done = sem("scores_done"), sem("max_ready"), sem("shift_ready"), sem("exp_done")
        pt_done, pt_hi_ready, pt_ready, pv_used = sem("pt_done"), sem("pt_hi_ready"), sem("pt_ready"), sem("pv_used")
        den_ready, den_inverted, probs_scaled = sem("den_ready"), sem("den_inverted"), sem("probs_scaled")
        attn_sq_ready, attn_sq_summed, gained_ready = sem("attn_sq_ready"), sem("attn_sq_summed"), sem("gained_ready")
        mix_a_hi_ready, mix_a_ready = sem("mix_a_hi_ready"), sem("mix_a_ready")
        a_mean_ready, a_inv_ready, a_root_ready = sem("a_mean_ready"), sem("a_inv_ready"), sem("a_root_ready")
        parts_scaled, x_plus_f, x_mixed = sem("parts_scaled"), sem("x_plus_f"), sem("x_mixed")
        sums_ready, mean_ready, final_root, final_rstd, rows_scaled, stored = (
            sem("sums_ready"), sem("mean_ready"), sem("final_root"), sem("final_rstd"), sem("rows_scaled"), sem("stored"))

        def norm_chunk(n):
            return IN_ORDER.index("k" if n == 0 else f"q{n - 1}")

        def count(i, k0, k1=0):
            return k0 if i is None else i * k1 + k0

        def need(eng, semaphore, value):
            if not isinstance(value, int) or value > 0:
                eng.wait_ge(semaphore, value)

        FFN = [Ffn(0, 0, [(0, HALF), (HALF, HALF)], U_FFN1_A, U_FFN1_B, [0, 4], [2, 6], [0, 2], ffns[0]),
               Ffn(1, N_META, [(0, SEQ)], U_FFN2_A, U_FFN2_B, [4, 2], [5, 3], [0, 1], ffns[1])]

        def banks(bank, spans):
            n = spans[0][1]
            return ps[:, bank, 0:n] if len(spans) == 1 else ps[:, bank:bank + 2, 0:n]

        def like(ap, spans):
            return ap if len(spans) == 1 else ap.rearrange("p (a n) -> p a n", a=2)

        HALVES = FFN[0].spans

        def pairs(eng, steps, body):
            body(0, 0, 0, None)
            body(1, 1, 0, None)
            with eng.Fori(0, (steps - 2) // 2) as i:
                body(0, 2, 2, i)
                body(1, 3, 2, i)

        block = ctx.enter_context(nc.Block())

        @block.sync
        def _(sp):
            def raw_slot(n, i=None, per=0):
                need(sp, split_ready, count(i, n + 1 - RING, per))
                return raw[n % RING], raw_landed[n % RING]

            def load_columns(w, unit, column, i=None, per=0):
                slot, landed = raw_slot(unit, i, per)
                sp.dma_start(slot[:], w.rearrange("(k p) n -> p k n", p=P)[:, :, bass.ds(column, P)]).then_inc(landed, 16)

            def ffn(f, after_first, w_gate, w_up, w_down):
                def step_a(parity, k0, k1, i):
                    column = count(i, k0 * P, k1 * P)
                    load_columns(w_gate, f.unit_a + 2 * k0, column, i, 2 * k1)
                    load_columns(w_up, f.unit_a + 2 * k0 + 1, column, i, 2 * k1)
                    if k0 == 0:
                        after_first()

                def step_b(parity, k0, k1, i):
                    for j, (f0, n) in enumerate(DOWN_UNITS):
                        slot, landed = raw_slot(f.unit_b + 4 * k0 + j, i, 4 * k1)
                        src = w_down.rearrange("(k p) n -> p k n", p=P)[:, f0:f0 + n, bass.ds(count(i, k0 * P, k1 * P), P)]
                        sp.dma_start(slot[:, 0:n, :], src).then_inc(landed, 16)

                pairs(sp, KF, step_a)
                pairs(sp, KD, step_b)

            sp.dma_start(square[:], t["square"].rearrange("p (a n) -> p a n", a=3)).then_inc(square_landed, 16)
            x_by_block = t["x"][0].rearrange("(b p) n -> p b n", p=P)

            def load_x(part):
                cols = slice(part * X_COLS, (part + 1) * X_COLS)
                sp.dma_start(x_rows[:, :, cols], x_by_block[:, :, cols]).then_inc(x_landed[part], 16)

            def rest_of_x():
                for part in range(1, X_PARTS):
                    load_x(part)

            load_x(0)
            ffn(FFN[0], rest_of_x, t["ffn1_w_gate"], t["ffn1_w_up"], t["ffn1_w_down"])
            w_in = t["w_in"].rearrange("(k p) n -> p k n", p=P)
            for j, name in enumerate(IN_ORDER):
                slot, landed = raw_slot(U_IN + j)
                if name[0] == "q":
                    for g in range(N_KV):
                        c = (g * GROUP + int(name[1])) * HEAD_DIM
                        sp.dma_start(slot[:, :, g * HEAD_DIM:(g + 1) * HEAD_DIM], w_in[:, :, c:c + HEAD_DIM]).then_inc(landed, 16)
                else:
                    c = ATTN_W + 2 * KV_W + P * int(name[1]) if name[0] == "f" else {"k": ATTN_W, "v": ATTN_W + KV_W}[name]
                    sp.dma_start(slot[:], w_in[:, :, c:c + P]).then_inc(landed, 16)
            for d in range(KD):
                slot, landed = raw_slot(U_OUT + d)
                cols = slice(d * P, (d + 1) * P)
                sp.dma_start(slot[:, 0:4, :], t["w_out"][ATTN_W:, cols].rearrange("(k p) n -> p k n", p=P)).then_inc(landed, 16)
                for g in range(N_KV):
                    rows = slice(g * GROUP * HEAD_DIM, (g + 1) * GROUP * HEAD_DIM)
                    sp.dma_start(slot[g * HEAD_DIM:(g + 1) * HEAD_DIM, 4:8, :],
                                 t["w_out"][rows, cols].rearrange("(j p) n -> p j n", p=HEAD_DIM)).then_inc(landed, 16)
            ffn(FFN[1], lambda: None, t["ffn2_w_gate"], t["ffn2_w_up"], t["ffn2_w_down"])
            for b in range(NB):
                sp.wait_ge(rows_scaled, b + 1)
                sp.dma_start(out[0, b * P:(b + 1) * P, :], y_rows[:, b, :]).then_inc(stored, 16)
            sp.wait_ge(stored, 16 * NB)

        def transfers(n):
            if U_IN <= n < U_OUT:
                return 2 if IN_ORDER[n - U_IN][0] == "q" else 1
            return 3 if U_OUT <= n < U_FFN2_A else 1

        def landed_count(n):
            return 16 * sum(transfers(m) for m in range(n % RING, n + 1, RING))

        @block.gpsimd
        def _(pool):
            with nc.allow_non_contiguous_dma(reason="gains by feature: a few KB"):
                for n, name in enumerate(("mix_norm", "ffn2_norm")):
                    pool.dma_start(gains[:, n + 1, :], t[name].rearrange("(k p) -> p k", p=P)).then_inc(small_landed, 16)
                pool.dma_start(out_gain[:, 1, :], t["fourier_out_norm"].rearrange("(k p) -> p k", p=P)).then_inc(small_landed, 16)
                for g in range(N_KV):
                    rows = slice(g * HEAD_DIM, (g + 1) * HEAD_DIM)
                    width_g = GROUP * HEAD_DIM
                    pool.dma_start(out_gain[rows, 0, :], t["attn_out_norm"][g * width_g:(g + 1) * width_g].rearrange(
                        "(j p) -> p j", p=HEAD_DIM)).then_inc(small_landed, 16)
                    pool.dma_start(qk_gain[rows, 0:1], t["q_norm"].rearrange("(p a) -> p a", a=1)).then_inc(small_landed, 16)
                    pool.dma_start(qk_gain[rows, 1:2], t["k_norm"].rearrange("(p a) -> p a", a=1)).then_inc(small_landed, 16)
                pool.dma_start(sinks[:], t["sink"].rearrange("(a h) -> a h", a=1).to_broadcast([P, N_HEADS])).then_inc(small_landed, 16)
            pool.wait_ge(unit_used, 2)
            pool.dma_start(channel_hi[:], t["channel"][0]).then_inc(mix_tables_landed, 16)
            pool.dma_start(bias_tab[:], t["bias"]).then_inc(mix_tables_landed, 16)
            pool.wait_ge(unit_used, U_IN)
            pool.dma_start(channel_lo[:], t["channel"][1]).then_inc(mix_tables_landed, 16)
            pool.dma_start(position_hi[:], t["position"][0].rearrange("p (a b n) -> p a b n", a=1 + NB, b=2)).then_inc(position_landed, 16)
            pool.dma_start(position_lo[:], t["position"][1].rearrange("p (a b n) -> p a b n", a=1 + NB, b=2)).then_inc(position_landed, 16)
            nc.gpsimd.memset(v_hi[:].bitcast(F32), 0.0).then_inc(fills_ready, 1)
            nc.gpsimd.memset(v_lo[:].bitcast(F32), 0.0).then_inc(fills_ready, 1)
            pool.wait_ge(unit_used, U_FFN2_B)
            pool.dma_start(final_gain[:], t["final_norm"].rearrange("(a n) -> a n", a=1).to_broadcast([P, D_MODEL])).then_inc(gain_row_landed, 16)

        FILLS = 2

        @block.scalar
        def _(act):
            def split_hi(n, tiles, i=None, per=0):
                act.wait_ge(raw_landed[n % RING], count(i, landed_count(n), 16 * per // RING))
                need(act, unit_used, count(i, n + 1 - RING, per))
                nc.scalar.activation(w_hi[n % RING][:, 0:tiles, :], raw[n % RING][:, 0:tiles, :], ACT.Copy).then_inc(hi_ready, 1)

            def gained_hi(norm, ready, k, k1, i, first, spans):
                s = norms[norm]
                chunk = count(i, k, k1)
                n = sum(w for _, w in spans)
                if norm and k:
                    act.wait_ge(s.sq_added, count(i, k, k1))
                act.wait_ge(ready, count(i, k + 1, k1))
                nc.scalar.activation(xg_hi[:, chunk, 0:n], xT[:, chunk, first:first + n], ACT.Copy,
                                     scale=gains[:, norm, bass.ds(chunk, 1)]).then_inc(s.hi, 1)
                if norm == 0:
                    return
                nc.scalar.activation(scratch_a[k % 2][:, 0:n], xT[:, chunk, first:first + n], ACT.Square).then_inc(s.sq, 1)

            def norm_root(norm, bank, spans):
                n = sum(w for _, w in spans)
                act.wait_ge(norms[norm].summed, 1)
                nc.scalar.activation(like(rstd[:, 0:n], spans), banks(bank, spans), ACT.Sqrt, bias=eps[:, 0:1],
                                     scale=1.0 / D_MODEL).then_inc(norms[norm].root, 1)

            def ffn(f, at_first, at_second):
                s = f.s

                def finish_a(parity, k0, k1, i):
                    act.wait_ge(s.gate_scaled, count(i, k0 + 1, k1))
                    a = scratch_a[parity][:, 0:f.tokens]
                    nc.scalar.activation(a, a, ACT.Silu).then_inc(s.silu_ready, 1)
                    act.wait_ge(s.act_ready, count(i, k0 + 1, k1))
                    nc.scalar.activation(h_hi[:, count(i, k0, k1), 0:f.tokens], scratch_b[parity][:, 0:f.tokens],
                                         ACT.Copy).then_inc(s.h_hi_ready, 1)

                def step_a(parity, k0, k1, i):
                    if k0 == 0 and f.n == 0:
                        at_first()
                        return
                    if k0 != 1 or f.n == 1:
                        split_hi(f.unit_a + 2 * k0, KD, i, 2 * k1)
                        split_hi(f.unit_a + 2 * k0 + 1, KD, i, 2 * k1)
                    if k0 == 0:
                        at_first()
                    else:
                        if k0 == 1:
                            at_second()
                        finish_a(1 - parity, k0 - 1, k1, i)

                def finish_b(k0, k1, i):
                    if f.n == 0:
                        gained_hi(1, s.x_updated, k0, k1, i, 0, HALVES)
                    else:
                        act.wait_ge(s.turned, count(i, k0 + 1, k1))
                        for b in range(NB):
                            last = nc.scalar.activation(scratch_a[k0 % 2][:, b * P:(b + 1) * P], ps[:, 6 + k0 % 2, b * P:(b + 1) * P],
                                                        ACT.Square, accum_out=row_sums[:, b, bass.ds(count(i, k0, k1), 1)])
                        last.then_inc(sums_ready, 1)

                def step_b(parity, k0, k1, i):
                    for j, (_, n) in enumerate(DOWN_UNITS):
                        if j == 3:
                            if k0 == 0:
                                finish_a(1, KF - 1, 0, None)
                            else:
                                finish_b(k0 - 1, k1, i)
                        split_hi(f.unit_b + 4 * k0 + j, n, i, 4 * k1)

                pairs(act, KF, step_a)
                if f.n == 0:
                    act.wait_ge(small_landed, 16 * SMALL)
                pairs(act, KD, step_b)

            with nc.allow_non_contiguous_dma(reason="gains by feature: a few KB"):
                act.dma_start(meta_rows[0:N_META, :], t["meta_tokens"]).then_inc(meta_landed, 16)
                act.dma_start(gains[:, 0, :], t["ffn1_norm"].rearrange("(k p) -> p k", p=P)).then_inc(first_gain_landed, 16)

            def start():
                act.wait_ge(first_gain_landed, 16)
                gained_hi(0, x_copied, 0, 0, None, 0, HALVES)
                gained_hi(0, x_copied, 1, 0, None, 0, HALVES)
                split_hi(FFN[0].unit_a, KD)
                split_hi(FFN[0].unit_a + 1, KD)
                act.wait_ge(meta_landed, 16)
                act.wait_ge(constants_ready, 2)
                nc.scalar.activation(squared_rows[0:N_META, :], meta_rows[0:N_META, :], ACT.Square,
                                     accum_out=token_rstd[0:N_META, NB:NB + 1]).then_inc(rows_squared, 1)
                for part in range(X_PARTS):
                    act.wait_ge(x_landed[part], 16)
                for k in range(2, KD):
                    gained_hi(0, x_copied, k, 0, None, 0, HALVES)
                    b = k - 2
                    if b < NB:
                        act.wait_ge(rows_squared, b + 1)
                        nc.scalar.activation(squared_rows[:], x_rows[:, b, :], ACT.Square,
                                             accum_out=token_rstd[:, b:b + 1]).then_inc(rows_squared, 1)
                    elif b == NB:
                        act.wait_ge(rows_squared, NB + 1)
                        nc.scalar.activation(token_rstd[:], token_rstd[:], ACT.Sqrt, bias=eps[:, 0:1],
                                             scale=1.0 / D_MODEL).then_inc(token_root_ready, 1)
                split_hi(FFN[0].unit_a + 2, KD)
                split_hi(FFN[0].unit_a + 3, KD)

            def copy_first_rstd():
                act.wait_ge(rstd_spread, 1)
                nc.scalar.activation(rstd[:, N_META:L], ps[:, 7, :], ACT.Copy)
                nc.scalar.activation(rstd[:, 0:N_META], ps[:, 6, 0:N_META], ACT.Copy).then_inc(norms[0].rstd, 1)

            ffn(FFN[0], start, copy_first_rstd)

            def in_finish(e):
                name = IN_ORDER[e]
                a, b = scratch_a[e % 2], scratch_b[e % 2]
                if name[0] == "f":
                    act.wait_ge(in_read, e + 1)
                    nc.scalar.activation(f_hi[:, int(name[1]), :], b[:], ACT.Copy).then_inc(f_hi_ready, 1)
                elif name != "v":
                    act.wait_ge(in_read, e + 1)
                    nc.scalar.activation(a[:], b[:], ACT.Square).then_inc(qk_sq_ready, 1)

            def v_high():
                act.wait_ge(v_turned, 1)
                act.wait_ge(fills_ready, FILLS)
                for g in range(N_KV):
                    dims = slice(g * HEAD_DIM, (g + 1) * HEAD_DIM)
                    nc.scalar.activation(v_hi[:, g, 1:, dims], ps[:, 6, :].rearrange("p (a n) -> p a n", a=NB)[:, :, dims],
                                         ACT.Copy).then_inc(v_hi_ready, 1)
                    nc.scalar.activation(v_hi[0:N_META, g, 0, dims], ps[0:N_META, 7, dims], ACT.Copy).then_inc(v_hi_ready, 1)

            def qk_root(n):
                act.wait_ge(qk_summed, n + 1)
                a = scratch_a[norm_chunk(n) % 2]
                nc.scalar.activation(like(a[:], HALVES), banks(6, HALVES), ACT.Sqrt, bias=eps[:, 0:1],
                                     scale=1.0 / HEAD_DIM).then_inc(qk_root_ready, 1)

            def qk_hi(n):
                act.wait_ge(qk_normed, n + 1)
                if n == 0:
                    for g in range(N_KV):
                        for at in range(2):
                            nc.scalar.activation(k_hi[at * HEAD_DIM:(at + 1) * HEAD_DIM, g, :],
                                                 k_rows[g * HEAD_DIM:(g + 1) * HEAD_DIM, :], ACT.Copy).then_inc(qk_hi_ready, 1)
                else:
                    b = scratch_b[norm_chunk(n) % 2]
                    for g in range(N_KV):
                        rows = slice(g * HEAD_DIM, (g + 1) * HEAD_DIM)
                        nc.scalar.activation(q_stack[rows, g * GROUP + n - 1, :], b[rows, N_META:L], ACT.Copy).then_inc(qk_hi_ready, 1)

            split_hi(U_IN, KD)
            for j in range(len(IN_ORDER)):
                if j + 1 < len(IN_ORDER) and j:
                    split_hi(U_IN + j + 1, KD)
                if j == 0:
                    gained_hi(1, ffns[0].x_updated, KD - 1, 0, None, 0, HALVES)
                    split_hi(U_IN + 1, KD)
                    norm_root(1, 6, HALVES)
                else:
                    in_finish(j - 1)
                if j - 2 == V_AT:
                    v_high()
                elif 0 <= j - 2 and IN_ORDER[j - 2][0] in "kq":
                    n = max(j - 2 - V_AT, 0)
                    qk_root(n)
                    qk_hi(n)
            in_finish(len(IN_ORDER) - 1)

            def z_split(c):
                act.wait_ge(z_done, c + 1)
                if c >= 2:
                    act.wait_ge(waves_done, c - 1)
                bank = 3 * (c % 2)
                nc.scalar.activation(z_hi[c % 2][:, 1:, :].rearrange("p a n -> p (a n)"), ps[:, bank:bank + 2, :].rearrange("p a n -> p (a n)"),
                                     ACT.Copy).then_inc(z_hi_ready, 1)
                nc.scalar.activation(z_hi[c % 2][0:N_META, 0, :], ps[0:N_META, bank + 2, 0:2 * P], ACT.Copy).then_inc(z_hi_ready, 1)

            def copy_sine(c):
                act.wait_ge(waves_done, c + 1)
                if c >= 2:
                    act.wait_ge(waves_read, c - 1)
                nc.scalar.activation(scratch_b[c % 2][:, 0:HALF], ps[:, 7, 0:HALF], ACT.Copy).then_inc(sine_copied, 1)

            def square_f(c):
                act.wait_ge(waves_read, c + 1)
                need(act, fsq_added, c - 1)
                nc.scalar.activation(scratch_a[c % 2][:, 0:SEQ], f_out[:, c, :], ACT.Square).then_inc(fsq_ready, 1)

            z_split(0)
            z_split(1)
            copy_sine(0)
            z_split(2)
            copy_sine(1)
            square_f(0)
            z_split(3)
            copy_sine(2)
            square_f(1)
            copy_sine(3)

            def exps(s, half):
                b, g = STEPS[s]
                n = 2 * s + half
                act.wait_ge(shift_ready, 2 * (n + 1))
                need(act, pt_done, SEG_BASE[s - 1] if s >= 2 else 0)
                for h in range(2):
                    nc.scalar.activation(probs[s % 2][:, 2 * half + h, 0:SCORE_W[b]], ps[:, 2 * half + h, 0:SCORE_W[b]], ACT.Exp,
                                         bias=neg_max[:, n, h:h + 1], scale=HEAD_DIM ** -0.5,
                                         accum_out=prob_sums[:, n, h:h + 1]).then_inc(exp_done, 1)
                nc.scalar.activation(sink_exp[:, n, :], sink_diff[:, n, :], ACT.Exp).then_inc(exp_done, 1)

            def probs_hi(s, j):
                m = SEG_BASE[s] + j
                _, keys, _ = segments(STEPS[s][0])[j]
                act.wait_ge(pt_done, m + 1)
                need(act, pv_used, m - 1)
                nc.scalar.activation(pt_hi[m % 2][0:keys].rearrange("p a n -> p (a n)"), ps[0:keys, 4 + m % 2, :], ACT.Copy).then_inc(pt_hi_ready, 1)

            def square_attn(b):
                act.wait_ge(pv_used, SEG_BASE[2 * b + 2])
                need(act, attn_sq_summed, b)
                nc.scalar.activation(attn_sq[:].rearrange("p a n -> p (a n)"), ps[:, 6, :], ACT.Square).then_inc(attn_sq_ready, 1)

            def mix_hi(b):
                act.wait_ge(gained_ready, b + 1)
                nc.scalar.activation(mix_a_hi[:, :, b * P:(b + 1) * P], attn_gained[:], ACT.Copy).then_inc(mix_a_hi_ready, 1)

            def fourier_hi(c):
                nc.scalar.activation(mix_f_hi[:, c, :], f_out[:, c, :], ACT.Copy, scale=out_gain[:, 1, c:c + 1]).then_inc(mix_f_hi_ready, 1)

            exps(0, 0)
            exps(0, 1)
            square_f(2)
            square_f(3)
            for s in range(len(STEPS)):
                b, g = STEPS[s]
                n_seg = len(segments(b))
                probs_hi(s, 0)
                probs_hi(s, 1)
                if g == 0 and b > 0:
                    square_attn(b - 1)
                probs_hi(s, 2)
                if s + 1 < len(STEPS):
                    exps(s + 1, 0)
                if n_seg == 4:
                    probs_hi(s, 3)
                if s + 1 < len(STEPS):
                    exps(s + 1, 1)
                if g == 0 and b > 0:
                    mix_hi(b - 1)
                if s < 4:
                    fourier_hi(s)
                elif s < 6:
                    split_hi(U_OUT + s - 4, KD)
            square_attn(NB - 1)
            mix_hi(NB - 1)

            for d in range(KD):
                if d >= 1 and d + 1 < KD:
                    split_hi(U_OUT + d + 1, KD)
                if d == 0:
                    act.wait_ge(f_inv_ready, 1)
                    nc.scalar.activation(rstd_f[:], rstd_f[:], ACT.Sqrt).then_inc(f_root_ready, 1)
                    act.wait_ge(a_inv_ready, NB)
                    nc.scalar.activation(rstd_a[:], rstd_a[:], ACT.Sqrt).then_inc(a_root_ready, 1)
                else:
                    gained_hi(2, x_mixed, d - 1, 0, None, N_META, FFN[1].spans)

            def second_norm():
                gained_hi(2, x_mixed, KD - 1, 0, None, N_META, FFN[1].spans)

            ffn(FFN[1], second_norm, lambda: norm_root(2, 6, FFN[1].spans))
            act.wait_ge(ffns[1].turned, KD)
            for b in range(NB):
                last = nc.scalar.activation(scratch_a[1][:, b * P:(b + 1) * P], ps[:, 7, b * P:(b + 1) * P], ACT.Square,
                                            accum_out=row_sums[:, b, KD - 1:KD])
            last.then_inc(sums_ready, 1)
            act.wait_ge(mean_ready, 1)
            nc.scalar.activation(row_rstd[:], row_rstd[:], ACT.Sqrt, bias=eps[:, 0:1], scale=1.0 / D_MODEL).then_inc(final_root, 1)

        @block.vector
        def _(dve):
            def split_lo(n, tiles, i=None, per=0):
                dve.wait_ge(hi_ready, count(i, n + 1, per))
                s = n % RING
                nc.vector.tensor_tensor(w_lo[s][:, 0:tiles, :], raw[s][:, 0:tiles, :], w_hi[s][:, 0:tiles, :].bitcast(F32),
                                        ALU.subtract).then_inc(split_ready, 1)

            def gained_lo(norm, k, k1, i, first, n):
                chunk = count(i, k, k1)
                dve.wait_ge(norms[norm].hi, count(i, k + 1, k1))
                nc.vector.scalar_tensor_tensor(xg_lo[:, chunk, 0:n], xT[:, chunk, first:first + n], gains[:, norm, bass.ds(chunk, 1)],
                                               xg_hi[:, chunk, 0:n].bitcast(F32), ALU.mult, ALU.subtract).then_inc(norms[norm].ready, 1)

            def add_squares(norm, k, k1, i, n):
                s = norms[norm]
                dve.wait_ge(s.sq, count(i, k + 1, k1))
                if k == 0:
                    nc.vector.tensor_copy(rstd[:, 0:n], scratch_a[0][:, 0:n]).then_inc(s.sq_added, 1)
                    return
                dve.wait_ge(s.sq_added, count(i, k, k1))
                nc.vector.tensor_tensor(rstd[:, 0:n], rstd[:, 0:n], scratch_a[k % 2][:, 0:n], ALU.add).then_inc(s.sq_added, 1)

            def norm_inverse(norm, n):
                dve.wait_ge(norms[norm].root, 1)
                nc.vector.reciprocal(rstd[:, 0:n], rstd[:, 0:n]).then_inc(norms[norm].rstd, 1)
                dve.wait_ge(norms[norm].rstd, 1)

            def first_diag():
                dve.wait_ge(token_root_ready, 1)
                nc.vector.reciprocal(token_rstd[:], token_rstd[:]).then_inc(token_inv_ready, 1)
                dve.wait_ge(token_inv_ready, 1)
                for b in range(NB + 1):
                    last = nc.vector.tensor_scalar(rstd_diag[:, b, :], ident, token_rstd[:, b:b + 1], None, ALU.mult)
                last.then_inc(diag_ready, 1)

            def start():
                dve.wait_ge(first_gain_landed, 16)
                dve.wait_ge(x_turned, 1)
                nc.vector.tensor_copy(xT[:, :, 0:N_META], ps[:, 3, 0:KD * N_META].rearrange("p (k n) -> p k n", k=KD))

                def copy(k):
                    dve.wait_ge(x_turned, k + 2)
                    nc.vector.tensor_copy(xT[:, k, N_META:L], ps[:, 4 + k % 4, :]).then_inc(x_copied, 1)

                copy(0)
                copy(1)
                gained_lo(0, 0, 0, None, 0, L)
                gained_lo(0, 1, 0, None, 0, L)
                split_lo(FFN[0].unit_a, KD)
                split_lo(FFN[0].unit_a + 1, KD)
                copy(2)
                copy(3)
                for k in range(2, KD):
                    gained_lo(0, k, 0, None, 0, L)
                    if k + 2 < KD:
                        copy(k + 2)
                first_diag()

            def ffn(f, at_first, at_second):
                s = f.s
                r = like(rstd[:, 0:f.tokens], f.spans)

                def scale_gate(parity, k0, k1, i):
                    dve.wait_ge(unit_used, count(i, f.unit_a + 2 * k0 + 1, 2 * k1))
                    nc.vector.tensor_tensor(like(scratch_a[parity][:, 0:f.tokens], f.spans), banks(f.gate_bank[parity], f.spans), r,
                                            ALU.mult).then_inc(s.gate_scaled, 1)

                def finish_a(parity, k0, k1, i):
                    a, b = scratch_a[parity][:, 0:f.tokens], scratch_b[parity][:, 0:f.tokens]
                    dve.wait_ge(unit_used, count(i, f.unit_a + 2 * k0 + 2, 2 * k1))
                    nc.vector.tensor_tensor(like(b, f.spans), banks(f.up_bank[parity], f.spans), r, ALU.mult).then_inc(s.up_scaled, 1)
                    dve.wait_ge(s.up_scaled, count(i, k0 + 1, k1))
                    dve.wait_ge(s.silu_ready, count(i, k0 + 1, k1))
                    nc.vector.tensor_tensor(b, b, a, ALU.mult).then_inc(s.act_ready, 1)
                    dve.wait_ge(s.h_hi_ready, count(i, k0 + 1, k1))
                    chunk = count(i, k0, k1)
                    nc.vector.tensor_tensor(h_lo[:, chunk, 0:f.tokens], b, h_hi[:, chunk, 0:f.tokens].bitcast(F32),
                                            ALU.subtract).then_inc(s.h_ready, 1)

                def step_a(parity, k0, k1, i):
                    if k0 == 0 and f.n == 0:
                        at_first()
                        return
                    split_lo(f.unit_a + 2 * k0, KD, i, 2 * k1)
                    if k0 > 1:
                        scale_gate(1 - parity, k0 - 1, k1, i)
                    split_lo(f.unit_a + 2 * k0 + 1, KD, i, 2 * k1)
                    if k0 == 0:
                        at_first()
                    else:
                        if k0 == 1:
                            at_second()
                            scale_gate(0, 0, 0, None)
                        finish_a(1 - parity, k0 - 1, k1, i)

                def finish_b(parity, k0, k1, i):
                    chunk = count(i, k0, k1)
                    x = xT[:, chunk, f.first:L]
                    dve.wait_ge(unit_used, count(i, f.unit_b + 4 * k0 + 4, 4 * k1))
                    total = x if f.n == 0 else scratch_b[parity][:, 0:SEQ]
                    nc.vector.scalar_tensor_tensor(like(total, f.spans), banks(f.down_bank[parity], f.spans), 0.5, like(x, f.spans),
                                                   ALU.mult, ALU.add).then_inc(s.x_updated, 1)
                    if f.n == 0:
                        gained_lo(1, k0, k1, i, 0, L)
                        add_squares(1, k0, k1, i, L)

                def gain_rows(k0, k1, i):
                    dve.wait_ge(sums_ready, count(i, k0 + 1, k1))
                    cols = bass.ds(count(i, k0 * P, k1 * P), P)
                    for b in range(NB):
                        last = nc.vector.tensor_tensor(y_rows[:, b, cols], ps[:, 6 + k0 % 2, b * P:(b + 1) * P], final_gain[:, cols], ALU.mult)
                    last.then_inc(s.turned_read, 1)

                def step_b(parity, k0, k1, i):
                    for j, (_, n) in enumerate(DOWN_UNITS):
                        if j == 3:
                            if k0 == 0:
                                scale_gate(1, KF - 1, 0, None)
                                finish_a(1, KF - 1, 0, None)
                            else:
                                finish_b(1 - parity, k0 - 1, k1, i)
                        split_lo(f.unit_b + 4 * k0 + j, n, i, 4 * k1)
                    if f.n == 1 and k0 >= 1:
                        if k0 == 1:
                            dve.wait_ge(gain_row_landed, 16)
                        gain_rows(k0 - 1, k1, i)

                pairs(dve, KF, step_a)
                if f.n == 0:
                    dve.wait_ge(small_landed, 16 * SMALL)
                pairs(dve, KD, step_b)
                return finish_b, gain_rows

            nc.vector.memset(eps[:], EPS).then_inc(constants_ready, 1)
            nc.vector.memset(token_rstd[:], 0.0).then_inc(constants_ready, 1)

            def first_rstd():
                dve.wait_ge(norms[0].rstd, 1)

            finish_b, _ = ffn(FFN[0], start, first_rstd)

            def in_finish(e):
                b = scratch_b[e % 2]
                dve.wait_ge(unit_used, U_IN + e + 1)
                if e >= 2:
                    done, value = {"k": (qk_normed, 1), "v": (v_turned, 1), "q": (qk_ready, 4 + 2 * (e - 2 - V_AT)),
                                   "f": (f_ready, e - 2 - IN_ORDER.index("f0") + 1)}[IN_ORDER[e - 2][0]]
                    dve.wait_ge(done, value)
                nc.vector.tensor_tensor(like(b[:], HALVES), banks(IN_BANKS[e % 3], HALVES), like(rstd[:], HALVES), ALU.mult).then_inc(in_read, 1)

            def f_low(e):
                c = int(IN_ORDER[e][1])
                dve.wait_ge(f_hi_ready, c + 1)
                nc.vector.tensor_tensor(f_lo[:, c, :], scratch_b[e % 2][:], f_hi[:, c, :].bitcast(F32), ALU.subtract).then_inc(f_ready, 1)

            def v_low():
                dve.wait_ge(v_hi_ready, 2 * N_KV)
                for g in range(N_KV):
                    dims = slice(g * HEAD_DIM, (g + 1) * HEAD_DIM)
                    nc.vector.tensor_tensor(v_lo[:, g, 1:, dims], ps[:, 6, :].rearrange("p (a n) -> p a n", a=NB)[:, :, dims],
                                            v_hi[:, g, 1:, dims].bitcast(F32), ALU.subtract).then_inc(v_ready, 1)
                    nc.vector.tensor_tensor(v_lo[0:N_META, g, 0, dims], ps[0:N_META, 7, dims],
                                            v_hi[0:N_META, g, 0, dims].bitcast(F32), ALU.subtract).then_inc(v_ready, 1)

            def qk_norm(n):
                a, b = scratch_a[norm_chunk(n) % 2], scratch_b[norm_chunk(n) % 2]
                dve.wait_ge(qk_root_ready, n + 1)
                nc.vector.reciprocal(a[:], a[:]).then_inc(qk_inv_ready, 1)
                dve.wait_ge(qk_inv_ready, n + 1)
                if n == 0:
                    for at, first, w in ((0, 0, N_META), (N_META, N_META, SEQ), (N_META + SEQ, 0, N_META)):
                        last = nc.vector.scalar_tensor_tensor(k_rows[:, at:at + w], b[:, first:first + w], qk_gain[:, 1:2],
                                                              a[:, first:first + w], ALU.mult, ALU.mult)
                else:
                    last = nc.vector.scalar_tensor_tensor(b[:], b[:], qk_gain[:, 0:1], a[:], ALU.mult, ALU.mult)
                last.then_inc(qk_normed, 1)

            def qk_low(n):
                if n == 0:
                    for g in range(N_KV):
                        rows = slice(g * HEAD_DIM, (g + 1) * HEAD_DIM)
                        dve.wait_ge(qk_hi_ready, 2 * g + 2)
                        for at in range(2):
                            nc.vector.tensor_tensor(k_lo[at * HEAD_DIM:(at + 1) * HEAD_DIM, g, :], k_rows[rows, :],
                                                    k_hi[rows, g, :].bitcast(F32), ALU.subtract).then_inc(qk_ready, 1)
                else:
                    b = scratch_b[norm_chunk(n) % 2]
                    for g in range(N_KV):
                        rows, other = slice(g * HEAD_DIM, (g + 1) * HEAD_DIM), slice((1 - g) * HEAD_DIM, (2 - g) * HEAD_DIM)
                        dve.wait_ge(qk_hi_ready, 4 + 2 * (n - 1) + g + 1)
                        nc.vector.tensor_tensor(q_stack[other, g * GROUP + n - 1, :], b[rows, N_META:L],
                                                q_stack[rows, g * GROUP + n - 1, :].bitcast(F32), ALU.subtract).then_inc(qk_ready, 1)

            split_lo(U_IN, KD)
            for j in range(len(IN_ORDER)):
                if j == 0:
                    finish_b(1, KD - 1, 0, None)
                    split_lo(U_IN + 1, KD)
                    norm_inverse(1, L)
                else:
                    in_finish(j - 1)
                    if j + 1 < len(IN_ORDER):
                        split_lo(U_IN + j + 1, KD)
                    if IN_ORDER[j - 1][0] == "f":
                        f_low(j - 1)
                if j - 2 == V_AT:
                    v_low()
                elif 0 <= j - 2 and IN_ORDER[j - 2][0] in "kq":
                    n = max(j - 2 - V_AT, 0)
                    qk_norm(n)
                    qk_low(n)
            in_finish(len(IN_ORDER) - 1)
            f_low(len(IN_ORDER) - 1)

            def z_low(c):
                bank = 3 * (c % 2)
                dve.wait_ge(z_hi_ready, 2 * (c + 1))
                nc.vector.tensor_tensor(z_lo[c % 2][:, 1:, :].rearrange("p a n -> p (a n)"), ps[:, bank:bank + 2, :].rearrange("p a n -> p (a n)"),
                                        z_hi[c % 2][:, 1:, :].rearrange("p a n -> p (a n)").bitcast(F32), ALU.subtract).then_inc(z_ready, 1)
                nc.vector.tensor_tensor(z_lo[c % 2][0:N_META, 0, :], ps[0:N_META, bank + 2, 0:2 * P],
                                        z_hi[c % 2][0:N_META, 0, :].bitcast(F32), ALU.subtract).then_inc(z_ready, 1)

            def waves(c):
                dve.wait_ge(sine_copied, c + 1)
                cosine, sine = ps[:, 6, 0:HALF], scratch_b[c % 2][:, 0:HALF]
                near = HALF - N_META
                nc.vector.tensor_tensor(f_out[:, c, 0:near], cosine[:, N_META - 1:HALF - 1], sine[:, N_META - 1:HALF - 1], ALU.subtract)
                nc.vector.tensor_tensor(f_out[:, c, near:SEQ][:, ::-1], cosine, sine, ALU.add).then_inc(waves_read, 1)

            def add_f_squares(c):
                dve.wait_ge(fsq_ready, c + 1)
                if c == 0:
                    nc.vector.tensor_copy(rstd_f[:], scratch_a[0][:, 0:SEQ]).then_inc(fsq_added, 1)
                    return
                dve.wait_ge(fsq_added, c)
                nc.vector.tensor_tensor(rstd_f[:], rstd_f[:], scratch_a[c % 2][:, 0:SEQ], ALU.add).then_inc(fsq_added, 1)

            def set_slopes():
                dve.wait_ge(z_done, 4)
                for h in range(N_HEADS):
                    last = nc.vector.tensor_scalar(slopes[:, h, :], ident, 2.0 ** -(h + 1) * HEAD_DIM ** 0.5, None, ALU.mult)
                last.then_inc(slopes_ready, 1)

            z_low(0)
            z_low(1)
            nc.vector.tensor_scalar(neg_sinks[:], sinks[:], -1.0, None, ALU.mult).then_inc(neg_sinks_ready, 1)
            waves(0)
            z_low(2)
            waves(1)
            z_low(3)
            set_slopes()
            waves(2)
            add_f_squares(0)
            add_f_squares(1)

            def maxima(s, half):
                b, g = STEPS[s]
                n = 2 * s + half
                heads = slice(g * GROUP + 2 * half, g * GROUP + 2 * half + 2)
                dve.wait_ge(scores_done, n + 1)
                nc.vector.tensor_reduce(score_max[:, n, :], ps[:, 2 * half:2 * half + 2, 0:SCORE_W[b]], AX_X, ALU.max).then_inc(max_ready, 1)
                dve.wait_ge(max_ready, n + 1)
                nc.vector.scalar_tensor_tensor(neg_max[:, n, :], score_max[:, n, :], -(HEAD_DIM ** -0.5), neg_sinks[:, heads],
                                               ALU.mult, ALU.min).then_inc(shift_ready, 1)
                dve.wait_ge(shift_ready, 2 * n + 1)
                nc.vector.tensor_tensor(sink_diff[:, n, :], neg_max[:, n, :], sinks[:, heads], ALU.add).then_inc(shift_ready, 1)

            def probs_low(s, j):
                m = SEG_BASE[s] + j
                _, keys, _ = segments(STEPS[s][0])[j]
                dve.wait_ge(pt_hi_ready, m + 1)
                nc.vector.tensor_tensor(pt_lo[m % 2][0:keys].rearrange("p a n -> p (a n)"), ps[0:keys, 4 + m % 2, :],
                                        pt_hi[m % 2][0:keys].rearrange("p a n -> p (a n)").bitcast(F32), ALU.subtract).then_inc(pt_ready, 1)

            def normalize(s, half):
                n = 2 * s + half
                dve.wait_ge(exp_done, EXPS * (n + 1))
                nc.vector.tensor_tensor(inv_den[:, n, :], prob_sums[:, n, :], sink_exp[:, n, :], ALU.add).then_inc(den_ready, 1)
                dve.wait_ge(den_ready, n + 1)
                nc.vector.reciprocal(inv_den[:, n, :], inv_den[:, n, :]).then_inc(den_inverted, 1)
                dve.wait_ge(den_inverted, n + 1)
                for h in range(2):
                    p = probs[s % 2][:, 2 * half + h, 0:SCORE_W[STEPS[s][0]]]
                    last = nc.vector.tensor_scalar(p, p, inv_den[:, n, h:h + 1], None, ALU.mult)
                last.then_inc(probs_scaled, 1)

            def gain_attn(b):
                dve.wait_ge(attn_sq_ready, b + 1)
                need(dve, mix_a_ready, b)
                gain = out_gain[:, 0, :].unsqueeze(2).to_broadcast([P, GROUP, P])
                nc.vector.tensor_tensor(attn_gained[:], ps[:, 6, :].rearrange("p (a n) -> p a n", a=GROUP), gain, ALU.mult).then_inc(gained_ready, 1)

            def mix_low(b):
                dve.wait_ge(mix_a_hi_ready, b + 1)
                nc.vector.tensor_tensor(mix_a_lo[:, :, b * P:(b + 1) * P], attn_gained[:], mix_a_hi[:, :, b * P:(b + 1) * P].bitcast(F32),
                                        ALU.subtract).then_inc(mix_a_ready, 1)

            def inverse_mean(sums, into, width, mean_ready, inv_ready, n):
                nc.vector.tensor_scalar(into, sums, 1.0 / width, EPS, ALU.mult, ALU.add).then_inc(mean_ready, 1)
                dve.wait_ge(mean_ready, n)
                nc.vector.reciprocal(into, into).then_inc(inv_ready, 1)

            def attn_inverse(b):
                dve.wait_ge(attn_sq_summed, b + 1)
                cols = slice(b * P, (b + 1) * P)
                inverse_mean(ps[:, 7, cols], rstd_a[:, cols], ATTN_W, a_mean_ready, a_inv_ready, b + 1)

            def fourier_lo(c):
                dve.wait_ge(mix_f_hi_ready, c + 1)
                nc.vector.scalar_tensor_tensor(mix_f_lo[:, c, :], f_out[:, c, :], out_gain[:, 1, c:c + 1], mix_f_hi[:, c, :].bitcast(F32),
                                               ALU.mult, ALU.subtract).then_inc(mix_f_ready, 1)

            dve.wait_ge(neg_sinks_ready, 1)
            maxima(0, 0)
            maxima(0, 1)
            waves(3)
            normalize(0, 0)
            normalize(0, 1)
            add_f_squares(2)
            add_f_squares(3)
            for s in range(len(STEPS)):
                b, g = STEPS[s]
                probs_low(s, 0)
                probs_low(s, 1)
                if g == 0 and b > 0:
                    gain_attn(b - 1)
                if s + 1 < len(STEPS):
                    maxima(s + 1, 0)
                probs_low(s, 2)
                if s + 1 < len(STEPS):
                    maxima(s + 1, 1)
                    normalize(s + 1, 0)
                if len(segments(b)) == 4:
                    probs_low(s, 3)
                if s + 1 < len(STEPS):
                    normalize(s + 1, 1)
                if g == 0 and b > 0:
                    mix_low(b - 1)
                if g == 1 and b > 0:
                    attn_inverse(b - 1)
                if s < 4:
                    fourier_lo(s)
                elif s < 6:
                    split_lo(U_OUT + s - 4, KD)
                if s == 1:
                    dve.wait_ge(fsq_summed, 1)
                    inverse_mean(ps[:, 7, :], rstd_f[:], F_W, f_mean_ready, f_inv_ready, 1)
            gain_attn(NB - 1)
            mix_low(NB - 1)
            attn_inverse(NB - 1)

            def out_finish(e):
                p, x = e % 2, xT[:, e, N_META:L]
                dve.wait_ge(unit_used, U_OUT + e + 1)
                nc.vector.tensor_tensor(fourier_part[:, p, :], ps[:, 2 * p, :], rstd_f[:], ALU.mult).then_inc(parts_scaled, 1)
                if e == 0:
                    dve.wait_ge(a_root_ready, 1)
                nc.vector.tensor_tensor(scratch_b[p][:, 0:SEQ], ps[:, 2 * p + 1, :], rstd_a[:], ALU.mult).then_inc(parts_scaled, 1)
                dve.wait_ge(parts_scaled, 2 * e + 1)
                nc.vector.tensor_tensor(x, x, fourier_part[:, p, :], ALU.add).then_inc(x_plus_f, 1)
                dve.wait_ge(parts_scaled, 2 * e + 2)
                dve.wait_ge(x_plus_f, e + 1)
                nc.vector.tensor_tensor(x, x, scratch_b[p][:, 0:SEQ], ALU.add).then_inc(x_mixed, 1)
                gained_lo(2, e, 0, None, N_META, SEQ)
                add_squares(2, e, 0, None, SEQ)

            for d in range(KD):
                if d >= 1 and d + 1 < KD:
                    split_lo(U_OUT + d + 1, KD)
                if d == 0:
                    dve.wait_ge(f_root_ready, 1)
                else:
                    out_finish(d - 1)

            def last_of_x():
                out_finish(KD - 1)

            finish_b, gain_rows = ffn(FFN[1], last_of_x, lambda: norm_inverse(2, SEQ))
            finish_b(1, KD - 1, 0, None)
            dve.wait_ge(sums_ready, KD)
            nc.vector.tensor_reduce(row_rstd[:], row_sums[:], AX_X, ALU.add).then_inc(mean_ready, 1)
            gain_rows(KD - 1, 0, None)
            dve.wait_ge(final_root, 1)
            nc.vector.reciprocal(row_rstd[:], row_rstd[:]).then_inc(final_rstd, 1)
            dve.wait_ge(final_rstd, 1)
            dve.wait_ge(ffns[1].turned_read, KD)
            for b in range(NB):
                nc.vector.tensor_scalar(y_rows[:, b, :], y_rows[:, b, :], row_rstd[:, b:b + 1], None, ALU.mult).then_inc(rows_scaled, 1)

        @block.tensor
        def _(pe):
            def mm3(outs, hi, lo, x_hi, x_lo, start, stop):
                for n, (w, x) in enumerate(((hi, x_hi), (hi, x_lo), (lo, x_hi))):
                    for o, m in zip(outs, x):
                        last = nc.tensor.matmul(o, w, m, start=start and n == 0, stop=stop and n == 2)
                return last

            def out_spans(bank, spans):
                return [ps[:, bank + a, 0:n] for a, (_, n) in enumerate(spans)]

            def xg(k, spans):
                return [xg_hi[:, k, c:c + n] for c, n in spans], [xg_lo[:, k, c:c + n] for c, n in spans]

            def sum_squares(norm, bank, spans):
                pe.wait_ge(norms[norm].sq_added, KD)
                for o, (c, n) in zip(out_spans(bank, spans), spans):
                    last = nc.tensor.matmul(o, ones, rstd[:, c:c + n], start=True, stop=True)
                last.then_inc(norms[norm].summed, 1)

            def ffn(f, norm, with_first, after_first, free):
                s = f.s

                def step_a(parity, k0, k1, i):
                    unit = f.unit_a + 2 * k0
                    gate, up = out_spans(f.gate_bank[parity], f.spans), out_spans(f.up_bank[parity], f.spans)
                    if k0 < 2:
                        free(k0)
                    else:
                        pe.wait_ge(s.up_scaled, count(i, k0 - 1, k1))
                    pe.wait_ge(split_ready, count(i, unit + 1, 2 * k1))
                    g, u = unit % RING, (unit + 1) % RING
                    if k0 == 0:
                        for k in range(KD):
                            pe.wait_ge(norms[norm].ready, k + 1)
                            a = mm3(gate, w_hi[g][:, k], w_lo[g][:, k], *xg(k, f.spans), k == 0, k == KD - 1)
                            if k == KD - 1:
                                a.then_inc(unit_used, 1)
                            if k == 0:
                                pe.wait_ge(split_ready, unit + 2)
                            b = mm3(up, w_hi[u][:, k], w_lo[u][:, k], *xg(k, f.spans), k == 0, k == KD - 1)
                            with_first(k)
                        b.then_inc(unit_used, 1)
                        after_first()
                        return
                    for k in range(KD):
                        a = mm3(gate, w_hi[g][:, k], w_lo[g][:, k], *xg(k, f.spans), k == 0, k == KD - 1)
                    a.then_inc(unit_used, 1)
                    pe.wait_ge(split_ready, count(i, unit + 2, 2 * k1))
                    for k in range(KD):
                        b = mm3(up, w_hi[u][:, k], w_lo[u][:, k], *xg(k, f.spans), k == 0, k == KD - 1)
                    b.then_inc(unit_used, 1)

                def turn_rows(k, i=None, k1=0):
                    pe.wait_ge(s.x_updated, count(i, k + 1, k1))
                    need(pe, s.turned_read, count(i, k, k1))
                    for b in range(NB):
                        last = nc.tensor.transpose(ps[:, 6 + k % 2, b * P:(b + 1) * P],
                                                   scratch_b[k % 2][:, b * P:(b + 1) * P], ident)
                    last.then_inc(s.turned, 1)

                def step_b(parity, k0, k1, i):
                    y = out_spans(f.down_bank[parity], f.spans)
                    if k0 == 0 and f.n == 0:
                        pe.wait_ge(s.up_scaled, KF - 1)
                    need(pe, s.x_updated, count(i, k0 - 1, k1))
                    for j, (f0, n) in enumerate(DOWN_UNITS):
                        unit = f.unit_b + 4 * k0 + j
                        slot = unit % RING
                        pe.wait_ge(split_ready, count(i, unit + 1, 4 * k1))
                        if k0 == 0:
                            pe.wait_ge(s.h_ready, f0 + n)
                        for m in range(n):
                            h = f0 + m
                            a = mm3(y, w_hi[slot][:, m], w_lo[slot][:, m], [h_hi[:, h, c:c + w] for c, w in f.spans],
                                    [h_lo[:, h, c:c + w] for c, w in f.spans], h == 0, h == KF - 1)
                        a.then_inc(unit_used, 1)
                        if j == 1 and k0 >= 1 and f.n == 1:
                            turn_rows(k0 - 1, i, k1)

                pairs(pe, KF, step_a)
                pairs(pe, KD, step_b)
                return turn_rows

            pe.wait_ge(square_landed, 16)
            pe.wait_ge(meta_landed, 16)
            for k in range(KD):
                last = nc.tensor.transpose(ps[:, 3, k * N_META:(k + 1) * N_META], meta_rows[0:N_META, k * P:(k + 1) * P], ident[0:N_META, 0:N_META])
            last.then_inc(x_turned, 1)

            def turn_x(k):
                need(pe, x_copied, k - 3)
                if k % (X_COLS // P) == 0:
                    pe.wait_ge(x_landed[k * P // X_COLS], 16)
                for b in range(NB):
                    last = nc.tensor.transpose(ps[:, 4 + k % 4, b * P:(b + 1) * P], x_rows[:, b, k * P:(k + 1) * P], ident)
                last.then_inc(x_turned, 1)

            def spread_rstd():
                pe.wait_ge(diag_ready, 1)
                nc.tensor.matmul(ps[:, 6, 0:N_META], ones[0:N_META, :], rstd_diag[0:N_META, NB, 0:N_META], start=True, stop=True)
                for b in range(NB):
                    last = nc.tensor.matmul(ps[:, 7, b * P:(b + 1) * P], ones, rstd_diag[:, b, :], start=True, stop=True)
                last.then_inc(rstd_spread, 1)

            turn_x(0)
            turn_x(1)

            def turn_more(k):
                for ahead in ([2, 3] if k == 0 else [k + 3]):
                    if ahead < KD:
                        turn_x(ahead)

            ffn(FFN[0], 0, turn_more, spread_rstd,
                lambda c: pe.wait_ge(norms[0].rstd, 1) if c else None)

            def qk_sums(n):
                a = scratch_a[norm_chunk(n) % 2]
                pe.wait_ge(qk_sq_ready, n + 1)
                if n == 0:
                    pe.wait_ge(norms[1].root, 1)
                elif n == 1:
                    pe.wait_ge(v_ready, 2 * N_KV)
                else:
                    pe.wait_ge(qk_root_ready, n)
                for o, (c, w) in zip(out_spans(6, HALVES), HALVES):
                    last = nc.tensor.matmul(o, pair_ones, a[:, c:c + w], start=True, stop=True)
                last.then_inc(qk_summed, 1)

            def turn_values():
                v = scratch_b[V_AT % 2]
                pe.wait_ge(in_read, V_AT + 1)
                pe.wait_ge(qk_root_ready, 1)
                nc.tensor.transpose(ps[0:N_META, 7, 0:P], v[:, 0:N_META], ident)
                for b in range(NB):
                    last = nc.tensor.transpose(ps[:, 6, b * P:(b + 1) * P], v[:, N_META + b * P:N_META + (b + 1) * P], ident)
                last.then_inc(v_turned, 1)

            for j, name in enumerate(IN_ORDER):
                slot = (U_IN + j) % RING
                outs = out_spans(IN_BANKS[j % 3], HALVES)
                pe.wait_ge(split_ready, U_IN + j + 1)
                if j >= 3:
                    pe.wait_ge(in_read, j - 2)
                elif j:
                    pe.wait_ge(ffns[0].x_updated, KD - 2 + j)
                for k in range(KD):
                    if j == 0:
                        pe.wait_ge(norms[1].ready, k + 1)
                    last = mm3(outs, w_hi[slot][:, k], w_lo[slot][:, k], *xg(k, HALVES), k == 0, k == KD - 1)
                last.then_inc(unit_used, 1)
                if j == 0:
                    sum_squares(1, 6, HALVES)
                elif j - 1 == V_AT:
                    turn_values()
                elif IN_ORDER[j - 1][0] in "kq":
                    qk_sums(max(j - 1 - V_AT, 0))

            def channel_stage(c):
                pe.wait_ge(f_ready, c + 1)
                if c >= 2:
                    pe.wait_ge(z_ready, 2 * (c - 1))
                else:
                    pe.wait_ge(in_read, len(IN_ORDER) - 1 + c)
                bank = 3 * (c % 2)
                for blk in range(1 + NB):
                    if blk == 0:
                        cols, o = slice(0, N_META), ps[0:N_META, bank + 2, 0:2 * P]
                    else:
                        cols = slice(N_META + (blk - 1) * P, N_META + blk * P)
                        o = ps[:, bank + (blk - 1) // 2, (blk - 1) % 2 * 2 * P:((blk - 1) % 2 + 1) * 2 * P]
                    last = mm3([o], f_hi[:, c, cols], f_lo[:, c, cols], [channel_hi[:]], [channel_lo[:]], True, True)
                last.then_inc(z_done, 1)

            def position_stage(c):
                pe.wait_ge(z_ready, 2 * (c + 1))
                if c:
                    pe.wait_ge(waves_read, c)
                else:
                    pe.wait_ge(qk_root_ready, NORMS)
                for part in range(2):
                    for blk in range(1 + NB):
                        rows = slice(0, N_META if blk == 0 else P)
                        cols = slice(part * P, (part + 1) * P)
                        last = mm3([ps[:, 6 + part, 0:HALF]], z_hi[c % 2][rows, blk, cols], z_lo[c % 2][rows, blk, cols],
                                   [position_hi[rows, blk, part, :]], [position_lo[rows, blk, part, :]], blk == 0, blk == NB)
                last.then_inc(waves_done, 1)

            def scores(s, half):
                b, g = STEPS[s]
                n = 2 * s + half
                w, at = SCORE_W[b], SCORE_AT[b]
                if s == 0:
                    pe.wait_ge(z_ready, 8)
                    pe.wait_ge(slopes_ready, 1)
                    pe.wait_ge(qk_ready, 4 + 2 * GROUP)
                else:
                    pe.wait_ge(exp_done, EXPS * (n - 1))
                for a in range(2):
                    h = g * GROUP + 2 * half + a
                    o = ps[:, 2 * half + a, 0:w]
                    q = q_stack[:, h, b * P:(b + 1) * P]
                    nc.tensor.matmul(o, q, k_hi[:, g, at:at + w], start=True, stop=False)
                    nc.tensor.matmul(o, q, k_lo[:, g, at:at + w], start=False, stop=False)
                    last = nc.tensor.matmul(o, slopes[:, h, :], bias_tab[:, BIAS_AT[b]:BIAS_AT[b] + w], start=False, stop=True)
                last.then_inc(scores_done, 1)

            def turn_probs(s, j):
                b, g = STEPS[s]
                m = SEG_BASE[s] + j
                col, keys, _ = segments(b)[j]
                need(pe, pt_ready, m - 1)
                for a in range(GROUP):
                    if j == 0 and a % 2 == 0:
                        pe.wait_ge(probs_scaled, 2 * s + a // 2 + 1)
                    last = nc.tensor.transpose(ps[0:keys, 4 + m % 2, a * P:(a + 1) * P], probs[s % 2][:, a, col:col + keys], ident)
                last.then_inc(pt_done, 1)

            def weigh_values(s, j):
                b, g = STEPS[s]
                m = SEG_BASE[s] + j
                _, keys, n = segments(b)[j]
                pe.wait_ge(pt_ready, m + 1)
                if j == 0 and g == 0:
                    need(pe, gained_ready, b)
                ph, pl = (x[m % 2][0:keys].rearrange("p a n -> p (a n)") for x in (pt_hi, pt_lo))
                last = mm3([ps[:, 6, :]], v_hi[0:keys, g, n, :], v_lo[0:keys, g, n, :], [ph], [pl],
                           g == 0 and j == 0, g == N_KV - 1 and j == len(segments(b)) - 1)
                last.then_inc(pv_used, 1)

            def sum_attn_squares(b):
                pe.wait_ge(attn_sq_ready, b + 1)
                if b == 0:
                    pe.wait_ge(f_mean_ready, 1)
                else:
                    pe.wait_ge(a_mean_ready, b)
                for j in range(GROUP):
                    last = nc.tensor.matmul(ps[:, 7, b * P:(b + 1) * P], ones, attn_sq[:, j, :], start=j == 0, stop=j == GROUP - 1)
                last.then_inc(attn_sq_summed, 1)

            pe.wait_ge(mix_tables_landed, 48)
            channel_stage(0)
            channel_stage(1)
            pe.wait_ge(position_landed, 32)
            position_stage(0)
            channel_stage(2)
            position_stage(1)
            channel_stage(3)
            position_stage(2)
            scores(0, 0)
            scores(0, 1)
            position_stage(3)
            pe.wait_ge(waves_read, 4)
            for s in range(len(STEPS)):
                b, g = STEPS[s]
                four = len(segments(b)) == 4
                turn_probs(s, 0)
                turn_probs(s, 1)
                if s + 1 < len(STEPS):
                    scores(s + 1, 0)
                weigh_values(s, 0)
                turn_probs(s, 2)
                if s + 1 < len(STEPS):
                    scores(s + 1, 1)
                weigh_values(s, 1)
                if four:
                    turn_probs(s, 3)
                weigh_values(s, 2)
                if four:
                    weigh_values(s, 3)
                if s == 0:
                    pe.wait_ge(fsq_added, 4)
                    nc.tensor.matmul(ps[:, 7, :], ones, rstd_f[:], start=True, stop=True).then_inc(fsq_summed, 1)
                if g == 0 and b > 0:
                    sum_attn_squares(b - 1)

            def out_part(d, part):
                slot = (U_OUT + d) % RING
                hi, lo = ((mix_f_hi, mix_f_lo), (mix_a_hi, mix_a_lo))[part]
                for k in range(4):
                    last = mm3([ps[:, 2 * (d % 2) + part, :]], w_hi[slot][:, 4 * part + k], w_lo[slot][:, 4 * part + k],
                               [hi[:, k, :]], [lo[:, k, :]], k == 0, k == 3)
                return last

            pe.wait_ge(exp_done, EXPS * 2 * len(STEPS))
            pe.wait_ge(mix_f_ready, 4)
            for d in range(2):
                pe.wait_ge(split_ready, U_OUT + d + 1)
                out_part(d, 0)
            sum_attn_squares(NB - 1)
            pe.wait_ge(mix_a_ready, NB)
            for d in range(KD):
                if d >= 2:
                    pe.wait_ge(split_ready, U_OUT + d + 1)
                    pe.wait_ge(parts_scaled, 2 * (d - 1))
                    out_part(d, 0)
                out_part(d, 1).then_inc(unit_used, 1)

            def second_norm_sum():
                pe.wait_ge(gained_ready, NB)
                sum_squares(2, 6, FFN[1].spans)

            turn_rows = ffn(FFN[1], 2, lambda k: None, second_norm_sum, lambda c: None)
            turn_rows(KD - 1)


SMALL = 2 + 1 + 3 * N_KV + 1
EXPS = 3

_INS = ["x", "meta_tokens", "ffn1_norm", "ffn1_w_gate", "ffn1_w_up", "ffn1_w_down", "mix_norm", "w_in", "q_norm", "k_norm",
        "sink", "attn_out_norm", "fourier_out_norm", "w_out", "ffn2_norm", "ffn2_w_gate", "ffn2_w_up", "ffn2_w_down", "final_norm"]


def kernel(**inputs):
    import concourse.bacc as _bacc
    from concourse.bass_utils import run_bass_kernel_spmd as _run

    nc = _bacc.Bacc("TRN2", target_bir_lowering=False, num_devices=1)
    arrays, tensors = {}, {}
    for name, a in [(n, inputs[n]) for n in _INS] + list(constant_tables().items()):
        a = np.ascontiguousarray(a)
        arrays[f"in_{name}_dram"] = a
        tensors[name] = nc.dram_tensor(f"in_{name}_dram", a.shape, mybir.dt.from_np(a.dtype), kind="ExternalInput").ap()
    out = nc.dram_tensor("out_0_dram", (1, SEQ, D_MODEL), F32, kind="ExternalOutput").ap()
    build(nc, tensors, out)
    r = _run(nc, [arrays], core_ids=[0])
    return r.results[0]["out_0_dram"]
```

```python
from contextlib import ExitStack

import numpy as np

import concourse.bass as bass
from concourse import mybir

F32 = mybir.dt.float32
F32R = mybir.dt.float32r
ALU = mybir.AluOpType
ACT = mybir.ActivationFunctionType
AX_X = mybir.AxisListType.X

P = 128
D_MODEL, SEQ, N_META = 1024, 512, 16
L = SEQ + N_META
HEAD_DIM, N_HEADS, N_KV = 64, 8, 2
GROUP = N_HEADS // N_KV
ATTN_W = N_HEADS * HEAD_DIM
KV_W = N_KV * HEAD_DIM
F_W = 512
F_DIM = 64
IN_W = ATTN_W + 2 * KV_W + F_W
WINDOW = 128
D_FF = 2816
EPS = 1e-6
MASKED = -float(2 ** 100)

KD = D_MODEL // P
KF = D_FF // P
NB = SEQ // P
HALF = L // 2
X_PARTS = 4
X_COLS = D_MODEL // X_PARTS
RING = 4
SLOT = 8
DOWN_UNITS = [(0, 6), (6, 6), (12, 5), (17, 5)]

SMALL = 2 + 1 + 3 * N_KV + 1
FILLS = 2
EXPS = 4
OUT_AHEAD = 3

U_FFN1_A = 0
U_FFN1_B = U_FFN1_A + 2 * KF
U_IN = U_FFN1_B + 4 * KD
U_OUT = U_IN + IN_W // P
U_FFN2_A = U_OUT + KD
U_FFN2_B = U_FFN2_A + 2 * KF

IN_ORDER = ["k", "v", "q0", "q1", "f0", "q2", "q3", "f1", "f2", "f3"]
V_AT = IN_ORDER.index("v")
NORMS = ["k"] + [f"q{j}" for j in range(GROUP)]
IN_BANKS = [4, 0, 2]

KEYS_W = N_META + SEQ + N_META
SCORE_W = [N_META + 2 * P, N_META + 3 * P, N_META + 3 * P, N_META + 2 * P]
SCORE_AT = [0, 0, N_META + P, N_META + 2 * P]
BIAS_AT = [sum(SCORE_W[:b]) for b in range(NB)]
BIAS_W = sum(SCORE_W)
MAX_W = max(SCORE_W)


def segments(b):
    real = [n for n in (b - 1, b, b + 1) if 0 <= n < NB]
    if b < 2:
        return [(0, N_META, 0)] + [(N_META + P * i, P, n + 1) for i, n in enumerate(real)]
    return [(P * i, P, n + 1) for i, n in enumerate(real)] + [(P * len(real), N_META, 0)]


STEPS = [(b, g) for b in range(NB) for g in range(N_KV)]
SEG_BASE = [sum(len(segments(b)) for b, _ in STEPS[:s]) for s in range(len(STEPS) + 1)]


def split_constant(a):
    a = np.asarray(a, np.float64).astype(np.float32)
    bits = a.view(np.uint32)
    hi = ((bits + np.uint32(0x7FF) + ((bits >> np.uint32(12)) & np.uint32(1))) & np.uint32(0xFFFFF000)).view(np.float32)
    return hi, a - hi


def constant_tables():
    ident = np.eye(P, dtype=np.float32)
    ones = np.ones((P, P), np.float32)
    pair = np.kron(np.eye(2), np.ones((HEAD_DIM, HEAD_DIM))).astype(np.float32)
    square = np.concatenate([ident, ones, pair], axis=1)

    c = np.arange(F_DIM)
    phase = 2 * np.pi * (np.outer(c, c) % F_DIM) / F_DIM
    channel = np.concatenate([np.kron(np.eye(2), np.cos(phase)), np.kron(np.eye(2), np.sin(phase))], axis=1)
    channel = np.stack(split_constant(channel / np.sqrt(F_DIM)))

    pos, t = np.arange(L), np.arange(1, HALF + 1)
    phase = 2 * np.pi * (np.outer(pos, t) % L) / L
    wave = np.stack([np.cos(phase), np.sin(phase)], axis=1) / np.sqrt(L)
    wave[:, 1, HALF - 1] = 0.0
    rows = np.zeros((1 + NB, P, 2, HALF))
    rows[0, :N_META] = wave[:N_META]
    rows[1:] = wave[N_META:].reshape(NB, P, 2, HALF)
    position = np.stack(split_constant(rows.transpose(1, 0, 2, 3).reshape(P, -1)))

    bias = np.full((P, BIAS_W), MASKED, np.float32)
    q = np.arange(P)
    for b in range(NB):
        for col, _, n in segments(b):
            at = BIAS_AT[b] + col
            if n == 0:
                dist = np.abs(N_META + b * P + q[:, None] - np.arange(N_META)[None])
                bias[:, at:at + N_META] = -np.minimum(dist, WINDOW)
            else:
                dist = np.abs(b * P + q[:, None] - ((n - 1) * P + q[None]))
                bias[:, at:at + P] = np.where(dist <= WINDOW, -dist, MASKED)
    return {"square": square, "channel": channel.astype(np.float32),
            "position": position.astype(np.float32), "bias": bias}


class NormSems:

    def __init__(self, sem, name):
        self.hi = sem(f"xg_hi_ready_{name}")
        self.ready = sem(f"xg_ready_{name}")
        self.sq = sem(f"squares_ready_{name}")
        self.sq_added = sem(f"squares_added_{name}")
        self.summed = sem(f"squares_summed_{name}")
        self.root = sem(f"root_ready_{name}")
        self.rstd = sem(f"rstd_ready_{name}")


class FfnSems:

    def __init__(self, sem, name):
        self.gate_scaled = sem(f"gate_scaled_{name}")
        self.silu_ready = sem(f"silu_ready_{name}")
        self.up_scaled = sem(f"up_scaled_{name}")
        self.act_ready = sem(f"act_ready_{name}")
        self.h_hi_ready = sem(f"h_hi_ready_{name}")
        self.h_ready = sem(f"h_ready_{name}")
        self.x_updated = sem(f"x_updated_{name}")
        self.turned = sem(f"turned_{name}")
        self.turned_read = sem(f"turned_read_{name}")


class Ffn:

    def __init__(self, n, first, spans, unit_a, unit_b, gate_bank, up_bank, down_bank, sems):
        self.n, self.first, self.spans, self.tokens = n, first, spans, sum(w for _, w in spans)
        self.unit_a, self.unit_b = unit_a, unit_b
        self.gate_bank, self.up_bank, self.down_bank = gate_bank, up_bank, down_bank
        self.s = sems


def build(nc, t, out):
    with ExitStack() as ctx:
        top = [((nc.sbuf_base + 31) // 32) * 32]

        def width(shape):
            n = 4
            for s in shape[1:]:
                n *= s
            return (n + 31) // 32 * 32

        def persist(name, shape, dt=F32):
            at = top[0]
            top[0] += width(shape)
            return nc.alloc_sbuf_tensor_at(name, shape, dt, offset=at)

        def region(start, items):
            got, at = {}, start
            for name, shape, dt in items:
                got[name] = nc.alloc_sbuf_tensor_at(name, shape, dt, offset=at)
                at += width(shape)
            return got, at

        xT = persist("xT", [P, KD, L])
        rstd = persist("rstd", [P, L])
        square = persist("square", [P, 3, P])
        gains = persist("gains", [P, 3, KD])
        out_gain = persist("out_gain", [P, 2, GROUP])
        qk_gain = persist("qk_gain", [P, 2])
        sinks = persist("sinks", [P, N_HEADS])
        neg_sinks = persist("neg_sinks", [P, N_HEADS])
        eps = persist("eps", [P, 1])
        table_load = persist("table_load", [P, 1])
        score_max = persist("score_max", [P, 2 * len(STEPS), 2])
        neg_max = persist("neg_max", [P, 2 * len(STEPS), 2])
        prob_sums = persist("prob_sums", [P, 2 * len(STEPS), 2])
        sink_exp = persist("sink_exp", [P, 2 * len(STEPS), 2])
        inv_den = persist("inv_den", [P, 2 * len(STEPS), 2])
        row_sums = persist("row_sums", [P, NB, KD])
        row_rstd = persist("row_rstd", [P, NB])
        token_rstd = persist("token_rstd", [P, NB + 1])
        scratch_a = [persist(f"scratch_a{p}", [P, L]) for p in range(2)]
        scratch_b = [persist(f"scratch_b{p}", [P, L]) for p in range(2)]
        raw = [persist(f"raw{s}", [P, SLOT, P]) for s in range(RING)]
        w_hi = [persist(f"w_hi{s}", [P, SLOT, P], F32R) for s in range(RING)]
        w_lo = [persist(f"w_lo{s}", [P, SLOT, P], F32R) for s in range(RING)]
        channel_hi = persist("channel_hi", [P, 2 * P], F32R)
        bias_tab = persist("bias_tab", [P, BIAS_W], F32R)

        x_region = top[0]
        xr, h_region = region(x_region, [("xg_hi", [P, KD, L], F32R), ("xg_lo", [P, KD, L], F32R)])
        xg_hi, xg_lo = xr["xg_hi"], xr["xg_lo"]
        hr, end = region(h_region, [("h_hi", [P, KF, L], F32R), ("h_lo", [P, KF, L], F32R)])
        h_hi, h_lo = hr["h_hi"], hr["h_lo"]
        assert end <= nc.sbuf_usable_end, (end, nc.sbuf_usable_end)

        st, _ = region(end - width([P, NB + 1, D_MODEL]), [("x_rows", [P, NB, D_MODEL], F32), ("meta_rows", [P, D_MODEL], F32)])
        x_rows, meta_rows = st["x_rows"], st["meta_rows"]
        sg, _ = region(h_region, [("squared_rows", [P, D_MODEL], F32), ("rstd_diag", [P, NB + 1, P], F32)])
        squared_rows, rstd_diag = sg["squared_rows"], sg["rstd_diag"]

        mx, mix_end = region(h_region, [
            ("f_hi", [P, 4, L], F32R), ("f_lo", [P, 4, L], F32R),
            ("q_stack", [P, N_HEADS, SEQ], F32R),
            ("k_hi", [P, N_KV, KEYS_W], F32R), ("k_lo", [P, N_KV, KEYS_W], F32R), ("k_norm_rows", [P, KEYS_W], F32),
            ("v_hi", [P, N_KV, 1 + NB, P], F32R), ("v_lo", [P, N_KV, 1 + NB, P], F32R),
            ("rstd_f", [P, SEQ], F32), ("rstd_a", [P, SEQ], F32), ("channel_lo", [P, 2 * P], F32R),
            ("mix_f_hi", [P, 4, SEQ], F32R), ("mix_f_lo", [P, 4, SEQ], F32R),
            ("mix_a_hi", [P, 4, SEQ], F32R), ("mix_a_lo", [P, 4, SEQ], F32R)])
        assert mix_end <= end
        f_hi, f_lo, q_stack, k_hi, k_lo, k_rows = (mx[n] for n in ("f_hi", "f_lo", "q_stack", "k_hi", "k_lo", "k_norm_rows"))
        v_hi, v_lo, rstd_f, rstd_a, channel_lo = (mx[n] for n in ("v_hi", "v_lo", "rstd_f", "rstd_a", "channel_lo"))
        mix_f_hi, mix_f_lo, mix_a_hi, mix_a_lo = (mx[n] for n in ("mix_f_hi", "mix_f_lo", "mix_a_hi", "mix_a_lo"))
        tb, tb_end = region(mix_end - 4 * width([P, 4, SEQ]), [("position_hi", [P, 1 + NB, 2, HALF], F32R),
                                                               ("position_lo", [P, 1 + NB, 2, HALF], F32R)])
        position_hi, position_lo = tb["position_hi"], tb["position_lo"]
        assert tb_end <= mix_end
        fr, fr_end = region(x_region, [("f_out", [P, 4, SEQ], F32), ("z_hi0", [P, 1 + NB, 2 * P], F32R), ("z_lo0", [P, 1 + NB, 2 * P], F32R),
                                       ("z_hi1", [P, 1 + NB, 2 * P], F32R), ("z_lo1", [P, 1 + NB, 2 * P], F32R)])
        assert fr_end <= h_region
        f_out, z_hi, z_lo = fr["f_out"], [fr["z_hi0"], fr["z_hi1"]], [fr["z_lo0"], fr["z_lo1"]]
        ar, ar_end = region(x_region + width([P, 4, SEQ]), [
            ("probs0", [P, GROUP, MAX_W], F32), ("probs1", [P, GROUP, MAX_W], F32),
            ("attn_sq", [P, GROUP, P], F32)])
        assert ar_end <= h_region
        probs, attn_sq = [ar["probs0"], ar["probs1"]], ar["attn_sq"]
        br, br_end = region(h_region, [
            ("slopes", [P, N_HEADS, P], F32R), ("pt_hi0", [P, GROUP, P], F32R), ("pt_lo0", [P, GROUP, P], F32R),
            ("pt_hi1", [P, GROUP, P], F32R), ("pt_lo1", [P, GROUP, P], F32R), ("attn_gained", [P, GROUP, P], F32)])
        assert br_end <= h_region + 2 * width([P, 4, L])
        slopes, attn_gained = br["slopes"], br["attn_gained"]
        pt_hi, pt_lo = [br["pt_hi0"], br["pt_hi1"]], [br["pt_lo0"], br["pt_lo1"]]
        fourier_part = region(h_region, [("fourier_part", [P, 2, SEQ], F32)])[0]["fourier_part"]
        er, er_end = region(x_region, [("y_rows", [P, NB, D_MODEL], F32), ("final_gain", [P, D_MODEL], F32)])
        assert er_end <= h_region
        y_rows, final_gain = er["y_rows"], er["final_gain"]

        ps = ctx.enter_context(nc.psum_tensor("ps", [P, 8, 512], F32))
        ident, ones, pair_ones = square[:, 0, :], square[:, 1, :], square[:, 2, :]

        def sem(name):
            return ctx.enter_context(nc.semaphore(name))

        x_landed = [sem(f"x_landed{i}") for i in range(X_PARTS)]
        meta_landed, first_gain_landed = sem("meta_landed"), sem("first_gain_landed")
        ident_landed, ones_landed, small_landed = sem("ident_landed"), sem("ones_landed"), sem("small_landed")
        first_landed = [sem(f"first_landed{u}") for u in range(2)]
        first_hi_ready, first_split_ready = sem("first_hi_ready"), sem("first_split_ready")
        mix_tables_landed, position_landed, gain_row_landed = sem("mix_tables_landed"), sem("position_landed"), sem("gain_row_landed")
        raw_landed = [sem(f"raw_landed{s}") for s in range(RING)]
        hi_ready, split_ready, unit_used = sem("hi_ready"), sem("split_ready"), sem("unit_used")
        constants_ready = sem("constants_ready")
        x_turned, x_copied = sem("x_turned"), sem("x_copied")
        rows_squared, token_root_ready, token_inv_ready = sem("rows_squared"), sem("token_root_ready"), sem("token_inv_ready")
        diag_ready, rstd_spread = sem("diag_ready"), sem("rstd_spread")
        norms = [NormSems(sem, n) for n in ("ffn1", "mix", "ffn2")]
        ffns = [FfnSems(sem, n) for n in ("ffn1", "ffn2")]
        in_read = sem("in_read")
        f_hi_ready, f_ready = sem("f_hi_ready"), sem("f_ready")
        fills_ready = sem("fills_ready")
        v_turned, v_hi_ready, v_ready = sem("v_turned"), sem("v_hi_ready"), sem("v_ready")
        qk_sq_ready, qk_summed, qk_root_ready = sem("qk_sq_ready"), sem("qk_summed"), sem("qk_root_ready")
        qk_inv_ready, qk_normed, qk_hi_ready, qk_ready = sem("qk_inv_ready"), sem("qk_normed"), sem("qk_hi_ready"), sem("qk_ready")
        z_done, z_hi_ready, z_ready = sem("z_done"), sem("z_hi_ready"), sem("z_ready")
        waves_done, sine_copied, waves_read = sem("waves_done"), sem("sine_copied"), sem("waves_read")
        fsq_ready, fsq_added, fsq_summed = sem("fsq_ready"), sem("fsq_added"), sem("fsq_summed")
        f_mean_ready, f_inv_ready, f_root_ready = sem("f_mean_ready"), sem("f_inv_ready"), sem("f_root_ready")
        f_gained = sem("f_gained")
        mix_f_hi_ready, mix_f_ready = sem("mix_f_hi_ready"), sem("mix_f_ready")
        slopes_ready, neg_sinks_ready = sem("slopes_ready"), sem("neg_sinks_ready")
        scores_done, max_ready, shift_ready, exp_done = sem("scores_done"), sem("max_ready"), sem("shift_ready"), sem("exp_done")
        pt_done, pt_hi_ready, pt_ready, pv_used = sem("pt_done"), sem("pt_hi_ready"), sem("pt_ready"), sem("pv_used")
        den_ready, den_inverted, heads_scaled = sem("den_ready"), sem("den_inverted"), sem("heads_scaled")
        last_head_scaled = sem("last_head_scaled")
        attn_sq_ready, attn_sq_summed, gained_ready = sem("attn_sq_ready"), sem("attn_sq_summed"), sem("gained_ready")
        mix_a_hi_ready, mix_a_ready = sem("mix_a_hi_ready"), sem("mix_a_ready")
        a_mean_ready, a_inv_ready, a_root_ready = sem("a_mean_ready"), sem("a_inv_ready"), sem("a_root_ready")
        parts_scaled, x_plus_f, x_mixed = sem("parts_scaled"), sem("x_plus_f"), sem("x_mixed")
        sums_ready, mean_ready, final_root, final_rstd = sem("sums_ready"), sem("mean_ready"), sem("final_root"), sem("final_rstd")
        half_done, half_updated, half_turned = sem("half_done"), sem("half_updated"), sem("half_turned")
        half_sums_ready = sem("half_sums_ready")
        rows_scaled, odd_rows_scaled, stored = sem("rows_scaled"), sem("odd_rows_scaled"), sem("stored")

        def norm_chunk(n):
            return IN_ORDER.index(NORMS[n])

        def count(i, k0, k1=0):
            return k0 if i is None else i * k1 + k0

        def need(eng, semaphore, value):
            if not isinstance(value, int) or value > 0:
                eng.wait_ge(semaphore, value)

        FFN = [Ffn(0, 0, [(0, HALF), (HALF, HALF)], U_FFN1_A, U_FFN1_B, [0, 4], [2, 6], [0, 2], ffns[0]),
               Ffn(1, N_META, [(0, SEQ)], U_FFN2_A, U_FFN2_B, [4, 2], [5, 3], [0, 1], ffns[1])]

        def banks(bank, spans):
            n = spans[0][1]
            return ps[:, bank, 0:n] if len(spans) == 1 else ps[:, bank:bank + 2, 0:n]

        def like(ap, spans):
            return ap if len(spans) == 1 else ap.rearrange("p (a n) -> p a n", a=2)

        HALVES = FFN[0].spans

        def pairs(eng, steps, body, peel=False):
            body(0, 0, 0, None)
            body(1, 1, 0, None)
            with eng.Fori(0, (steps - 4 if peel else steps - 2) // 2) as i:
                body(0, 2, 2, i)
                body(1, 3, 2, i)
            if peel:
                body(0, steps - 2, 0, None)

        LAST = KD - 1
        NORMED = LAST * P

        def half_cols(half):
            return slice(half * SEQ // 2, (half + 1) * SEQ // 2)

        def half_blocks(half):
            return range(half * NB // 2, (half + 1) * NB // 2)

        block = ctx.enter_context(nc.Block())

        @block.sync
        def _(sp):
            def raw_slot(n, i=None, per=0):
                need(sp, split_ready, count(i, n + 1 - RING, per))
                return raw[n % RING], raw_landed[n % RING]

            def load_columns(w, unit, column, i=None, per=0):
                slot, landed = raw_slot(unit, i, per)
                sp.dma_start(slot[:], w.rearrange("(k p) n -> p k n", p=P)[:, :, bass.ds(column, P)]).then_inc(landed, 16)

            def ffn(f, first, w_gate, w_up, w_down):
                def step_a(parity, k0, k1, i):
                    if k0 == 0 and f.n == 0:
                        first()
                        return
                    column = count(i, k0 * P, k1 * P)
                    load_columns(w_gate, f.unit_a + 2 * k0, column, i, 2 * k1)
                    load_columns(w_up, f.unit_a + 2 * k0 + 1, column, i, 2 * k1)

                def step_b(parity, k0, k1, i):
                    for j, (f0, n) in enumerate(DOWN_UNITS):
                        slot, landed = raw_slot(f.unit_b + 4 * k0 + j, i, 4 * k1)
                        src = w_down.rearrange("(k p) n -> p k n", p=P)[:, f0:f0 + n, bass.ds(count(i, k0 * P, k1 * P), P)]
                        sp.dma_start(slot[:, 0:n, :], src).then_inc(landed, 16)

                pairs(sp, KF, step_a)
                pairs(sp, KD, step_b)

            squares = t["square"].rearrange("p (a n) -> p a n", a=3)
            sp.dma_start(square[:, 0, :], squares[:, 0, :]).then_inc(ident_landed, 16)
            x_by_block = t["x"][0].rearrange("(b p) n -> p b n", p=P)

            def load_x(part):
                cols = slice(part * X_COLS, (part + 1) * X_COLS)
                sp.dma_start(x_rows[:, :, cols], x_by_block[:, :, cols]).then_inc(x_landed[part], 16)

            def first_weights(half):
                tiles = slice(half * SLOT // 2, (half + 1) * SLOT // 2)
                for u, name in enumerate(("ffn1_w_gate", "ffn1_w_up")):
                    sp.dma_start(raw[u][:, tiles, :], t[name].rearrange("(k p) n -> p k n", p=P)[:, tiles, 0:P]).then_inc(
                        (first_landed, raw_landed)[half][u], 16)

            def first_loads():
                load_x(0)
                first_weights(0)
                load_x(1)
                first_weights(1)
                for part in range(2, X_PARTS):
                    load_x(part)
                sp.dma_start(square[:, 1:, :], squares[:, 1:, :]).then_inc(ones_landed, 16)

            ffn(FFN[0], first_loads, t["ffn1_w_gate"], t["ffn1_w_up"], t["ffn1_w_down"])
            w_in = t["w_in"].rearrange("(k p) n -> p k n", p=P)
            for j, name in enumerate(IN_ORDER):
                slot, landed = raw_slot(U_IN + j)
                if name[0] == "q":
                    for g in range(N_KV):
                        c = (g * GROUP + int(name[1])) * HEAD_DIM
                        sp.dma_start(slot[:, :, g * HEAD_DIM:(g + 1) * HEAD_DIM], w_in[:, :, c:c + HEAD_DIM]).then_inc(landed, 16)
                else:
                    c = ATTN_W + 2 * KV_W + P * int(name[1]) if name[0] == "f" else {"k": ATTN_W, "v": ATTN_W + KV_W}[name]
                    sp.dma_start(slot[:], w_in[:, :, c:c + P]).then_inc(landed, 16)
            for d in range(KD):
                slot, landed = raw_slot(U_OUT + d)
                cols = slice(d * P, (d + 1) * P)
                sp.dma_start(slot[:, 0:4, :], t["w_out"][ATTN_W:, cols].rearrange("(k p) n -> p k n", p=P)).then_inc(landed, 16)
                for g in range(N_KV):
                    rows = slice(g * GROUP * HEAD_DIM, (g + 1) * GROUP * HEAD_DIM)
                    sp.dma_start(slot[g * HEAD_DIM:(g + 1) * HEAD_DIM, 4:8, :],
                                 t["w_out"][rows, cols].rearrange("(j p) n -> p j n", p=HEAD_DIM)).then_inc(landed, 16)
            ffn(FFN[1], None, t["ffn2_w_gate"], t["ffn2_w_up"], t["ffn2_w_down"])
            for b in range(NB):
                sp.wait_ge(rows_scaled, 3 * (b // 2) + 2 + b % 2)
                if b % 2:
                    sp.wait_ge(odd_rows_scaled, b // 2 + 1)
                sp.dma_start(out[0, b * P:(b + 1) * P, :], y_rows[:, b, :]).then_inc(stored, 16)
            sp.wait_ge(stored, 16 * NB)

        def transfers(n):
            if U_IN <= n < U_OUT:
                return 2 if IN_ORDER[n - U_IN][0] == "q" else 1
            return 3 if U_OUT <= n < U_FFN2_A else 1

        def landed_count(n):
            return 16 * sum(transfers(m) for m in range(n % RING, n + 1, RING))

        @block.gpsimd
        def _(pool):
            pool.wait_ge(unit_used, 1)
            with nc.allow_non_contiguous_dma(reason="gains by feature: a few KB"):
                for n, name in enumerate(("mix_norm", "ffn2_norm")):
                    pool.dma_start(gains[:, n + 1, :], t[name].rearrange("(k p) -> p k", p=P)).then_inc(small_landed, 16)
                pool.dma_start(out_gain[:, 1, :], t["fourier_out_norm"].rearrange("(k p) -> p k", p=P)).then_inc(small_landed, 16)
                for g in range(N_KV):
                    rows = slice(g * HEAD_DIM, (g + 1) * HEAD_DIM)
                    width_g = GROUP * HEAD_DIM
                    pool.dma_start(out_gain[rows, 0, :], t["attn_out_norm"][g * width_g:(g + 1) * width_g].rearrange(
                        "(j p) -> p j", p=HEAD_DIM)).then_inc(small_landed, 16)
                    pool.dma_start(qk_gain[rows, 0:1], t["q_norm"].rearrange("(p a) -> p a", a=1)).then_inc(small_landed, 16)
                    pool.dma_start(qk_gain[rows, 1:2], t["k_norm"].rearrange("(p a) -> p a", a=1)).then_inc(small_landed, 16)
                pool.dma_start(sinks[:], t["sink"].rearrange("(a h) -> a h", a=1).to_broadcast([P, N_HEADS])).then_inc(small_landed, 16)
            pool.dma_start(channel_hi[:], t["channel"][0]).then_inc(mix_tables_landed, 16)
            pool.dma_start(bias_tab[:], t["bias"]).then_inc(mix_tables_landed, 16)
            pool.wait_ge(unit_used, U_IN)
            pool.dma_start(channel_lo[:], t["channel"][1]).then_inc(mix_tables_landed, 16)
            pool.dma_start(position_hi[:], t["position"][0].rearrange("p (a b n) -> p a b n", a=1 + NB, b=2)).then_inc(position_landed, 16)
            pool.dma_start(position_lo[:], t["position"][1].rearrange("p (a b n) -> p a b n", a=1 + NB, b=2)).then_inc(position_landed, 16)
            nc.gpsimd.memset(v_hi[:].bitcast(F32), 0.0).then_inc(fills_ready, 1)
            nc.gpsimd.memset(v_lo[:].bitcast(F32), 0.0).then_inc(fills_ready, 1)
            def fourier_lo(c):
                pool.wait_ge(mix_f_hi_ready, c + 1)
                nc.gpsimd.tensor_tensor(mix_f_lo[:, c, :], f_out[:, c, :], mix_f_hi[:, c, :].bitcast(F32),
                                        ALU.subtract).then_inc(mix_f_ready, 1)

            def mix_low(b):
                pool.wait_ge(mix_a_hi_ready, b + 1)
                cols = slice(b * P, (b + 1) * P)
                nc.gpsimd.tensor_tensor(mix_a_lo[:, :, cols], attn_gained[:], mix_a_hi[:, :, cols].bitcast(F32),
                                        ALU.subtract).then_inc(mix_a_ready, 1)

            def split_lo(n):
                pool.wait_ge(hi_ready, n + 1)
                slot = n % RING
                nc.gpsimd.tensor_tensor(w_lo[slot][:], raw[slot][:], w_hi[slot][:].bitcast(F32), ALU.subtract).then_inc(split_ready, 1)

            pool.wait_ge(fsq_ready, 4)
            for c in range(4):
                nc.gpsimd.tensor_scalar(f_out[:, c, :], f_out[:, c, :], out_gain[:, 1, c:c + 1], None, ALU.mult).then_inc(f_gained, 1)
            pool.wait_ge(f_gained, 4)
            fourier_lo(0)
            mix_low(0)
            fourier_lo(1)
            fourier_lo(2)
            mix_low(1)
            fourier_lo(3)
            split_lo(U_OUT)
            mix_low(2)
            split_lo(U_OUT + 1)
            split_lo(U_OUT + 2)

            for k in range(KD):
                s = norms[2]
                pool.wait_ge(s.sq, k + 1)
                total, squares = rstd[:, 0:SEQ], scratch_a[k % 2][:, 0:SEQ]
                if k == 0:
                    nc.gpsimd.tensor_copy(total, squares).then_inc(s.sq_added, 1)
                else:
                    pool.wait_ge(s.sq_added, k)
                    nc.gpsimd.tensor_tensor(total, total, squares, ALU.add).then_inc(s.sq_added, 1)
            pool.wait_ge(unit_used, U_FFN2_B)
            pool.dma_start(final_gain[:], t["final_norm"].rearrange("(a n) -> a n", a=1).to_broadcast([P, D_MODEL])).then_inc(gain_row_landed, 16)


        @block.scalar
        def _(act):
            def split_hi(n, tiles, i=None, per=0):
                act.wait_ge(raw_landed[n % RING], count(i, landed_count(n), 16 * per // RING))
                need(act, unit_used, count(i, n + 1 - RING, per))
                nc.scalar.activation(w_hi[n % RING][:, 0:tiles, :], raw[n % RING][:, 0:tiles, :], ACT.Copy).then_inc(hi_ready, 1)

            def gained_hi(norm, ready, k, k1, i, first, spans):
                s = norms[norm]
                chunk = count(i, k, k1)
                n = sum(w for _, w in spans)
                if norm and k:
                    act.wait_ge(s.sq_added, count(i, k, k1))
                act.wait_ge(ready, count(i, k + 1, k1))
                nc.scalar.activation(xg_hi[:, chunk, 0:n], xT[:, chunk, first:first + n], ACT.Copy,
                                     scale=gains[:, norm, bass.ds(chunk, 1)]).then_inc(s.hi, 1)
                if norm == 0:
                    return
                nc.scalar.activation(scratch_a[k % 2][:, 0:n], xT[:, chunk, first:first + n], ACT.Square).then_inc(s.sq, 1)

            def norm_root(norm, bank, spans):
                n = sum(w for _, w in spans)
                act.wait_ge(norms[norm].summed, 1)
                nc.scalar.activation(like(rstd[:, 0:n], spans), banks(bank, spans), ACT.Sqrt, bias=eps[:, 0:1],
                                     scale=1.0 / D_MODEL).then_inc(norms[norm].root, 1)

            def ffn(f, at_first, at_second):
                s = f.s

                def finish_a(parity, k0, k1, i):
                    act.wait_ge(s.gate_scaled, count(i, k0 + 1, k1))
                    a = scratch_a[parity][:, 0:f.tokens]
                    nc.scalar.activation(a, a, ACT.Silu).then_inc(s.silu_ready, 1)
                    act.wait_ge(s.act_ready, count(i, k0 + 1, k1))
                    nc.scalar.activation(h_hi[:, count(i, k0, k1), 0:f.tokens], scratch_b[parity][:, 0:f.tokens],
                                         ACT.Copy).then_inc(s.h_hi_ready, 1)

                def step_a(parity, k0, k1, i):
                    if k0 == 0:
                        at_first()
                        return
                    if k0 >= 2 or k0 == 1 and f.n == 1:
                        split_hi(f.unit_a + 2 * k0, KD, i, 2 * k1)
                        split_hi(f.unit_a + 2 * k0 + 1, KD, i, 2 * k1)
                    if k0 == 1:
                        at_second()
                    finish_a(1 - parity, k0 - 1, k1, i)

                def finish_b(k0, k1, i):
                    if f.n == 0:
                        gained_hi(1, s.x_updated, k0, k1, i, 0, HALVES)
                    else:
                        act.wait_ge(s.turned, count(i, k0 + 1, k1))
                        for b in range(NB):
                            last = nc.scalar.activation(scratch_a[k0 % 2][:, b * P:(b + 1) * P], ps[:, 6 + k0 % 2, b * P:(b + 1) * P],
                                                        ACT.Square, accum_out=row_sums[:, b, bass.ds(count(i, k0, k1), 1)])
                        last.then_inc(sums_ready, 1)

                def step_b(parity, k0, k1, i):
                    for j, (_, n) in enumerate(DOWN_UNITS):
                        if j == 3:
                            if k0 == 0:
                                finish_a(1, KF - 1, 0, None)
                                nc.scalar.activation(table_load[:], eps[:], ACT.Sqrt)
                            elif f.n == 0 or k0 < LAST:
                                finish_b(k0 - 1, k1, i)
                        split_hi(f.unit_b + 4 * k0 + j, n, i, 4 * k1)
                    if f.n == 1 and k0 == LAST:
                        finish_b(k0 - 1, k1, i)

                pairs(act, KF, step_a)
                if f.n == 0:
                    act.wait_ge(small_landed, 16 * SMALL)
                if f.n == 0:
                    pairs(act, KD, step_b)
                else:
                    pairs(act, KD, step_b, peel=True)
                    step_b(1, LAST, 0, None)

            with nc.allow_non_contiguous_dma(reason="gains by feature: a few KB"):
                act.dma_start(meta_rows[0:N_META, :], t["meta_tokens"]).then_inc(meta_landed, 16)
                act.dma_start(gains[:, 0, :], t["ffn1_norm"].rearrange("(k p) -> p k", p=P)).then_inc(first_gain_landed, 16)

            act.wait_ge(constants_ready, 1)
            nc.scalar.activation(table_load[:], eps[:], ACT.Silu)

            def start():
                act.wait_ge(first_gain_landed, 16)
                gained_hi(0, x_copied, 0, 0, None, 0, HALVES)
                gained_hi(0, x_copied, 1, 0, None, 0, HALVES)
                for half in range(2):
                    tiles = slice(half * SLOT // 2, (half + 1) * SLOT // 2)
                    for u in range(2):
                        act.wait_ge((first_landed, raw_landed)[half][u], 16)
                        nc.scalar.activation(w_hi[u][:, tiles, :], raw[u][:, tiles, :], ACT.Copy).then_inc((first_hi_ready, hi_ready)[half], 1)
                act.wait_ge(meta_landed, 16)
                act.wait_ge(constants_ready, 2)
                nc.scalar.activation(squared_rows[0:N_META, :], meta_rows[0:N_META, :], ACT.Square,
                                     accum_out=token_rstd[0:N_META, NB:NB + 1]).then_inc(rows_squared, 1)
                for k in range(2, KD):
                    gained_hi(0, x_copied, k, 0, None, 0, HALVES)
                    b = k - 3
                    if b == 0:
                        for part in range(X_PARTS):
                            act.wait_ge(x_landed[part], 16)
                    if 0 <= b < NB:
                        act.wait_ge(rows_squared, b + 1)
                        nc.scalar.activation(squared_rows[:], x_rows[:, b, :], ACT.Square,
                                             accum_out=token_rstd[:, b:b + 1]).then_inc(rows_squared, 1)
                    elif b == NB:
                        act.wait_ge(rows_squared, NB + 1)
                        nc.scalar.activation(token_rstd[:], token_rstd[:], ACT.Sqrt, bias=eps[:, 0:1],
                                             scale=1.0 / D_MODEL).then_inc(token_root_ready, 1)
                split_hi(FFN[0].unit_a + 2, KD)
                split_hi(FFN[0].unit_a + 3, KD)

            def copy_first_rstd():
                act.wait_ge(rstd_spread, 1)
                nc.scalar.activation(rstd[:, N_META:L], ps[:, 7, :], ACT.Copy)
                nc.scalar.activation(rstd[:, 0:N_META], ps[:, 6, 0:N_META], ACT.Copy).then_inc(norms[0].rstd, 1)

            ffn(FFN[0], start, copy_first_rstd)

            def in_finish(e):
                name = IN_ORDER[e]
                a, b = scratch_a[e % 2], scratch_b[e % 2]
                if name[0] == "f":
                    act.wait_ge(in_read, e + 1)
                    nc.scalar.activation(f_hi[:, int(name[1]), :], b[:], ACT.Copy).then_inc(f_hi_ready, 1)
                elif name != "v":
                    act.wait_ge(in_read, e + 1)
                    nc.scalar.activation(a[:], b[:], ACT.Square).then_inc(qk_sq_ready, 1)

            def v_high():
                act.wait_ge(v_turned, 1)
                act.wait_ge(fills_ready, FILLS)
                for g in range(N_KV):
                    dims = slice(g * HEAD_DIM, (g + 1) * HEAD_DIM)
                    nc.scalar.activation(v_hi[:, g, 1:, dims], ps[:, 6, :].rearrange("p (a n) -> p a n", a=NB)[:, :, dims],
                                         ACT.Copy).then_inc(v_hi_ready, 1)
                    nc.scalar.activation(v_hi[0:N_META, g, 0, dims], ps[0:N_META, 7, dims], ACT.Copy).then_inc(v_hi_ready, 1)

            def qk_root(n):
                act.wait_ge(qk_summed, n + 1)
                a = scratch_a[norm_chunk(n) % 2]
                nc.scalar.activation(like(a[:], HALVES), banks(6, HALVES), ACT.Sqrt, bias=eps[:, 0:1],
                                     scale=1.0 / HEAD_DIM).then_inc(qk_root_ready, 1)

            def qk_hi(n):
                act.wait_ge(qk_normed, n + 1)
                if n == 0:
                    for g in range(N_KV):
                        for at in range(2):
                            nc.scalar.activation(k_hi[at * HEAD_DIM:(at + 1) * HEAD_DIM, g, :],
                                                 k_rows[g * HEAD_DIM:(g + 1) * HEAD_DIM, :], ACT.Copy).then_inc(qk_hi_ready, 1)
                else:
                    b = scratch_b[norm_chunk(n) % 2]
                    for g in range(N_KV):
                        rows = slice(g * HEAD_DIM, (g + 1) * HEAD_DIM)
                        nc.scalar.activation(q_stack[rows, g * GROUP + n - 1, :], b[rows, N_META:L], ACT.Copy).then_inc(qk_hi_ready, 1)

            split_hi(U_IN, KD)
            for j in range(len(IN_ORDER)):
                if j + 1 < len(IN_ORDER) and j:
                    split_hi(U_IN + j + 1, KD)
                if j == 0:
                    gained_hi(1, ffns[0].x_updated, KD - 1, 0, None, 0, HALVES)
                    split_hi(U_IN + 1, KD)
                    norm_root(1, 6, HALVES)
                else:
                    if j - 2 == V_AT:
                        v_high()
                    in_finish(j - 1)
                if j >= 2 and IN_ORDER[j - 2] in NORMS:
                    n = NORMS.index(IN_ORDER[j - 2])
                    qk_root(n)
                    qk_hi(n)
            def z_split(c):
                act.wait_ge(z_done, c + 1)
                if c >= 2:
                    act.wait_ge(waves_done, c - 1)
                bank = 3 * (c % 2)
                nc.scalar.activation(z_hi[c % 2][:, 1:, :].rearrange("p a n -> p (a n)"), ps[:, bank:bank + 2, :].rearrange("p a n -> p (a n)"),
                                     ACT.Copy).then_inc(z_hi_ready, 1)
                nc.scalar.activation(z_hi[c % 2][0:N_META, 0, :], ps[0:N_META, bank + 2, 0:2 * P], ACT.Copy).then_inc(z_hi_ready, 1)

            def copy_sine(c):
                act.wait_ge(waves_done, c + 1)
                if c >= 2:
                    act.wait_ge(waves_read, c - 1)
                nc.scalar.activation(scratch_b[c % 2][:, 0:HALF], ps[:, 7, 0:HALF], ACT.Copy).then_inc(sine_copied, 1)

            def square_f(c):
                act.wait_ge(waves_read, c + 1)
                need(act, fsq_added, c - 1)
                nc.scalar.activation(scratch_a[c % 2][:, 0:SEQ], f_out[:, c, :], ACT.Square).then_inc(fsq_ready, 1)

            z_split(0)
            in_finish(len(IN_ORDER) - 1)
            z_split(1)
            copy_sine(0)
            z_split(2)
            copy_sine(1)
            square_f(0)
            z_split(3)
            copy_sine(2)
            square_f(1)

            def exps(s, half):
                b, g = STEPS[s]
                n = 2 * s + half
                act.wait_ge(shift_ready, n + 1)
                for h in range(2):
                    head = g * GROUP + 2 * half + h
                    nc.scalar.activation(sink_exp[:, n, h:h + 1], neg_max[:, n, h:h + 1], ACT.Exp, bias=sinks[:, head:head + 1]).then_inc(exp_done, 1)
                need(act, pt_done, SEG_BASE[s - 1] if s >= 2 else 0)
                for h in range(2):
                    nc.scalar.activation(probs[s % 2][:, 2 * half + h, 0:SCORE_W[b]], ps[:, 2 * half + h, 0:SCORE_W[b]], ACT.Exp,
                                         bias=neg_max[:, n, h:h + 1], scale=HEAD_DIM ** -0.5,
                                         accum_out=prob_sums[:, n, h:h + 1]).then_inc(exp_done, 1)

            def scale_last(s):
                n = 2 * s + 1
                act.wait_ge(den_inverted, n + 1)
                p = probs[s % 2][:, GROUP - 1, 0:SCORE_W[STEPS[s][0]]]
                nc.scalar.activation(p, p, ACT.Copy, scale=inv_den[:, n, 1:2]).then_inc(last_head_scaled, 1)

            def probs_hi(s, j):
                m = SEG_BASE[s] + j
                _, keys, _ = segments(STEPS[s][0])[j]
                act.wait_ge(pt_done, m + 1)
                need(act, pv_used, m - 1)
                nc.scalar.activation(pt_hi[m % 2][0:keys].rearrange("p a n -> p (a n)"), ps[0:keys, 4 + m % 2, :], ACT.Copy).then_inc(pt_hi_ready, 1)

            def square_attn(b):
                act.wait_ge(pv_used, SEG_BASE[2 * b + 2])
                need(act, attn_sq_summed, b)
                nc.scalar.activation(attn_sq[:].rearrange("p a n -> p (a n)"), ps[:, 6, :], ACT.Square).then_inc(attn_sq_ready, 1)

            def mix_hi(b):
                act.wait_ge(gained_ready, b + 1)
                nc.scalar.activation(mix_a_hi[:, :, b * P:(b + 1) * P], attn_gained[:], ACT.Copy).then_inc(mix_a_hi_ready, 1)

            def fourier_hi(c):
                act.wait_ge(f_gained, c + 1)
                nc.scalar.activation(mix_f_hi[:, c, :], f_out[:, c, :], ACT.Copy).then_inc(mix_f_hi_ready, 1)

            exps(0, 0)
            exps(0, 1)
            scale_last(0)
            copy_sine(3)
            for s in range(len(STEPS)):
                b, g = STEPS[s]
                n_seg = len(segments(b))
                if g == 0 and b > 0:
                    square_attn(b - 1)
                probs_hi(s, 0)
                probs_hi(s, 1)
                if s + 1 < len(STEPS):
                    exps(s + 1, 0)
                probs_hi(s, 2)
                if g == 0 and b > 0:
                    mix_hi(b - 1)
                if s == 0:
                    square_f(2)
                    square_f(3)
                elif s <= 4:
                    fourier_hi(s - 1)
                else:
                    split_hi(U_OUT + s - 5, KD)
                if n_seg == 4:
                    probs_hi(s, 3)
                if s + 1 < len(STEPS):
                    exps(s + 1, 1)
                    scale_last(s + 1)
            square_attn(NB - 1)
            mix_hi(NB - 1)

            for d in range(KD):
                if d:
                    split_hi(U_OUT + OUT_AHEAD + d - 1, KD)
                if d == 0:
                    act.wait_ge(f_inv_ready, 1)
                    nc.scalar.activation(rstd_f[:], rstd_f[:], ACT.Sqrt).then_inc(f_root_ready, 1)
                    act.wait_ge(a_inv_ready, NB)
                    nc.scalar.activation(rstd_a[:], rstd_a[:], ACT.Sqrt).then_inc(a_root_ready, 1)
                else:
                    gained_hi(2, x_mixed, d - 1, 0, None, N_META, FFN[1].spans)

            def second_norm():
                gained_hi(2, x_mixed, KD - 1, 0, None, N_META, FFN[1].spans)

            ffn(FFN[1], second_norm, lambda: norm_root(2, 6, FFN[1].spans))
            for half in range(2):
                act.wait_ge(half_turned, half + 1)
                for b in half_blocks(half):
                    last = nc.scalar.activation(scratch_a[1][:, b * P:(b + 1) * P], ps[:, 7 - half, b * P:(b + 1) * P], ACT.Square,
                                                accum_out=row_sums[:, b, LAST:KD])
                last.then_inc(half_sums_ready, 1)
                act.wait_ge(mean_ready, half + 1)
                r = row_rstd[:, 2 * half:2 * half + 2]
                nc.scalar.activation(r, r, ACT.Sqrt, bias=eps[:, 0:1], scale=1.0 / D_MODEL).then_inc(final_root, 1)
                act.wait_ge(final_rstd, half + 1)
                act.wait_ge(ffns[1].turned_read, LAST)
                b = 2 * half + 1
                nc.scalar.activation(y_rows[:, b, 0:NORMED], y_rows[:, b, 0:NORMED], ACT.Copy,
                                     scale=row_rstd[:, b:b + 1]).then_inc(odd_rows_scaled, 1)

        @block.vector
        def _(dve):
            def split_lo(n, tiles, i=None, per=0):
                dve.wait_ge(hi_ready, count(i, n + 1, per))
                s = n % RING
                nc.vector.tensor_tensor(w_lo[s][:, 0:tiles, :], raw[s][:, 0:tiles, :], w_hi[s][:, 0:tiles, :].bitcast(F32),
                                        ALU.subtract).then_inc(split_ready, 1)

            def gained_lo(norm, k, k1, i, first, n):
                chunk = count(i, k, k1)
                dve.wait_ge(norms[norm].hi, count(i, k + 1, k1))
                nc.vector.scalar_tensor_tensor(xg_lo[:, chunk, 0:n], xT[:, chunk, first:first + n], gains[:, norm, bass.ds(chunk, 1)],
                                               xg_hi[:, chunk, 0:n].bitcast(F32), ALU.mult, ALU.subtract).then_inc(norms[norm].ready, 1)

            def add_squares(norm, k, k1, i, n):
                s = norms[norm]
                dve.wait_ge(s.sq, count(i, k + 1, k1))
                if k == 0:
                    nc.vector.tensor_copy(rstd[:, 0:n], scratch_a[0][:, 0:n]).then_inc(s.sq_added, 1)
                    return
                dve.wait_ge(s.sq_added, count(i, k, k1))
                nc.vector.tensor_tensor(rstd[:, 0:n], rstd[:, 0:n], scratch_a[k % 2][:, 0:n], ALU.add).then_inc(s.sq_added, 1)

            def norm_inverse(norm, n):
                dve.wait_ge(norms[norm].root, 1)
                nc.vector.reciprocal(rstd[:, 0:n], rstd[:, 0:n]).then_inc(norms[norm].rstd, 1)
                dve.wait_ge(norms[norm].rstd, 1)

            def first_diag():
                dve.wait_ge(token_root_ready, 1)
                nc.vector.reciprocal(token_rstd[:], token_rstd[:]).then_inc(token_inv_ready, 1)
                dve.wait_ge(token_inv_ready, 1)
                for b in range(NB + 1):
                    last = nc.vector.tensor_scalar(rstd_diag[:, b, :], ident, token_rstd[:, b:b + 1], None, ALU.mult)
                last.then_inc(diag_ready, 1)

            def start():
                dve.wait_ge(first_gain_landed, 16)
                dve.wait_ge(x_turned, 1)
                nc.vector.tensor_copy(xT[:, :, 0:N_META], ps[:, 3, 0:KD * N_META].rearrange("p (k n) -> p k n", k=KD))

                def copy(k):
                    dve.wait_ge(x_turned, k + 2)
                    nc.vector.tensor_copy(xT[:, k, N_META:L], ps[:, 4 + k % 4, :]).then_inc(x_copied, 1)

                copy(0)
                copy(1)
                gained_lo(0, 0, 0, None, 0, L)
                gained_lo(0, 1, 0, None, 0, L)
                for half in range(2):
                    tiles = slice(half * SLOT // 2, (half + 1) * SLOT // 2)
                    for u in range(2):
                        dve.wait_ge((first_hi_ready, hi_ready)[half], u + 1)
                        nc.vector.tensor_tensor(w_lo[u][:, tiles, :], raw[u][:, tiles, :], w_hi[u][:, tiles, :].bitcast(F32),
                                                ALU.subtract).then_inc((first_split_ready, split_ready)[half], 1)
                    if half == 0:
                        copy(2)
                        copy(3)
                for k in range(2, KD):
                    gained_lo(0, k, 0, None, 0, L)
                    if k + 2 < KD:
                        copy(k + 2)
                first_diag()

            def ffn(f, at_first, at_second):
                s = f.s
                r = like(rstd[:, 0:f.tokens], f.spans)

                def scale_gate(parity, k0, k1, i):
                    dve.wait_ge(unit_used, count(i, f.unit_a + 2 * k0 + 1, 2 * k1))
                    nc.vector.tensor_tensor(like(scratch_a[parity][:, 0:f.tokens], f.spans), banks(f.gate_bank[parity], f.spans), r,
                                            ALU.mult).then_inc(s.gate_scaled, 1)

                def finish_a(parity, k0, k1, i):
                    a, b = scratch_a[parity][:, 0:f.tokens], scratch_b[parity][:, 0:f.tokens]
                    dve.wait_ge(unit_used, count(i, f.unit_a + 2 * k0 + 2, 2 * k1))
                    nc.vector.tensor_tensor(like(b, f.spans), banks(f.up_bank[parity], f.spans), r, ALU.mult).then_inc(s.up_scaled, 1)
                    dve.wait_ge(s.up_scaled, count(i, k0 + 1, k1))
                    dve.wait_ge(s.silu_ready, count(i, k0 + 1, k1))
                    nc.vector.tensor_tensor(b, b, a, ALU.mult).then_inc(s.act_ready, 1)
                    dve.wait_ge(s.h_hi_ready, count(i, k0 + 1, k1))
                    chunk = count(i, k0, k1)
                    nc.vector.tensor_tensor(h_lo[:, chunk, 0:f.tokens], b, h_hi[:, chunk, 0:f.tokens].bitcast(F32),
                                            ALU.subtract).then_inc(s.h_ready, 1)

                def step_a(parity, k0, k1, i):
                    if k0 == 0:
                        at_first()
                        return
                    split_lo(f.unit_a + 2 * k0, KD, i, 2 * k1)
                    if k0 > 1:
                        scale_gate(1 - parity, k0 - 1, k1, i)
                    split_lo(f.unit_a + 2 * k0 + 1, KD, i, 2 * k1)
                    if k0 == 1:
                        at_second()
                        scale_gate(0, 0, 0, None)
                    finish_a(1 - parity, k0 - 1, k1, i)

                def finish_b(parity, k0, k1, i):
                    chunk = count(i, k0, k1)
                    x = xT[:, chunk, f.first:L]
                    dve.wait_ge(unit_used, count(i, f.unit_b + 4 * k0 + 4, 4 * k1))
                    total = x if f.n == 0 else scratch_b[parity][:, 0:SEQ]
                    nc.vector.scalar_tensor_tensor(like(total, f.spans), banks(f.down_bank[parity], f.spans), 0.5, like(x, f.spans),
                                                   ALU.mult, ALU.add).then_inc(s.x_updated, 1)
                    if f.n == 0:
                        gained_lo(1, k0, k1, i, 0, L)
                        add_squares(1, k0, k1, i, L)

                def gain_rows(k0, k1, i):
                    dve.wait_ge(sums_ready, count(i, k0 + 1, k1))
                    cols = bass.ds(count(i, k0 * P, k1 * P), P)
                    for b in range(NB):
                        last = nc.vector.tensor_tensor(y_rows[:, b, cols], ps[:, 6 + k0 % 2, b * P:(b + 1) * P], final_gain[:, cols], ALU.mult)
                    last.then_inc(s.turned_read, 1)

                def step_b(parity, k0, k1, i):
                    for j, (_, n) in enumerate(DOWN_UNITS):
                        if j == 3:
                            if k0 == 0:
                                scale_gate(1, KF - 1, 0, None)
                                finish_a(1, KF - 1, 0, None)
                            else:
                                finish_b(1 - parity, k0 - 1, k1, i)
                        split_lo(f.unit_b + 4 * k0 + j, n, i, 4 * k1)
                    if f.n == 1 and k0 >= 1:
                        if k0 == 1:
                            dve.wait_ge(gain_row_landed, 16)
                        gain_rows(k0 - 1, k1, i)

                pairs(dve, KF, step_a)
                if f.n == 0:
                    dve.wait_ge(small_landed, 16 * SMALL)
                if f.n == 0:
                    pairs(dve, KD, step_b)
                else:
                    pairs(dve, KD, step_b, peel=True)
                    step_b(1, LAST, 0, None)
                return finish_b

            nc.vector.memset(eps[:], EPS).then_inc(constants_ready, 1)
            nc.vector.memset(token_rstd[:], 0.0).then_inc(constants_ready, 1)

            def first_rstd():
                dve.wait_ge(norms[0].rstd, 1)

            finish_b = ffn(FFN[0], start, first_rstd)

            def in_finish(e):
                b = scratch_b[e % 2]
                dve.wait_ge(unit_used, U_IN + e + 1)
                if e >= 2:
                    name = IN_ORDER[e - 2]
                    if name[0] == "q":
                        done, value = qk_ready, 4 + 2 * NORMS.index(name)
                    else:
                        done, value = {"k": (qk_normed, 1), "v": (v_turned, 1), "f": (f_ready, int(name[-1]) + 1 if name[0] == "f" else 0)}[name[0]]
                    dve.wait_ge(done, value)
                nc.vector.tensor_tensor(like(b[:], HALVES), banks(IN_BANKS[e % 3], HALVES), like(rstd[:], HALVES), ALU.mult).then_inc(in_read, 1)

            def f_low(e):
                c = int(IN_ORDER[e][1])
                dve.wait_ge(f_hi_ready, c + 1)
                nc.vector.tensor_tensor(f_lo[:, c, :], scratch_b[e % 2][:], f_hi[:, c, :].bitcast(F32), ALU.subtract).then_inc(f_ready, 1)

            def v_low():
                dve.wait_ge(v_hi_ready, 2 * N_KV)
                for g in range(N_KV):
                    dims = slice(g * HEAD_DIM, (g + 1) * HEAD_DIM)
                    nc.vector.tensor_tensor(v_lo[:, g, 1:, dims], ps[:, 6, :].rearrange("p (a n) -> p a n", a=NB)[:, :, dims],
                                            v_hi[:, g, 1:, dims].bitcast(F32), ALU.subtract).then_inc(v_ready, 1)
                    nc.vector.tensor_tensor(v_lo[0:N_META, g, 0, dims], ps[0:N_META, 7, dims],
                                            v_hi[0:N_META, g, 0, dims].bitcast(F32), ALU.subtract).then_inc(v_ready, 1)

            def qk_norm(n):
                a, b = scratch_a[norm_chunk(n) % 2], scratch_b[norm_chunk(n) % 2]
                dve.wait_ge(qk_root_ready, n + 1)
                nc.vector.reciprocal(a[:], a[:]).then_inc(qk_inv_ready, 1)
                dve.wait_ge(qk_inv_ready, n + 1)
                if n == 0:
                    for at, first, w in ((0, 0, N_META), (N_META, N_META, SEQ), (N_META + SEQ, 0, N_META)):
                        last = nc.vector.scalar_tensor_tensor(k_rows[:, at:at + w], b[:, first:first + w], qk_gain[:, 1:2],
                                                              a[:, first:first + w], ALU.mult, ALU.mult)
                else:
                    last = nc.vector.scalar_tensor_tensor(b[:], b[:], qk_gain[:, 0:1], a[:], ALU.mult, ALU.mult)
                last.then_inc(qk_normed, 1)

            def qk_low(n):
                if n == 0:
                    for g in range(N_KV):
                        rows = slice(g * HEAD_DIM, (g + 1) * HEAD_DIM)
                        dve.wait_ge(qk_hi_ready, 2 * g + 2)
                        for at in range(2):
                            nc.vector.tensor_tensor(k_lo[at * HEAD_DIM:(at + 1) * HEAD_DIM, g, :], k_rows[rows, :],
                                                    k_hi[rows, g, :].bitcast(F32), ALU.subtract).then_inc(qk_ready, 1)
                else:
                    b = scratch_b[norm_chunk(n) % 2]
                    for g in range(N_KV):
                        rows, other = slice(g * HEAD_DIM, (g + 1) * HEAD_DIM), slice((1 - g) * HEAD_DIM, (2 - g) * HEAD_DIM)
                        dve.wait_ge(qk_hi_ready, 4 + 2 * (n - 1) + g + 1)
                        nc.vector.tensor_tensor(q_stack[other, g * GROUP + n - 1, :], b[rows, N_META:L],
                                                q_stack[rows, g * GROUP + n - 1, :].bitcast(F32), ALU.subtract).then_inc(qk_ready, 1)

            split_lo(U_IN, KD)
            for j in range(len(IN_ORDER)):
                if j == 0:
                    finish_b(1, KD - 1, 0, None)
                    split_lo(U_IN + 1, KD)
                    norm_inverse(1, L)
                else:
                    if j - 2 == V_AT:
                        v_low()
                    in_finish(j - 1)
                    if j + 1 < len(IN_ORDER):
                        split_lo(U_IN + j + 1, KD)
                    if IN_ORDER[j - 1][0] == "f":
                        f_low(j - 1)
                if j >= 2 and IN_ORDER[j - 2] in NORMS:
                    n = NORMS.index(IN_ORDER[j - 2])
                    qk_norm(n)
                    qk_low(n)
            in_finish(len(IN_ORDER) - 1)

            def z_low(c):
                bank = 3 * (c % 2)
                dve.wait_ge(z_hi_ready, 2 * (c + 1))
                nc.vector.tensor_tensor(z_lo[c % 2][:, 1:, :].rearrange("p a n -> p (a n)"), ps[:, bank:bank + 2, :].rearrange("p a n -> p (a n)"),
                                        z_hi[c % 2][:, 1:, :].rearrange("p a n -> p (a n)").bitcast(F32), ALU.subtract).then_inc(z_ready, 1)
                nc.vector.tensor_tensor(z_lo[c % 2][0:N_META, 0, :], ps[0:N_META, bank + 2, 0:2 * P],
                                        z_hi[c % 2][0:N_META, 0, :].bitcast(F32), ALU.subtract).then_inc(z_ready, 1)

            def waves(c):
                dve.wait_ge(sine_copied, c + 1)
                cosine, sine = ps[:, 6, 0:HALF], scratch_b[c % 2][:, 0:HALF]
                near = HALF - N_META
                nc.vector.tensor_tensor(f_out[:, c, 0:near], cosine[:, N_META - 1:HALF - 1], sine[:, N_META - 1:HALF - 1], ALU.subtract)
                nc.vector.tensor_tensor(f_out[:, c, near:SEQ][:, ::-1], cosine, sine, ALU.add).then_inc(waves_read, 1)

            def add_f_squares(c):
                dve.wait_ge(fsq_ready, c + 1)
                if c == 0:
                    nc.vector.tensor_copy(rstd_f[:], scratch_a[0][:, 0:SEQ]).then_inc(fsq_added, 1)
                    return
                dve.wait_ge(fsq_added, c)
                nc.vector.tensor_tensor(rstd_f[:], rstd_f[:], scratch_a[c % 2][:, 0:SEQ], ALU.add).then_inc(fsq_added, 1)

            def set_slopes():
                dve.wait_ge(z_done, 4)
                for h in range(N_HEADS):
                    last = nc.vector.tensor_scalar(slopes[:, h, :], ident, 2.0 ** -(h + 1) * HEAD_DIM ** 0.5, None, ALU.mult)
                last.then_inc(slopes_ready, 1)

            z_low(0)
            f_low(len(IN_ORDER) - 1)
            z_low(1)
            nc.vector.tensor_scalar(neg_sinks[:], sinks[:], -1.0, None, ALU.mult).then_inc(neg_sinks_ready, 1)
            waves(0)
            z_low(2)
            waves(1)
            set_slopes()
            z_low(3)
            waves(2)
            add_f_squares(0)
            add_f_squares(1)

            def maxima(s, half):
                b, g = STEPS[s]
                n = 2 * s + half
                heads = slice(g * GROUP + 2 * half, g * GROUP + 2 * half + 2)
                dve.wait_ge(scores_done, n + 1)
                nc.vector.tensor_reduce(score_max[:, n, :], ps[:, 2 * half:2 * half + 2, 0:SCORE_W[b]], AX_X, ALU.max).then_inc(max_ready, 1)
                dve.wait_ge(max_ready, n + 1)
                nc.vector.scalar_tensor_tensor(neg_max[:, n, :], score_max[:, n, :], -(HEAD_DIM ** -0.5), neg_sinks[:, heads],
                                               ALU.mult, ALU.min).then_inc(shift_ready, 1)

            def probs_low(s, j):
                m = SEG_BASE[s] + j
                _, keys, _ = segments(STEPS[s][0])[j]
                dve.wait_ge(pt_hi_ready, m + 1)
                nc.vector.tensor_tensor(pt_lo[m % 2][0:keys].rearrange("p a n -> p (a n)"), ps[0:keys, 4 + m % 2, :],
                                        pt_hi[m % 2][0:keys].rearrange("p a n -> p (a n)").bitcast(F32), ALU.subtract).then_inc(pt_ready, 1)

            def invert_sum(s, half):
                n = 2 * s + half
                dve.wait_ge(exp_done, EXPS * (n + 1))
                nc.vector.tensor_tensor(inv_den[:, n, :], prob_sums[:, n, :], sink_exp[:, n, :], ALU.add).then_inc(den_ready, 1)
                dve.wait_ge(den_ready, n + 1)
                nc.vector.reciprocal(inv_den[:, n, :], inv_den[:, n, :]).then_inc(den_inverted, 1)
                dve.wait_ge(den_inverted, n + 1)

            def scale_head(s, a):
                p = probs[s % 2][:, a, 0:SCORE_W[STEPS[s][0]]]
                nc.vector.tensor_scalar(p, p, inv_den[:, 2 * s + a // 2, a % 2:a % 2 + 1], None, ALU.mult).then_inc(heads_scaled, 1)

            def gain_attn(b):
                dve.wait_ge(attn_sq_ready, b + 1)
                need(dve, mix_a_ready, b)
                gain = out_gain[:, 0, :].unsqueeze(2).to_broadcast([P, GROUP, P])
                nc.vector.tensor_tensor(attn_gained[:], ps[:, 6, :].rearrange("p (a n) -> p a n", a=GROUP), gain, ALU.mult).then_inc(gained_ready, 1)

            def mix_low(b):
                dve.wait_ge(mix_a_hi_ready, b + 1)
                nc.vector.tensor_tensor(mix_a_lo[:, :, b * P:(b + 1) * P], attn_gained[:], mix_a_hi[:, :, b * P:(b + 1) * P].bitcast(F32),
                                        ALU.subtract).then_inc(mix_a_ready, 1)

            def attn_inverse(b):
                dve.wait_ge(attn_sq_summed, b + 1)
                r = rstd_a[:, b * P:(b + 1) * P]
                nc.vector.tensor_scalar(r, ps[:, 7, b * P:(b + 1) * P], 1.0 / ATTN_W, EPS, ALU.mult, ALU.add).then_inc(a_mean_ready, 1)
                dve.wait_ge(a_mean_ready, b + 1)
                nc.vector.reciprocal(r, r).then_inc(a_inv_ready, 1)

            dve.wait_ge(neg_sinks_ready, 1)
            maxima(0, 0)
            maxima(0, 1)
            invert_sum(0, 0)
            scale_head(0, 0)
            scale_head(0, 1)
            invert_sum(0, 1)
            scale_head(0, 2)
            waves(3)
            maxima(1, 0)
            for s in range(len(STEPS)):
                b, g = STEPS[s]
                if g == 0 and b > 0:
                    gain_attn(b - 1)
                probs_low(s, 0)
                probs_low(s, 1)
                if g == 1 and b > 0:
                    attn_inverse(b - 1)
                if s == 1:
                    dve.wait_ge(fsq_summed, 1)
                    nc.vector.tensor_scalar(rstd_f[:], ps[:, 7, :], 1.0 / F_W, EPS, ALU.mult, ALU.add).then_inc(f_mean_ready, 1)
                probs_low(s, 2)
                if s + 1 < len(STEPS):
                    maxima(s + 1, 1)
                    invert_sum(s + 1, 0)
                    scale_head(s + 1, 0)
                if len(segments(b)) == 4:
                    probs_low(s, 3)
                if s + 1 < len(STEPS):
                    scale_head(s + 1, 1)
                    invert_sum(s + 1, 1)
                    scale_head(s + 1, 2)
                if s == 0:
                    add_f_squares(2)
                    add_f_squares(3)
                if s + 2 < len(STEPS):
                    maxima(s + 2, 0)
            gain_attn(NB - 1)
            mix_low(NB - 1)
            dve.wait_ge(f_mean_ready, 1)
            nc.vector.reciprocal(rstd_f[:], rstd_f[:]).then_inc(f_inv_ready, 1)
            attn_inverse(NB - 1)

            def out_finish(e):
                p, x = e % 2, xT[:, e, N_META:L]
                dve.wait_ge(unit_used, U_OUT + e + 1)
                nc.vector.tensor_tensor(fourier_part[:, p, :], ps[:, 2 * p, :], rstd_f[:], ALU.mult).then_inc(parts_scaled, 1)
                if e == 0:
                    dve.wait_ge(a_root_ready, 1)
                nc.vector.tensor_tensor(scratch_b[p][:, 0:SEQ], ps[:, 2 * p + 1, :], rstd_a[:], ALU.mult).then_inc(parts_scaled, 1)
                dve.wait_ge(parts_scaled, 2 * e + 1)
                nc.vector.tensor_tensor(x, x, fourier_part[:, p, :], ALU.add).then_inc(x_plus_f, 1)
                dve.wait_ge(parts_scaled, 2 * e + 2)
                dve.wait_ge(x_plus_f, e + 1)
                nc.vector.tensor_tensor(x, x, scratch_b[p][:, 0:SEQ], ALU.add).then_inc(x_mixed, 1)
                if e + 1 < KD:
                    split_lo(U_OUT + OUT_AHEAD + e, KD)
                gained_lo(2, e, 0, None, N_META, SEQ)

            for d in range(KD):
                if d == 0:
                    dve.wait_ge(f_root_ready, 1)
                    dve.wait_ge(split_ready, U_OUT + OUT_AHEAD)
                else:
                    out_finish(d - 1)

            def last_of_x():
                out_finish(KD - 1)

            ffn(FFN[1], last_of_x, lambda: norm_inverse(2, SEQ))
            for half in range(2):
                cols = half_cols(half)
                dve.wait_ge(half_done, half + 1)
                nc.vector.scalar_tensor_tensor(scratch_b[1][:, cols], ps[:, 1 + half, cols], 0.5, xT[:, LAST, N_META:L][:, cols],
                                               ALU.mult, ALU.add).then_inc(half_updated, 1)
                dve.wait_ge(half_sums_ready, half + 1)
                dve.wait_ge(sums_ready, LAST)
                r = row_rstd[:, 2 * half:2 * half + 2]
                nc.vector.tensor_reduce(r, row_sums[:, 2 * half:2 * half + 2, :], AX_X, ALU.add).then_inc(mean_ready, 1)
                dve.wait_ge(final_root, half + 1)
                nc.vector.reciprocal(r, r).then_inc(final_rstd, 1)
                dve.wait_ge(final_rstd, half + 1)
                dve.wait_ge(ffns[1].turned_read, LAST)
                for b in half_blocks(half):
                    nc.vector.scalar_tensor_tensor(y_rows[:, b, NORMED:], ps[:, 7 - half, b * P:(b + 1) * P], row_rstd[:, b:b + 1],
                                                   final_gain[:, NORMED:], ALU.mult, ALU.mult).then_inc(rows_scaled, 1)
                    if b % 2 == 0:
                        nc.vector.tensor_scalar(y_rows[:, b, 0:NORMED], y_rows[:, b, 0:NORMED], row_rstd[:, b:b + 1], None,
                                                ALU.mult).then_inc(rows_scaled, 1)

        @block.tensor
        def _(pe):
            def mm3(outs, hi, lo, x_hi, x_lo, start, stop):
                for n, (w, x) in enumerate(((hi, x_hi), (hi, x_lo), (lo, x_hi))):
                    for o, m in zip(outs, x):
                        last = nc.tensor.matmul(o, w, m, start=start and n == 0, stop=stop and n == 2)
                return last

            def out_spans(bank, spans):
                return [ps[:, bank + a, 0:n] for a, (_, n) in enumerate(spans)]

            def xg(k, spans):
                return [xg_hi[:, k, c:c + n] for c, n in spans], [xg_lo[:, k, c:c + n] for c, n in spans]

            def sum_squares(norm, bank, spans):
                pe.wait_ge(norms[norm].sq_added, KD)
                for o, (c, n) in zip(out_spans(bank, spans), spans):
                    last = nc.tensor.matmul(o, ones, rstd[:, c:c + n], start=True, stop=True)
                last.then_inc(norms[norm].summed, 1)

            def ffn(f, norm, with_first, after_first, free):
                s = f.s

                def step_a(parity, k0, k1, i):
                    unit = f.unit_a + 2 * k0
                    gate, up = out_spans(f.gate_bank[parity], f.spans), out_spans(f.up_bank[parity], f.spans)
                    if k0 < 2:
                        free(k0)
                    else:
                        pe.wait_ge(s.up_scaled, count(i, k0 - 1, k1))
                    early = k0 == 0 and f.n == 0
                    if early:
                        pe.wait_ge(first_split_ready, 2)
                    else:
                        pe.wait_ge(split_ready, count(i, unit + 1, 2 * k1))
                    g, u = unit % RING, (unit + 1) % RING
                    if k0 == 0:
                        for k in range(KD):
                            pe.wait_ge(norms[norm].ready, k + 1)
                            if early and k == SLOT // 2:
                                pe.wait_ge(split_ready, unit + 2)
                            a = mm3(gate, w_hi[g][:, k], w_lo[g][:, k], *xg(k, f.spans), k == 0, k == KD - 1)
                            if k == KD - 1:
                                a.then_inc(unit_used, 1)
                            if k == 0 and not early:
                                pe.wait_ge(split_ready, unit + 2)
                            b = mm3(up, w_hi[u][:, k], w_lo[u][:, k], *xg(k, f.spans), k == 0, k == KD - 1)
                            with_first(k)
                        b.then_inc(unit_used, 1)
                        after_first()
                        return
                    for k in range(KD):
                        a = mm3(gate, w_hi[g][:, k], w_lo[g][:, k], *xg(k, f.spans), k == 0, k == KD - 1)
                    a.then_inc(unit_used, 1)
                    pe.wait_ge(split_ready, count(i, unit + 2, 2 * k1))
                    for k in range(KD):
                        b = mm3(up, w_hi[u][:, k], w_lo[u][:, k], *xg(k, f.spans), k == 0, k == KD - 1)
                    b.then_inc(unit_used, 1)

                def turn_rows(k, i=None, k1=0):
                    pe.wait_ge(s.x_updated, count(i, k + 1, k1))
                    need(pe, s.turned_read, count(i, k, k1))
                    for b in range(NB):
                        last = nc.tensor.transpose(ps[:, 6 + k % 2, b * P:(b + 1) * P],
                                                   scratch_b[k % 2][:, b * P:(b + 1) * P], ident)
                    last.then_inc(s.turned, 1)

                def step_b(parity, k0, k1, i):
                    y = out_spans(f.down_bank[parity], f.spans)
                    if k0 == 0 and f.n == 0:
                        pe.wait_ge(s.up_scaled, KF - 1)
                    need(pe, s.x_updated, count(i, k0 - 1, k1))
                    for j, (f0, n) in enumerate(DOWN_UNITS):
                        unit = f.unit_b + 4 * k0 + j
                        slot = unit % RING
                        pe.wait_ge(split_ready, count(i, unit + 1, 4 * k1))
                        if k0 == 0:
                            pe.wait_ge(s.h_ready, f0 + n)
                        for m in range(n):
                            h = f0 + m
                            a = mm3(y, w_hi[slot][:, m], w_lo[slot][:, m], [h_hi[:, h, c:c + w] for c, w in f.spans],
                                    [h_lo[:, h, c:c + w] for c, w in f.spans], h == 0, h == KF - 1)
                        a.then_inc(unit_used, 1)
                        if j == 1 and k0 >= 1 and f.n == 1:
                            turn_rows(k0 - 1, i, k1)

                def turn_half(half):
                    pe.wait_ge(half_updated, half + 1)
                    pe.wait_ge(s.turned_read, LAST - 1 + half)
                    for b in half_blocks(half):
                        last = nc.tensor.transpose(ps[:, 7 - half, b * P:(b + 1) * P], scratch_b[1][:, b * P:(b + 1) * P], ident)
                    last.then_inc(half_turned, 1)

                def last_chunk():
                    pe.wait_ge(s.x_updated, LAST - 1)
                    pe.wait_ge(s.up_scaled, KF)
                    for half in range(2):
                        cols = half_cols(half)
                        for j, (f0, n) in enumerate(DOWN_UNITS):
                            unit = f.unit_b + 4 * LAST + j
                            slot = unit % RING
                            pe.wait_ge(split_ready, unit + 1)
                            for h in range(f0, f0 + n):
                                last = mm3([ps[:, 1 + half, cols]], w_hi[slot][:, h - f0], w_lo[slot][:, h - f0],
                                           [h_hi[:, h, cols]], [h_lo[:, h, cols]], h == 0, h == KF - 1)
                            if j == 1 and half == 0:
                                turn_rows(LAST - 1)
                            if j == 0 and half == 1:
                                turn_half(0)
                        last.then_inc(half_done, 1)
                    turn_half(1)

                pairs(pe, KF, step_a)
                if f.n == 0:
                    pairs(pe, KD, step_b)
                else:
                    pairs(pe, KD, step_b, peel=True)
                    last_chunk()

            pe.wait_ge(ident_landed, 16)
            pe.wait_ge(meta_landed, 16)
            for k in range(KD):
                last = nc.tensor.transpose(ps[:, 3, k * N_META:(k + 1) * N_META], meta_rows[0:N_META, k * P:(k + 1) * P], ident[0:N_META, 0:N_META])
            last.then_inc(x_turned, 1)

            def turn_x(k):
                need(pe, x_copied, k - 3)
                if k % (X_COLS // P) == 0:
                    pe.wait_ge(x_landed[k * P // X_COLS], 16)
                for b in range(NB):
                    last = nc.tensor.transpose(ps[:, 4 + k % 4, b * P:(b + 1) * P], x_rows[:, b, k * P:(k + 1) * P], ident)
                last.then_inc(x_turned, 1)

            def spread_rstd():
                pe.wait_ge(ones_landed, 16)
                pe.wait_ge(diag_ready, 1)
                nc.tensor.matmul(ps[:, 6, 0:N_META], ones[0:N_META, :], rstd_diag[0:N_META, NB, 0:N_META], start=True, stop=True)
                for b in range(NB):
                    last = nc.tensor.matmul(ps[:, 7, b * P:(b + 1) * P], ones, rstd_diag[:, b, :], start=True, stop=True)
                last.then_inc(rstd_spread, 1)

            for k in range(4):
                turn_x(k)

            def turn_more(k):
                if k + 4 < KD:
                    turn_x(k + 4)

            ffn(FFN[0], 0, turn_more, spread_rstd,
                lambda c: pe.wait_ge(norms[0].rstd, 1) if c else None)

            def qk_sums(n):
                a = scratch_a[norm_chunk(n) % 2]
                pe.wait_ge(qk_sq_ready, n + 1)
                if n == 0:
                    pe.wait_ge(norms[1].root, 1)
                elif n == 1:
                    pe.wait_ge(v_ready, 2 * N_KV)
                else:
                    pe.wait_ge(qk_root_ready, n)
                for o, (c, w) in zip(out_spans(6, HALVES), HALVES):
                    last = nc.tensor.matmul(o, pair_ones, a[:, c:c + w], start=True, stop=True)
                last.then_inc(qk_summed, 1)

            def turn_values():
                v = scratch_b[V_AT % 2]
                pe.wait_ge(in_read, V_AT + 1)
                pe.wait_ge(qk_root_ready, 1)
                nc.tensor.transpose(ps[0:N_META, 7, 0:P], v[:, 0:N_META], ident)
                for b in range(NB):
                    last = nc.tensor.transpose(ps[:, 6, b * P:(b + 1) * P], v[:, N_META + b * P:N_META + (b + 1) * P], ident)
                last.then_inc(v_turned, 1)

            for j, name in enumerate(IN_ORDER):
                slot = (U_IN + j) % RING
                outs = out_spans(IN_BANKS[j % 3], HALVES)
                pe.wait_ge(split_ready, U_IN + j + 1)
                if j >= 3:
                    pe.wait_ge(in_read, j - 2)
                elif j:
                    pe.wait_ge(ffns[0].x_updated, KD - 2 + j)
                for k in range(KD):
                    if j == 0:
                        pe.wait_ge(norms[1].ready, k + 1)
                    last = mm3(outs, w_hi[slot][:, k], w_lo[slot][:, k], *xg(k, HALVES), k == 0, k == KD - 1)
                last.then_inc(unit_used, 1)
                if j == 0:
                    sum_squares(1, 6, HALVES)
                elif j - 1 == V_AT:
                    turn_values()
                elif IN_ORDER[j - 1] in NORMS:
                    qk_sums(NORMS.index(IN_ORDER[j - 1]))

            def channel_stage(c):
                pe.wait_ge(f_ready, c + 1)
                if c >= 2:
                    pe.wait_ge(z_ready, 2 * (c - 1))
                else:
                    pe.wait_ge(in_read, len(IN_ORDER) - 1 + c)
                bank = 3 * (c % 2)
                for blk in range(1 + NB):
                    if blk == 0:
                        cols, o = slice(0, N_META), ps[0:N_META, bank + 2, 0:2 * P]
                    else:
                        cols = slice(N_META + (blk - 1) * P, N_META + blk * P)
                        o = ps[:, bank + (blk - 1) // 2, (blk - 1) % 2 * 2 * P:((blk - 1) % 2 + 1) * 2 * P]
                    last = mm3([o], f_hi[:, c, cols], f_lo[:, c, cols], [channel_hi[:]], [channel_lo[:]], True, True)
                last.then_inc(z_done, 1)

            def position_stage(c):
                pe.wait_ge(z_ready, 2 * (c + 1))
                if c:
                    pe.wait_ge(waves_read, c)
                else:
                    pe.wait_ge(qk_root_ready, len(NORMS))
                for part in range(2):
                    for blk in range(1 + NB):
                        rows = slice(0, N_META if blk == 0 else P)
                        cols = slice(part * P, (part + 1) * P)
                        last = mm3([ps[:, 6 + part, 0:HALF]], z_hi[c % 2][rows, blk, cols], z_lo[c % 2][rows, blk, cols],
                                   [position_hi[rows, blk, part, :]], [position_lo[rows, blk, part, :]], blk == 0, blk == NB)
                last.then_inc(waves_done, 1)

            def scores(s, half):
                b, g = STEPS[s]
                n = 2 * s + half
                w, at = SCORE_W[b], SCORE_AT[b]
                if s == 0:
                    pe.wait_ge(z_ready, 8)
                    pe.wait_ge(slopes_ready, 1)
                    pe.wait_ge(qk_ready, 4 + 2 * GROUP)
                else:
                    pe.wait_ge(exp_done, EXPS * (n - 1))
                for a in range(2):
                    h = g * GROUP + 2 * half + a
                    o = ps[:, 2 * half + a, 0:w]
                    q = q_stack[:, h, b * P:(b + 1) * P]
                    nc.tensor.matmul(o, q, k_hi[:, g, at:at + w], start=True, stop=False)
                    nc.tensor.matmul(o, q, k_lo[:, g, at:at + w], start=False, stop=False)
                    last = nc.tensor.matmul(o, slopes[:, h, :], bias_tab[:, BIAS_AT[b]:BIAS_AT[b] + w], start=False, stop=True)
                last.then_inc(scores_done, 1)

            def turn_probs(s, j):
                b, g = STEPS[s]
                m = SEG_BASE[s] + j
                col, keys, _ = segments(b)[j]
                need(pe, pt_ready, m - 1)
                for a in range(GROUP):
                    if j == 0:
                        if a < GROUP - 1:
                            pe.wait_ge(heads_scaled, (GROUP - 1) * s + a + 1)
                        else:
                            pe.wait_ge(last_head_scaled, s + 1)
                    last = nc.tensor.transpose(ps[0:keys, 4 + m % 2, a * P:(a + 1) * P], probs[s % 2][:, a, col:col + keys], ident)
                last.then_inc(pt_done, 1)

            def weigh_values(s, j):
                b, g = STEPS[s]
                m = SEG_BASE[s] + j
                _, keys, n = segments(b)[j]
                pe.wait_ge(pt_ready, m + 1)
                if m == 0:
                    pe.wait_ge(waves_read, 4)
                elif j == 0 and g == 0:
                    pe.wait_ge(gained_ready, b)
                ph, pl = (x[m % 2][0:keys].rearrange("p a n -> p (a n)") for x in (pt_hi, pt_lo))
                last = mm3([ps[:, 6, :]], v_hi[0:keys, g, n, :], v_lo[0:keys, g, n, :], [ph], [pl],
                           g == 0 and j == 0, g == N_KV - 1 and j == len(segments(b)) - 1)
                last.then_inc(pv_used, 1)

            def sum_attn_squares(b):
                pe.wait_ge(attn_sq_ready, b + 1)
                if b == 0:
                    pe.wait_ge(f_mean_ready, 1)
                else:
                    pe.wait_ge(a_mean_ready, b)
                for j in range(GROUP):
                    last = nc.tensor.matmul(ps[:, 7, b * P:(b + 1) * P], ones, attn_sq[:, j, :], start=j == 0, stop=j == GROUP - 1)
                last.then_inc(attn_sq_summed, 1)

            pe.wait_ge(mix_tables_landed, 48)
            channel_stage(0)
            channel_stage(1)
            pe.wait_ge(position_landed, 32)
            position_stage(0)
            channel_stage(2)
            position_stage(1)
            channel_stage(3)
            position_stage(2)
            scores(0, 0)
            scores(0, 1)
            position_stage(3)
            scores(1, 0)
            for s in range(len(STEPS)):
                b, g = STEPS[s]
                last = len(segments(b)) - 1
                turn_probs(s, 0)
                turn_probs(s, 1)
                if g == 1 and b > 0:
                    sum_attn_squares(b - 1)
                weigh_values(s, 0)
                turn_probs(s, 2)
                if s + 1 < len(STEPS):
                    scores(s + 1, 1)
                weigh_values(s, 1)
                if last == 3:
                    turn_probs(s, 3)
                    weigh_values(s, 2)
                if s + 2 < len(STEPS):
                    scores(s + 2, 0)
                weigh_values(s, last)
                if s == 0:
                    pe.wait_ge(fsq_added, 4)
                    nc.tensor.matmul(ps[:, 7, :], ones, rstd_f[:], start=True, stop=True).then_inc(fsq_summed, 1)

            def out_part(d, part):
                slot = (U_OUT + d) % RING
                hi, lo = ((mix_f_hi, mix_f_lo), (mix_a_hi, mix_a_lo))[part]
                for k in range(4):
                    last = mm3([ps[:, 2 * (d % 2) + part, :]], w_hi[slot][:, 4 * part + k], w_lo[slot][:, 4 * part + k],
                               [hi[:, k, :]], [lo[:, k, :]], k == 0, k == 3)
                return last

            pe.wait_ge(exp_done, EXPS * 2 * len(STEPS))
            pe.wait_ge(mix_f_ready, 4)
            for d in range(2):
                pe.wait_ge(split_ready, U_OUT + d + 1)
                out_part(d, 0)
            sum_attn_squares(NB - 1)
            pe.wait_ge(mix_a_ready, NB)
            for d in range(KD):
                if d >= 2:
                    pe.wait_ge(split_ready, U_OUT + d + 1)
                    pe.wait_ge(parts_scaled, 2 * (d - 1))
                    out_part(d, 0)
                out_part(d, 1).then_inc(unit_used, 1)

            def second_norm_sum():
                pe.wait_ge(gained_ready, NB)
                sum_squares(2, 6, FFN[1].spans)

            ffn(FFN[1], 2, lambda k: None, second_norm_sum, lambda c: None)


_INS = ["x", "meta_tokens", "ffn1_norm", "ffn1_w_gate", "ffn1_w_up", "ffn1_w_down", "mix_norm", "w_in", "q_norm", "k_norm",
        "sink", "attn_out_norm", "fourier_out_norm", "w_out", "ffn2_norm", "ffn2_w_gate", "ffn2_w_up", "ffn2_w_down", "final_norm"]


def kernel(**inputs):
    import concourse.bacc as _bacc
    from concourse.bass_utils import run_bass_kernel_spmd as _run

    nc = _bacc.Bacc("TRN2", target_bir_lowering=False, num_devices=1)
    arrays, tensors = {}, {}
    for name, a in [(n, inputs[n]) for n in _INS] + list(constant_tables().items()):
        a = np.ascontiguousarray(a)
        arrays[f"in_{name}_dram"] = a
        tensors[name] = nc.dram_tensor(f"in_{name}_dram", a.shape, mybir.dt.from_np(a.dtype), kind="ExternalInput").ap()
    out = nc.dram_tensor("out_0_dram", (1, SEQ, D_MODEL), F32, kind="ExternalOutput").ap()
    build(nc, tensors, out)
    r = _run(nc, [arrays], core_ids=[0])
    return r.results[0]["out_0_dram"]
```
